# Optimizing a Trainium2 kernel written in Bass

```python
import math
import jax, jax.numpy as jnp
from jax import lax
import numpy as np

D_MODEL = 2048
BATCH = 1
SEQ = 256
DEPTH = 2

F32 = jnp.float32

ALPHA = (2.0 * DEPTH) ** 0.25
BETA = (8.0 * DEPTH) ** -0.25

RWKV_HEAD_DIM = 64
RWKV_DIM = D_MODEL // 2
RWKV_HEADS = RWKV_DIM // RWKV_HEAD_DIM
DECAY_LORA = 96
ICL_LORA = 96
GATE_LORA = 256
W_DECAY_SCALE = 0.606531
RWKV_GN_EPS = 64e-5
RWKV_SHIFT_COLS = 3 * RWKV_DIM + DECAY_LORA + ICL_LORA + GATE_LORA

GLA_HEADS = 4
GLA_VDIM = D_MODEL // 2
GLA_KDIM = GLA_VDIM // 2
GLA_DK = GLA_KDIM // GLA_HEADS
GLA_DV = GLA_VDIM // GLA_HEADS
GLA_GATE_LORA = 16
GLA_GATE_NORMALIZER = 16.0
GLA_CHUNK = 64
AB_IN = RWKV_SHIFT_COLS + 2 * GLA_KDIM + GLA_VDIM + GLA_GATE_LORA + GLA_VDIM
AB_OUT = RWKV_DIM + GLA_VDIM

DIFF_HEAD_DIM = 64
DIFF_V_DIM = 2 * DIFF_HEAD_DIM
DIFF_HEADS = D_MODEL // DIFF_V_DIM
DIFF_Q_DIM = DIFF_HEADS * 2 * DIFF_HEAD_DIM
DIFF_VDIM_TOT = DIFF_HEADS * DIFF_V_DIM
Q_BLOCK = 128
ROPE_THETA = 10000.0

D_FF = -(-(8 * D_MODEL) // (3 * 256)) * 256

N_EVEN = (DEPTH + 1) // 2
N_ODD = DEPTH // 2

kernel_name = "bidir_hybrid_rwkv7_gla_diffattn_deepnorm_adaln"

def _split(z, sizes):
    idx = np.cumsum(sizes)[:-1].tolist()
    return jnp.split(z, idx, axis=-1)

def _layer_norm(x, g, b, eps=1e-5):
    xf = x.astype(F32)
    mu = jnp.mean(xf, -1, keepdims=True)
    var = jnp.mean(jnp.square(xf - mu), -1, keepdims=True)
    return ((xf - mu) * lax.rsqrt(var + eps)).astype(x.dtype) * g + b

def _rms_norm(x, g, eps=1e-5):
    xf = x.astype(F32)
    return (xf * lax.rsqrt(jnp.mean(xf * xf, -1, keepdims=True) + eps)).astype(x.dtype) * g

def _l2norm(t, eps=1e-12):
    tf = t.astype(F32)
    return (tf / jnp.maximum(jnp.sqrt(jnp.sum(tf * tf, -1, keepdims=True)), eps)).astype(t.dtype)

def _centred_shift(z):
    zp = jnp.pad(z, ((0, 0), (1, 1), (0, 0)))
    return 0.5 * (zp[:, :-2] + zp[:, 2:])

def _ada(c, w, b):
    mod = jax.nn.silu(c) @ w + b
    shift, scale, gate = jnp.split(mod[:, None, :], 3, axis=-1)
    return shift, scale, gate

def _rwkv7_scan(r, w, k, v, kk, a):
    dt = r.dtype
    xs = tuple(t.astype(F32) for t in (r, w, k, v, kk, a))

    def step(S, inp):
        r_t, w_t, k_t, v_t, kk_t, a_t = inp
        sa = -jnp.einsum('dbhvk,dbhk->dbhv', S, kk_t)
        S = (S * w_t[..., None, :] + sa[..., :, None] * (kk_t * a_t)[..., None, :]
             + v_t[..., :, None] * k_t[..., None, :])
        return S, jnp.einsum('dbhvk,dbhk->dbhv', S, r_t)

    S0 = jnp.zeros(r.shape[1:] + (r.shape[-1],), F32)
    _, y = lax.scan(step, S0, xs)
    return y.astype(dt)

def _rwkv7_mixer(z, mu, w0, w_up, a0, a_up, g_up, k_k, k_a, r_k, gn_g, gn_b):
    B, T, _ = z.shape
    H, N = RWKV_HEADS, RWKV_HEAD_DIM
    z = z + (_centred_shift(z) - z) * mu
    r, k, v, wd, ad, gd = _split(z, (RWKV_DIM, RWKV_DIM, RWKV_DIM, DECAY_LORA, ICL_LORA, GATE_LORA))
    w = jnp.exp(-W_DECAY_SCALE * jax.nn.sigmoid(
        w0[:, None, None, :] + jnp.einsum('btr,drc->dbtc', jnp.tanh(wd), w_up)))
    a = jax.nn.sigmoid(a0 + ad @ a_up)
    g = jax.nn.sigmoid(gd) @ g_up
    heads = lambda t: t.reshape(t.shape[:-1] + (H, N))
    kk = _l2norm(heads(k * k_k))
    k = k * (1.0 + (a - 1.0) * k_a)
    r_h, k_h, v_h, a_h, w_h = heads(r), heads(k), heads(v), heads(a), heads(w)
    tm = lambda t: jnp.moveaxis(t, 1, 0)

    def both(t):
        t = tm(t)
        return jnp.stack([t, t[::-1]], axis=1)

    w_t = jnp.stack([tm(w_h[0]), tm(w_h[1])[::-1]], axis=1)
    y = _rwkv7_scan(both(r_h), w_t, both(k_h), both(v_h), both(kk), both(a_h))
    y = jnp.moveaxis(y[:, 0] + y[::-1, 1], 0, 1)
    y = _layer_norm(y, gn_g.reshape(H, N), gn_b.reshape(H, N), eps=RWKV_GN_EPS)
    y = y + jnp.sum(r_h * k_h * r_k, -1, keepdims=True) * v_h
    return y.reshape(B, T, RWKV_DIM) * g

def _gla_chunked(q, k, v, log_g):
    dt = v.dtype
    q, k, v, log_g = (t.astype(F32) for t in (q, k, v, log_g))
    T = q.shape[-2]
    n = T // GLA_CHUNK
    chunk = lambda t: t.reshape(t.shape[:-2] + (n, GLA_CHUNK, t.shape[-1]))
    q, k, v, log_g = chunk(q), chunk(k), chunk(v), chunk(log_g)
    b = lax.cumsum(log_g, axis=log_g.ndim - 2)
    b_last = b[..., -1:, :]
    qb = q * jnp.exp(b)
    kb = k * jnp.exp(-b)
    mask = jnp.tril(jnp.ones((GLA_CHUNK, GLA_CHUNK), bool))
    att = jnp.where(mask, jnp.einsum('...nid,...njd->...nij', qb, kb), 0.0)
    o = jnp.einsum('...nij,...njv->...niv', att, v)
    kv = jnp.einsum('...ncd,...ncv->...ndv', k * jnp.exp(b_last - b), v)
    decay = jnp.exp(b_last[..., 0, :])

    def step(S, inp):
        dec, kv_n = inp
        return S * dec[..., :, None] + kv_n, S

    S0 = jnp.zeros(kv.shape[:-3] + kv.shape[-2:], F32)
    _, S_prev = lax.scan(step, S0, (jnp.moveaxis(decay, -2, 0), jnp.moveaxis(kv, -3, 0)))
    S_prev = jnp.moveaxis(S_prev, 0, -3)
    o = o + jnp.einsum('...ncd,...ndv->...ncv', qb, S_prev)
    return o.reshape(o.shape[:-3] + (T, o.shape[-1])).astype(dt)

def _gla_mixer(q, k, v, gg, og, gate_up, gate_b, norm_g):
    B, T, _ = q.shape
    H = GLA_HEADS
    log_g = jax.nn.log_sigmoid(jnp.einsum('btr,drc->dbtc', gg, gate_up)
                               + gate_b[:, None, None, :]) / GLA_GATE_NORMALIZER

    def heads(t, dh):
        return jnp.swapaxes(t.reshape(t.shape[:-1] + (H, dh)), -3, -2)

    qh = heads(q, GLA_DK) * (GLA_DK ** -0.5)
    kh, vh, gh = heads(k, GLA_DK), heads(v, GLA_DV), heads(log_g, GLA_DK)
    flip = lambda t: t[..., ::-1, :]
    both = lambda t: jnp.stack([t, flip(t)])
    o = _gla_chunked(both(qh), both(kh), both(vh), jnp.stack([gh[0], flip(gh[1])]))
    o = o[0] + flip(o[1])
    o = _rms_norm(o, norm_g)
    o = jnp.swapaxes(o, 1, 2).reshape(B, T, GLA_VDIM)
    return o * jax.nn.silu(og)

def _mixer_ab(h, w_in, w_out, mu, w0, w_up, a0, a_up, g_up, k_k, k_a, r_k, gn_g, gn_b,
              gate_up, gate_b, norm_g):
    z = h @ w_in
    z_a, q, k, v, gg, og = _split(z, (RWKV_SHIFT_COLS, GLA_KDIM, GLA_KDIM, GLA_VDIM, GLA_GATE_LORA, GLA_VDIM))
    y_a = _rwkv7_mixer(z_a, mu, w0, w_up, a0, a_up, g_up, k_k, k_a, r_k, gn_g, gn_b)
    y_b = _gla_mixer(q, k, v, gg, og, gate_up, gate_b, norm_g)
    return jnp.concatenate([y_a, y_b], -1) @ w_out

def _rope_tables(T, d, dtype):
    inv = ROPE_THETA ** (-jnp.arange(0, d, 2, dtype=F32) / d)
    ang = jnp.arange(T, dtype=F32)[:, None] * inv[None, :]
    return jnp.cos(ang).astype(dtype), jnp.sin(ang).astype(dtype)

def _apply_rope(x, cos, sin):
    cos, sin = cos[:, None, None, :], sin[:, None, None, :]
    x1, x2 = jnp.split(x, 2, axis=-1)
    return jnp.concatenate([x1 * cos - x2 * sin, x2 * cos + x1 * sin], -1)

def _lambda_init(layer):
    return 0.8 - 0.6 * math.exp(-0.3 * layer)

def _mixer_c(h, w_in, w_out, lam_params, subln_g, lambda_init):
    B, T, _ = h.shape
    H, d = DIFF_HEADS, DIFF_HEAD_DIM
    q, k, v = _split(h @ w_in, (DIFF_Q_DIM, DIFF_Q_DIM, DIFF_VDIM_TOT))
    q = q.reshape(B, T, H, 2, d)
    k = k.reshape(B, T, H, 2, d)
    v = v.reshape(B, T, H, DIFF_V_DIM)
    cos, sin = _rope_tables(T, d, q.dtype)
    q, k = _apply_rope(q, cos, sin), _apply_rope(k, cos, sin)
    lp = lam_params.astype(F32)
    lam = jnp.exp(jnp.sum(lp[0] * lp[1])) - jnp.exp(jnp.sum(lp[2] * lp[3])) + lambda_init
    scale = d ** -0.5
    q_blocks = jnp.moveaxis(q.reshape(B, T // Q_BLOCK, Q_BLOCK, H, 2, d), 1, 0)

    def block(q_blk):
        s = jnp.einsum('bqhcd,bkhcd->bhcqk', q_blk, k, preferred_element_type=F32) * scale
        p = jax.nn.softmax(s, axis=-1)
        p = p[:, :, 0] - lam * p[:, :, 1]
        return jnp.einsum('bhqk,bkhv->bqhv', p.astype(v.dtype), v)

    o = lax.map(block, q_blocks)
    o = jnp.moveaxis(o, 0, 1).reshape(B, T, H, DIFF_V_DIM)
    o = _rms_norm(o, subln_g) * (1.0 - lambda_init)
    return o.reshape(B, T, DIFF_VDIM_TOT) @ w_out

def _swiglu(h, w_in, w_out):
    gate, up = jnp.split(h @ w_in, 2, axis=-1)
    return (jax.nn.silu(gate) * up) @ w_out

def setup_inputs(seed: int = 0) -> dict:
    key = jax.random.key(seed)
    ks = iter(jax.random.split(key, 40))
    nrm = lambda shape, s: jax.random.normal(next(ks), shape, F32) * s
    D = D_MODEL
    return {
        "x": nrm((BATCH, SEQ, D), 1.0),
        "c": nrm((BATCH, D), 1.0),
        "ada_w": nrm((DEPTH, 2, D, 3 * D), 0.2 * D ** -0.5),
        "ada_b": nrm((DEPTH, 2, 3 * D), 0.01),
        "ln_g": 1.0 + nrm((DEPTH, 2, D), 0.02),
        "ln_b": nrm((DEPTH, 2, D), 0.02),
        "ffn_w_in": nrm((DEPTH, D, 2 * D_FF), D ** -0.5),
        "ffn_w_out": nrm((DEPTH, D_FF, D), BETA * D_FF ** -0.5),
        "ab_w_in": nrm((N_EVEN, D, AB_IN), D ** -0.5),
        "ab_w_out": nrm((N_EVEN, AB_OUT, D), BETA * AB_OUT ** -0.5),
        "rwkv_mu": jax.random.uniform(next(ks), (N_EVEN, RWKV_SHIFT_COLS), F32),
        "rwkv_w0": jax.random.uniform(next(ks), (N_EVEN, 2, RWKV_DIM), F32, -4.0, 1.0),
        "rwkv_w_up": nrm((N_EVEN, 2, DECAY_LORA, RWKV_DIM), 0.1),
        "rwkv_a0": nrm((N_EVEN, RWKV_DIM), 0.5),
        "rwkv_a_up": nrm((N_EVEN, ICL_LORA, RWKV_DIM), ICL_LORA ** -0.5),
        "rwkv_g_up": nrm((N_EVEN, GATE_LORA, RWKV_DIM), GATE_LORA ** -0.5),
        "rwkv_k_k": 0.85 + nrm((N_EVEN, RWKV_DIM), 0.1),
        "rwkv_k_a": 1.0 + nrm((N_EVEN, RWKV_DIM), 0.1),
        "rwkv_r_k": nrm((N_EVEN, RWKV_HEADS, RWKV_HEAD_DIM), 0.1),
        "rwkv_gn_g": 1.0 + nrm((N_EVEN, RWKV_DIM), 0.02),
        "rwkv_gn_b": nrm((N_EVEN, RWKV_DIM), 0.02),
        "gla_gate_up": nrm((N_EVEN, 2, GLA_GATE_LORA, GLA_KDIM), GLA_GATE_LORA ** -0.5),
        "gla_gate_b": nrm((N_EVEN, 2, GLA_KDIM), 1.0),
        "gla_norm_g": 1.0 + nrm((N_EVEN, GLA_DV), 0.02),
        "diff_w_in": nrm((N_ODD, D, 2 * DIFF_Q_DIM + DIFF_VDIM_TOT), D ** -0.5),
        "diff_w_out": nrm((N_ODD, DIFF_VDIM_TOT, D), BETA * DIFF_VDIM_TOT ** -0.5),
        "diff_lambda": nrm((N_ODD, 4, DIFF_HEAD_DIM), 0.1),
        "diff_subln_g": 1.0 + nrm((N_ODD, DIFF_V_DIM), 0.02),
    }

def reference(x, c, ada_w, ada_b, ln_g, ln_b, ffn_w_in, ffn_w_out, ab_w_in, ab_w_out,
              rwkv_mu, rwkv_w0, rwkv_w_up, rwkv_a0, rwkv_a_up, rwkv_g_up, rwkv_k_k, rwkv_k_a,
              rwkv_r_k, rwkv_gn_g, rwkv_gn_b, gla_gate_up, gla_gate_b, gla_norm_g,
              diff_w_in, diff_w_out, diff_lambda, diff_subln_g):
    for i in range(DEPTH):
        j = i // 2
        shift, scale, gate = _ada(c, ada_w[i, 0], ada_b[i, 0])
        h = x * (1.0 + scale) + shift
        if i % 2 == 0:
            y = _mixer_ab(h, ab_w_in[j], ab_w_out[j], rwkv_mu[j], rwkv_w0[j], rwkv_w_up[j],
                          rwkv_a0[j], rwkv_a_up[j], rwkv_g_up[j], rwkv_k_k[j], rwkv_k_a[j],
                          rwkv_r_k[j], rwkv_gn_g[j], rwkv_gn_b[j],
                          gla_gate_up[j], gla_gate_b[j], gla_norm_g[j])
        else:
            y = _mixer_c(h, diff_w_in[j], diff_w_out[j], diff_lambda[j], diff_subln_g[j],
                         _lambda_init(i))
        x = _layer_norm(ALPHA * x + (1.0 + gate) * y, ln_g[i, 0], ln_b[i, 0])
        shift, scale, gate = _ada(c, ada_w[i, 1], ada_b[i, 1])
        h = x * (1.0 + scale) + shift
        y = _swiglu(h, ffn_w_in[i], ffn_w_out[i])
        x = _layer_norm(ALPHA * x + (1.0 + gate) * y, ln_g[i, 1], ln_b[i, 1])
    return x


_drawn_inputs = setup_inputs


def setup_inputs(seed=0):
    import zlib

    import numpy as np

    out = dict(_drawn_inputs(seed))
    spreads = {}
    factors = {'ada_b': 3.552,
     'rwkv_w_up': 4.433,
     'rwkv_k_k': 7.293,
     'rwkv_k_a': 3.36,
     'rwkv_gn_g': 8.0,
     'rwkv_gn_b': 8.0,
     'gla_gate_up': 3.569,
     'gla_norm_g': 8.0,
     'diff_subln_g': 8.0}
    for name, (base, spread) in spreads.items():
        noise = np.random.default_rng([zlib.crc32(name.encode()), seed]).standard_normal(out[name].shape)
        drawn = base * np.exp(spread * noise) if base else spread * noise
        out[name] = __import__('jax').numpy.asarray(drawn.astype(out[name].dtype))
    for name, factor in factors.items():
        out[name] = (out[name] * factor).astype(out[name].dtype)
    return out
```

```python
from contextlib import ExitStack

import numpy as np

import concourse.bass as bass
from concourse import mybir

ALU = mybir.AluOpType
ACT = mybir.ActivationFunctionType
F32 = mybir.dt.float32
F32R = mybir.dt.float32r
AX_X = mybir.AxisListType.X

P = 128
D = 2048
SEQ = 256
NT = SEQ // P
KT = D // P
W = 512
UK = 4
D_FF = 5632
FG = D_FF // W
HN = 64
RW = D // 2
PAIRS = RW // P
LORA = 96
GATE = 256
Z_WD = 3 * RW
Z_AD = Z_WD + LORA
Z_GD = Z_AD + LORA
Z_Q = Z_GD + GATE
GH = 4
DK = 128
DV = 256
Z_K = Z_Q + GH * DK
Z_V = Z_K + GH * DK
Z_GG = Z_V + GH * DV
GLORA = 16
Z_OG = Z_GG + GLORA
Z = Z_OG + GH * DV
ABC = -(-Z // W)
CH = 64
NCH = SEQ // CH
NU = 2 * NCH
LEVELS = 6
DH = 16
ALPHA = (2.0 * 2) ** 0.25
DECAY = 0.606531
LAMBDA_INIT = 0.8 - 0.6 * float(np.exp(-0.3))
EPS = 1e-5
GN_EPS = 64e-5

T_LN_G, T_LN_B = 0, 64
T_MU, T_W0, T_A0, T_KK, T_KA, T_RK, T_GNG, T_GNB = 128, 156, 172, 180, 188, 196, 204, 212
T_GB, T_NG, T_SUB, T_C = 220, 228, 230, 231
T_ADA = 247
T_N = T_ADA + 192
TABS = (0, 128, 247, 343, 439)

C_ID, C_ONES, C_HEADS, C_SCORE, C_GLA, C_LEVEL, C_RESET, C_COS, C_SIN = (
    0, 128, 256, 384, 640, 896, 896 + 2 * LEVELS * CH, 896 + 2 * LEVELS * CH + SEQ, 896 + 2 * LEVELS * CH + SEQ + 64)
C_I2 = C_SIN + 64
C_N = C_I2 + CH


def constants():
    c = np.zeros((P, C_N), np.float32)
    p = np.arange(P)
    c[:, C_ID:C_ID + P] = np.eye(P)
    c[:, C_ONES:C_ONES + P] = 1.0
    c[:, C_HEADS:C_HEADS + P] = (p[:, None] // HN == p[None, :] // HN)
    s, t = (p % CH)[:, None], np.arange(CH)[None, :]
    c[:, C_SCORE:C_SCORE + P] = np.concatenate([s < t, s <= t], 1)
    c[:, C_SCORE + P:C_SCORE + 2 * P] = np.concatenate([s > t, s >= t], 1)
    same = p[:, None] // CH == p[None, :] // CH
    c[:, C_GLA:C_GLA + P] = same & (p[:, None] <= p[None, :])
    c[:, C_GLA + P:C_GLA + 2 * P] = same & (p[:, None] >= p[None, :])
    for d in range(2):
        for lv in range(LEVELS):
            b = 1 << lv
            row, col = (p % CH)[:, None], np.arange(CH)[None, :]
            if d:
                row, col = CH - 1 - row, CH - 1 - col
            m = (row // (2 * b) == col // (2 * b)) & (row // b % 2 == 1) & (col // b % 2 == 0)
            at = C_LEVEL + (d * LEVELS + lv) * CH
            c[:, at:at + CH] = m
    c[:, C_RESET:C_RESET + SEQ] = (np.arange(SEQ) % CH != 0)
    inv = (10000.0 ** (-np.arange(0, 64, 2, dtype=np.float32) / 64)).astype(np.float32)
    for i in range(NT):
        ang = ((i * P + p).astype(np.float32)[:, None] * inv[None, :]).astype(np.float32)
        c[:, C_COS + 32 * i:C_COS + 32 * i + 32] = np.cos(ang)
        c[:, C_SIN + 32 * i:C_SIN + 32 * i + 32] = np.sin(ang)
    c[:, C_I2:C_I2 + CH] = np.eye(CH)[np.arange(P) % CH]
    return c


def build_trunk(nc, x_in, c_in, ada_w, ada_b, ln_g, ln_b, ffn_w_in, ffn_w_out, ab_w_in, ab_w_out,
                rwkv_mu, rwkv_w0, rwkv_w_up, rwkv_a0, rwkv_a_up, rwkv_g_up, rwkv_k_k, rwkv_k_a,
                rwkv_r_k, rwkv_gn_g, rwkv_gn_b, gla_gate_up, gla_gate_b, gla_norm_g,
                diff_w_in, diff_w_out, diff_lambda, diff_subln_g, consts, out):
    with ExitStack() as ctx:
        def sb(name, shape, dt=F32, stack=ctx):
            return stack.enter_context(nc.sbuf_tensor("s_" + name, shape, dt))

        def sem(name):
            return ctx.enter_context(nc.semaphore(name))

        cst = sb("cst", [P, C_N])
        tab = sb("tab", [P, T_N])
        ada = sb("ada", [P, 4, 48])
        silu_c = sb("silu_c", [P, KT])
        hmu = sb("hmu", [P, 28])
        omu = sb("omu", [P, 28])
        neg = sb("neg", [P, 32])
        small = sb("small", [P, 96])
        raw = sb("raw", [P, 4, UK, W])
        adaw = sb("adaw", [P, 2, UK, W])
        acc = sb("acc", [P, 2, W])
        asum = sb("asum", [P, W])
        xt = sb("xt", [P, NT, D])
        xf = xt[:].rearrange("p a d -> p (a d)").rearrange("p (k t) -> p k t", t=SEQ)

        r1 = ExitStack()
        z = sb("z", [P, NT, Z], stack=r1)
        r1.close()
        r1 = ExitStack()
        qkv = sb("qkv", [P, NT, 3 * D], stack=r1)
        r1.close()
        r1 = ExitStack()
        ysum = sb("ysum", [P, NT, D], stack=r1)
        gu = sb("gu", [P, NT, W], stack=r1)
        guh = sb("guh", [P, UK, SEQ], F32R, stack=r1)
        gul = sb("gul", [P, UK, SEQ], F32R, stack=r1)
        r1.close()
        hold = sb("hold", [P, NT, Z])

        r2 = ExitStack()
        wh = sb("wh", [P, 2, UK, W], F32R, stack=r2)
        wl = sb("wl", [P, 2, UK, W], F32R, stack=r2)
        hth = sb("hth", [P, KT, SEQ], F32R, stack=r2)
        htl = sb("htl", [P, KT, SEQ], F32R, stack=r2)
        htmp = sb("htmp", [P, 2, 2, SEQ], stack=r2)
        r2.close()
        r2 = ExitStack()
        rows = sb("rows", [P, 4, P], stack=r2)
        r2.close()
        r2 = ExitStack()
        sb("skip", [P, 2, 2, UK, W], stack=r2)
        lng = sb("lng", [P, D], stack=r2)
        lnb = sb("lnb", [P, D], stack=r2)
        gate_bc = sb("gate_bc", [P, D], stack=r2)
        diag = sb("diag", [P, 4, P], stack=r2)
        r2.close()
        r2 = ExitStack()
        R_zs = sb("R_zs", [P, NT, 3, P], stack=r2)
        R_zf = sb("R_zf", [P, 3, SEQ + 2], stack=r2)
        r2.close()
        r2 = ExitStack()
        R_qc = sb("R_qc", [P, NU, CH], stack=r2)
        R_vc = sb("R_vc", [P, NU, CH], stack=r2)
        R_wc = sb("R_wc", [P, NU, CH], stack=r2)
        sb("R_pad", [P, 32], stack=r2)
        R_rk = sb("R_rk", [P, 2, SEQ], stack=r2)
        R_vp = sb("R_vp", [P, CH + SEQ + CH], stack=r2)
        R_lw = sb("R_lw", [P, 3, SEQ], stack=r2)
        R_b = sb("R_b", [P, 2, SEQ], stack=r2)
        R_e1 = sb("R_e1", [P, 2, SEQ], stack=r2)
        R_e2 = sb("R_e2", [P, 2, SEQ], stack=r2)
        R_g = sb("R_g", [P, SEQ], stack=r2)
        R_kk = sb("R_kk", [P, SEQ], stack=r2)
        R_KR = sb("R_KR", [P, NU, P], stack=r2)
        R_Kbd = sb("R_Kbd", [P, NU, P], stack=r2)
        R_Rbd = sb("R_Rbd", [P, NU, P], stack=r2)
        R_AB = sb("R_AB", [P, NU, P], stack=r2)
        R_ABt = sb("R_ABt", [P, NU, P], stack=r2)
        R_UV = sb("R_UV", [P, 2, NU, CH], stack=r2)
        R_G = sb("R_G", [P, 2, NU, P], stack=r2)
        R_Lbd = sb("R_Lbd", [P, NU, P], stack=r2)
        R_Wbd = sb("R_Wbd", [P, NU, P], stack=r2)
        R_Qbd = sb("R_Qbd", [P, NU, P], stack=r2)
        R_S = sb("R_S", [P, 2, CH], stack=r2)
        R_X = sb("R_X", [P, 2, CH], stack=r2)
        R_y = sb("R_y", [P, NCH, CH], stack=r2)
        R_st = sb("R_st", [P, NCH, 6], stack=r2)
        R_mv = sb("R_mv", [P, NCH, 2], stack=r2)
        R_lora = sb("R_lora", [P, 4, SEQ], stack=r2)
        R_up = sb("R_up", [P, 5, P], stack=r2)
        r2.close()
        r2 = ExitStack()
        L_zs = sb("L_zs", [P, NT, 2, P], stack=r2)
        L_v = sb("L_v", [P, NT, DV], stack=r2)
        L_qk = sb("L_qk", [P, 2, SEQ], stack=r2)
        L_up = sb("L_up", [P, 2, P], stack=r2)
        L_gg = sb("L_gg", [P, SEQ], stack=r2)
        L_x = sb("L_x", [P, 2, SEQ], stack=r2)
        L_t = sb("L_t", [P, 2, SEQ], stack=r2)
        L_b = sb("L_b", [P, 2, SEQ], stack=r2)
        L_e1 = sb("L_e1", [P, 2, SEQ], stack=r2)
        L_e2 = sb("L_e2", [P, 2, SEQ], stack=r2)
        L_e3 = sb("L_e3", [P, 2, SEQ], stack=r2)
        L_qb = sb("L_qb", [P, 2, SEQ], stack=r2)
        L_kb = sb("L_kb", [P, 2, SEQ], stack=r2)
        L_kd = sb("L_kd", [P, 2, SEQ], stack=r2)
        L_kdt = sb("L_kdt", [P, 2, NT, P], stack=r2)
        L_att = sb("L_att", [P, 2, NT, P], stack=r2)
        L_S = sb("L_S", [P, 2, NCH - 1, DV], stack=r2)
        L_o = sb("L_o", [P, NT, DV], stack=r2)
        L_sq = sb("L_sq", [P, NT, DV], stack=r2)
        r2.close()
        r2 = ExitStack()
        A_qk = sb("A_qk", [P, NT, 2, 2, 64], stack=r2)
        A_t = sb("A_t", [P, NT, 2, 2, 32], stack=r2)
        A_qkT = sb("A_qkT", [P, 2, SEQ], stack=r2)
        A_p = sb("A_p", [P, 2, NT, SEQ], stack=r2)
        A_pT = sb("A_pT", [P, NT, SEQ], stack=r2)
        A_v = sb("A_v", [P, NT, P], stack=r2)
        A_o = sb("A_o", [P, NT, P], stack=r2)
        A_sq = sb("A_sq", [P, P], stack=r2)
        A_t2 = sb("A_t2", [P, 1, SEQ], stack=r2)
        A_lam = sb("A_lam", [P, 4 * 64 + 8], stack=r2)
        r2.close()
        R_sh = R_ABt[:].rearrange("p u c -> p (u c)")[:, 0:3 * SEQ].rearrange("p (j t) -> p j t", t=SEQ)

        pa = ctx.enter_context(nc.psum_tensor("pa", [P, 2, W], F32))
        pb = ctx.enter_context(nc.psum_tensor("pb", [P, 2, W], F32))
        py = ctx.enter_context(nc.psum_tensor("py", [P, 2, W], F32))
        pt = ctx.enter_context(nc.psum_tensor("pt", [P, 2, W], F32))
        ident = cst[:, C_ID:C_ID + P]
        ones = cst[:, C_ONES:C_ONES + P]
        heads1 = cst[:, C_HEADS:C_HEADS + P]
        ada_flat = ada[:].rearrange("p a b -> p (a b)")

        n_of = {0: 17, FG: 17 + FG + 12 + 4}
        C_FFN0, C_DIFF, C_OUT1, C_FFN1 = 17, 17 + 33, 17 + 33 + 12, 17 + 33 + 16
        PA_SKIP = {0: 0, C_DIFF: C_DIFF - (17 + FG)}

        const_in = sem("const_in")
        rows_zero = sem("rows_zero")
        rows_in = sem("rows_in")
        x_in_sem = sem("x_in_sem")
        tab_turned = sem("tab_turned")
        tab_copied = sem("tab_copied")
        silu_ready = sem("silu_ready")
        raw_in = [sem(f"raw_in{s}") for s in range(4)]
        hi_done = sem("hi_done")
        lo_done = sem("lo_done")
        unit_done = sem("unit_done")
        adaw_in = [sem(f"adaw_in{s}") for s in range(2)]
        ada_step = sem("ada_step")
        ada_cols = sem("ada_cols")
        ada_out = sem("ada_out")
        tr_done = sem("tr_done")
        h_scaled = sem("h_scaled")
        h_hi = sem("h_hi")
        h_lo = sem("h_lo")
        pa_done = sem("pa_done")
        pa_free = sem("pa_free")

        lora_turned = sem("lora_turned")
        lora_padded = sem("lora_padded")
        lora_mixed = sem("lora_mixed")
        lora_ready = sem("lora_ready")
        bd_zero = sem("bd_zero")
        pool_passed = sem("pool_passed")
        pair_done = sem("pair_done")
        zs_ready = sem("zs_ready")
        up_in = sem("up_in")
        rk_turned = sem("rk_turned")
        zf_ready = sem("zf_ready")
        rkv_mixed = sem("rkv_mixed")
        v_turned = sem("v_turned")
        uv_ready = sem("uv_ready")
        sq_ready = sem("sq_ready")
        ss_done = sem("ss_done")
        ss_clamped = sem("ss_clamped")
        rn_ready = sem("rn_ready")
        q_ready = sem("q_ready")
        bonus_done = sem("bonus_done")
        up_done = sem("up_done")
        up_act = sem("up_act")
        logs_ready = sem("logs_ready")
        exps_ready = sem("exps_ready")
        kr_ready = sem("kr_ready")
        krbd_ready = sem("krbd_ready")
        ab_ready = sem("ab_ready")
        scores_done = sem("scores_done")
        g_ready = sem("g_ready")
        l_ready = sem("l_ready")
        init_ready = sem("init_ready")
        ab_turned = sem("ab_turned")
        abt_ready = sem("abt_ready")
        q_done = sem("q_done")
        qc_ready = sem("qc_ready")
        qbd_ready = sem("qbd_ready")
        v_done = sem("v_done")
        w_done = sem("w_done")
        wc_ready = sem("wc_ready")
        wbd_ready = sem("wbd_ready")
        ys1_ready = sem("ys1_ready")
        ys_var = sem("ys_var")
        ys_rstd = sem("ys_rstd")
        yn_ready = sem("yn_ready")
        ybd_ready = sem("ybd_ready")
        yt_done = sem("yt_done")
        gg_turned = sem("gg_turned")
        gg_ready = sem("gg_ready")
        og_ready = sem("og_ready")
        gla_in = sem("gla_in")
        head_done = sem("head_done")
        gz_ready = sem("gz_ready")
        g_turned = sem("g_turned")
        g_qk = sem("g_qk")
        g_gate = sem("g_gate")
        g_x = sem("g_x")
        g_soft = sem("g_soft")
        g_logs = sem("g_logs")
        g_exps = sem("g_exps")
        g_prod = sem("g_prod")
        g_att = sem("g_att")
        g_kdt_done = sem("g_kdt_done")
        g_kdt = sem("g_kdt")
        g_attm = sem("g_attm")
        g_kv = sem("g_kv")
        g_states = sem("g_states")
        g_o = sem("g_o")
        g_sq = sem("g_sq")
        g_var = sem("g_var")
        g_rstd = sem("g_rstd")
        g_on = sem("g_on")
        g_oT = sem("g_oT")
        split_hi = sem("split_hi")
        split_lo = sem("split_lo")
        ln_in = sem("ln_in")
        diag_ready = sem("diag_ready")
        gate_mm = sem("gate_mm")
        gate_out = sem("gate_out")
        end_var = sem("end_var")
        end_rstd = sem("end_rstd")
        x_ready = sem("x_ready")
        pb_done = sem("pb_done")
        pb_free = sem("pb_free")
        py_done = sem("py_done")
        py_free = sem("py_free")
        gu_turned = sem("gu_turned")
        guh_ready = sem("guh_ready")
        gul_ready = sem("gul_ready")
        ysum_zero = sem("ysum_zero")
        lam_in = sem("lam_in")
        lam_prod = sem("lam_prod")
        lam_exp = sem("lam_exp")
        lam_mm = sem("lam_mm")
        at_rot0 = sem("at_rot0")
        at_rot1 = sem("at_rot1")
        at_turned = sem("at_turned")
        at_T = sem("at_T")
        at_scores = sem("at_scores")
        at_bias = sem("at_bias")
        at_exp = sem("at_exp")
        at_p = sem("at_p")
        at_pturned = sem("at_pturned")
        at_pT = sem("at_pT")
        at_o = sem("at_o")
        at_sq = sem("at_sq")
        at_var = sem("at_var")
        at_rstd = sem("at_rstd")
        at_on = sem("at_on")
        at_oT = sem("at_oT")
        at_scaled = sem("at_scaled")
        at_hi = sem("at_hi")
        at_done = sem("at_done")
        out_sem = sem("out_sem")
        x_done = [sem(f"x_done{d}") for d in range(2)]
        xs_ready = [sem(f"xs_ready{d}") for d in range(2)]
        u_ready = [sem(f"u_ready{d}") for d in range(2)]
        s_done = [sem(f"s_done{d}") for d in range(2)]
        s_ready = [sem(f"s_ready{d}") for d in range(2)]
        u_done = [sem(f"u_done{d}") for d in range(2)]
        y_done = [sem(f"y_done{d}") for d in range(2)]

        block = ctx.enter_context(nc.Block())
        cond = ada_w.rearrange("a b (s i p) (j w) -> (a b) j s p i w", p=P, i=UK, w=W)

        def load_unit(sp, c, s, src, width=W, first=False):
            if not first:
                sp.wait_ge(lo_done, c * 4 + s + 1)
            sp.dma_start(raw[:, s, :, 0:width], src).then_inc(raw_in[s], 16)

        def load_cond(sp, j, s, src, first=False):
            if not first:
                sp.wait_ge(ada_step, j * 17 + (5 + 4 * (s - 2) if s >= 2 else 4 * s - 4))
            sp.dma_start(adaw[:, s % 2], src).then_inc(adaw_in[s % 2], 16)

        def high(act, c, s, width=W):
            act.wait_ge(raw_in[s], c * 16 + 16)
            act.wait_ge(unit_done, c * 4 + s + 1)
            act.activation(wh[:, s % 2, :, 0:width], raw[:, s, :, 0:width], ACT.Copy).then_inc(hi_done, 1)

        def low(dve, c, s, width=W):
            dve.wait_ge(hi_done, c * 4 + s + 1)
            dve.tensor_tensor(wl[:, s % 2, :, 0:width], raw[:, s, :, 0:width],
                              wh[:, s % 2, :, 0:width].bitcast(F32), ALU.subtract).then_inc(lo_done, 1)

        def cond_unit(dve, j, s):
            dve.wait_ge(adaw_in[s % 2], j * 32 + 16 * (s // 2) + 16)
            for i in range(UK):
                k = UK * s + i
                if k < 2:
                    dve.wait_ge(ada_step, j * 17 + 1)
                    dve.tensor_scalar(acc[:, k % 2], adaw[:, s % 2, i], silu_c[:, k:k + 1], None,
                                      ALU.mult).then_inc(ada_step, 1)
                else:
                    dve.wait_ge(ada_step, j * 17 + k)
                    dve.scalar_tensor_tensor(acc[:, k % 2], adaw[:, s % 2, i], silu_c[:, k:k + 1],
                                             acc[:, k % 2], ALU.mult, ALU.add).then_inc(ada_step, 1)

        def cond_sum(dve, j, first=False):
            dve.wait_ge(ada_step, j * 17 + 17)
            if not first:
                dve.wait_ge(ada_cols, j)
            dve.tensor_tensor(asum[:], acc[:, 0], acc[:, 1], ALU.add).then_inc(ada_step, 1)

        def cond_cols(pe, j, first=False):
            pe.wait_ge(ada_step, j * 17 + 18)
            if not first:
                pe.wait_ge(ada_out, j)
            for m in range(4):
                mm = pe.matmul(pt[:, 1, m:m + 1], asum[:, m * P:(m + 1) * P], ones[:, 0:1], start=(m == 0),
                               stop=True, skip_group_check=True)
            mm.then_inc(ada_cols, 1)

        def cond_store(dve, j):
            dve.wait_ge(ada_cols, j + 1)
            dve.tensor_tensor(ada_flat[:, bass.ds(j * 4, 4)], pt[:, 1, 0:4], tab[:, bass.ds(j * 4 + T_ADA, 4)],
                              ALU.add).then_inc(ada_out, 1)

        def multiply(pe, c, s, lhs, bank, width=W, start=True, stop=True, tile0=None, k0=None):
            pe.wait_ge(lo_done, c * 4 + s + 5)
            hi, lo = lhs
            for i in range(NT):
                for k in range(UK):
                    kk = (k0 if k0 is not None else UK * s) + k
                    a_hi, a_lo = hi[:, kk, i * P:(i + 1) * P], lo[:, kk, i * P:(i + 1) * P]
                    w_hi, w_lo = wh[:, s % 2, k, 0:width], wl[:, s % 2, k, 0:width]
                    o = bank[:, i, 0:width]
                    pe.matmul(o, a_hi, w_hi, start=start and k == 0, stop=False)
                    pe.matmul(o, a_hi, w_lo, start=False, stop=False)
                    mm = pe.matmul(o, a_lo, w_hi, start=False, stop=stop and k == UK - 1)
                if i == 0 and tile0 is not None:
                    mm.then_inc(tile0, 1)
            mm.then_inc(unit_done, 1)

        def project(pe, c, n, lhs, done, free, bank, width=W):
            for s in range(4):
                if s == 0:
                    pe.wait_ge(free, n * 2 + 2)
                multiply(pe, c, s, lhs, bank, width, start=(s == 0), stop=(s == 3), tile0=done if s == 3 else None)

        def turn_pe(pe, call):
            for g in range(KT // 2):
                n = call * 8 + g
                if n >= 2:
                    pe.wait_ge(h_scaled, n - 1)
                for j in range(2):
                    for i in range(NT):
                        mm = pe.transpose(py[:, g % 2, j * SEQ + i * P:j * SEQ + (i + 1) * P],
                                          xt[:, i, (2 * g + j) * P:(2 * g + j + 1) * P], ident)
                mm.then_inc(tr_done, 1)

        def turn_act(act, call):
            for g in range(KT // 2):
                n = call * 8 + g
                act.wait_ge(h_scaled, n + 1)
                act.activation(hth[:, 2 * g:2 * g + 2, :], htmp[:, g % 2], ACT.Copy).then_inc(h_hi, 1)

        def turn_dve(dve, call, sub):
            dve.tensor_scalar(small[:, 0:16], ada[:, sub, 16:32], 1.0, None, ALU.add)
            dve.drain()

            def lower(g):
                dve.wait_ge(h_hi, call * 8 + g + 1)
                dve.tensor_tensor(htl[:, 2 * g:2 * g + 2, :], htmp[:, g % 2],
                                  hth[:, 2 * g:2 * g + 2, :].bitcast(F32), ALU.subtract).then_inc(h_lo, 1)
            for g in range(KT // 2):
                dve.wait_ge(tr_done, call * 8 + g + 1)
                if g >= 2:
                    dve.wait_ge(h_lo, call * 8 + g - 1)
                for j in range(2):
                    k = 2 * g + j
                    ins = dve.tensor_scalar(htmp[:, g % 2, j], py[:, g % 2, j * SEQ:(j + 1) * SEQ],
                                            small[:, k:k + 1], ada[:, sub, k:k + 1], ALU.mult, ALU.add)
                ins.then_inc(h_scaled, 1)
                if g:
                    lower(g - 1)
            lower(KT // 2 - 1)

        def split_act(act, call):
            for g in range(KT // 2):
                act.activation(hth[:, 2 * g:2 * g + 2], xf[:, 2 * g:2 * g + 2], ACT.Copy).then_inc(split_hi, 1)

        def split_dve(dve, call):
            for g in range(KT // 2):
                dve.wait_ge(split_hi, call * 8 + g + 1)
                dve.tensor_tensor(htl[:, 2 * g:2 * g + 2], xf[:, 2 * g:2 * g + 2],
                                  hth[:, 2 * g:2 * g + 2].bitcast(F32), ALU.subtract).then_inc(split_lo, 1)

        def end_load(act, n, c):
            act.wait_ge(unit_done, c * 4 + 6)
            act.dma_start(lng[:], ln_g[n // 2, n % 2].partition_broadcast(P)).then_inc(ln_in, 16)
            act.dma_start(lnb[:], ln_b[n // 2, n % 2].partition_broadcast(P)).then_inc(ln_in, 16)

        def end_pe(pe, n):
            for g in range(4):
                pe.wait_ge(diag_ready, n * 4 + g + 1)
                if n * 4 + g >= 2:
                    pe.wait_ge(gate_out, n * 4 + g - 1)
                for m in range(4):
                    mm = pe.matmul(pb[:, g % 2, m * P:(m + 1) * P], ones, diag[:, m], start=True, stop=True)
                mm.then_inc(gate_mm, 1)

        def end_act(act, n):
            for g in range(4):
                act.wait_ge(gate_mm, n * 4 + g + 1)
                act.activation(gate_bc[:, g * W:(g + 1) * W], pb[:, g % 2], ACT.Copy, bias=1.0).then_inc(gate_out, 1)
            for i in range(NT):
                act.wait_ge(end_var, n * NT + i + 1)
                act.activation(small[:, 36 + i:37 + i], small[:, 34 + i:35 + i], ACT.Ln)
                act.drain()
                act.activation(small[:, 38 + i:39 + i], small[:, 36 + i:37 + i], ACT.Exp, scale=-0.5).then_inc(end_rstd, 1)

        def end_dve(dve, n):
            for g in range(4):
                if g or n:
                    dve.wait_ge(gate_mm, n * 4 + g)
                for m in range(4):
                    k = 32 + 4 * g + m
                    ins = dve.tensor_scalar(diag[:, m], ident, ada[:, n, k:k + 1], None, ALU.mult)
                ins.then_inc(diag_ready, 1)
            dve.wait_ge(gate_out, n * 4 + 4)
            stats = small[:, 40:40 + 24].rearrange("p (c s) -> p c s", s=6)
            for i in range(NT):
                dve.tensor_tensor(ysum[:, i], ysum[:, i], gate_bc[:], ALU.mult)
                dve.drain()
                dve.scalar_tensor_tensor(xt[:, i], xt[:, i], ALPHA, ysum[:, i], ALU.mult, ALU.add)
                dve.drain()
                for c in range(4):
                    dve.bn_stats(stats[:, c], xt[:, i, c * W:(c + 1) * W])
                dve.drain()
                dve.bn_aggr(small[:, 64 + 2 * i:66 + 2 * i], stats.rearrange("p c s -> p (c s)"))
                dve.drain()
                dve.tensor_scalar(small[:, 34 + i:35 + i], small[:, 65 + 2 * i:66 + 2 * i], EPS, None, ALU.add).then_inc(end_var, 1)
            dve.wait_ge(ln_in, n * 32 + 32)
            for i in range(NT):
                dve.wait_ge(end_rstd, n * NT + i + 1)
                dve.tensor_scalar(xt[:, i], xt[:, i], small[:, 64 + 2 * i:65 + 2 * i], small[:, 38 + i:39 + i],
                                  ALU.subtract, ALU.mult)
            dve.drain()
            for i in range(NT):
                dve.tensor_tensor(xt[:, i], xt[:, i], lng[:], ALU.mult)
            dve.drain()
            for i in range(NT):
                dve.tensor_tensor(xt[:, i], xt[:, i], lnb[:], ALU.add).then_inc(x_ready, 1)

        def out_sp(sp, c0, wv, j0=None, sub=None):
            for q in range(4):
                for s in range(4):
                    load_unit(sp, c0 + q, s, wv[s, :, :, q * W:(q + 1) * W])
                    if j0 is not None:
                        load_cond(sp, j0 + q, s, cond[sub, (j0 + q) % 12, s])

        def out_act(act, c0, n0):
            for q in range(4):
                for s in range(4):
                    high(act, c0 + q, s)
                    if q and s == 0:
                        act.wait_ge(pa_done, n0 + q)
                        act.activation(ysum[:, 0, (q - 1) * W:q * W], pa[:, 0], ACT.Copy).then_inc(pa_free, 1)
                    if q and s == 1:
                        act.wait_ge(unit_done, (c0 + q) * 4 + 2)
                        act.activation(ysum[:, 1, (q - 1) * W:q * W], pa[:, 1], ACT.Copy).then_inc(pa_free, 1)
            act.wait_ge(pa_done, n0 + 4)
            act.activation(ysum[:, 0, 3 * W:], pa[:, 0], ACT.Copy).then_inc(pa_free, 1)
            act.wait_ge(unit_done, (c0 + 4) * 4 + 2)
            act.activation(ysum[:, 1, 3 * W:], pa[:, 1], ACT.Copy).then_inc(pa_free, 1)

        def out_dve(dve, c0, j0=None):
            for q in range(4):
                for s in range(4):
                    low(dve, c0 + q, s)
                    if j0 is not None:
                        cond_unit(dve, j0 + q, s)
                if j0 is not None:
                    cond_sum(dve, j0 + q)
                    cond_store(dve, j0 + q)

        def out_pe(pe, c0, n0, j0=None):
            for q in range(4):
                project(pe, c0 + q, n0 + q, (hth, htl), pa_done, pa_free, pa)
                if j0 is not None:
                    cond_cols(pe, j0 + q)

        def rotate(eng, t, i):
            src = qkv[:, i, 0:2 * D].rearrange("p (j n) -> p j n", j=2)[:, :, bass.ds(t * P, P)].rearrange(
                "p j (c f) -> p j c f", c=2)
            x1, x2 = src[:, :, :, 0:32], src[:, :, :, 32:64]
            o1, o2 = A_qk[:, i, :, :, 0:32], A_qk[:, i, :, :, 32:64]

            def wave(at):
                return cst[:, at + 32 * i:at + 32 * i + 32].unsqueeze(1).unsqueeze(1).to_broadcast((P, 2, 2, 32))
            cos, sin = wave(C_COS), wave(C_SIN)
            eng.tensor_tensor(o1, x1, cos, ALU.mult)
            eng.tensor_tensor(A_t[:, i], x2, sin, ALU.mult)
            eng.tensor_tensor(o2, x2, cos, ALU.mult)
            eng.drain()
            eng.tensor_tensor(o1, o1, A_t[:, i], ALU.subtract)
            eng.drain()
            eng.tensor_tensor(A_t[:, i], x1, sin, ALU.mult)
            eng.drain()
            eng.tensor_tensor(o2, o2, A_t[:, i], ALU.add)

        def turn_pe_at(pe, n):
            pe.wait_ge(x_ready, 2 * n)
            turn_pe(pe, n)
            pe.wait_ge(h_lo, 8 * n + 8)

        def in_act(act, c0, dest, last):
            high(act, c0, 0)
            high(act, c0, 1)
            with act.Fori(0, 11) as t:
                high(act, t + c0, 2)
                high(act, t + c0, 3)
                act.wait_ge(pa_done, t + c0 + 1 - PA_SKIP[c0])
                act.activation(dest[:, 0, bass.ds(t * W, W)], pa[:, 0], ACT.Copy).then_inc(pa_free, 1)
                high(act, t + c0 + 1, 0)
                act.wait_ge(unit_done, t * 4 + 4 * c0 + 6)
                act.activation(dest[:, 1, bass.ds(t * W, W)], pa[:, 1], ACT.Copy).then_inc(pa_free, 1)
                high(act, t + c0 + 1, 1)
            high(act, c0 + 11, 2)
            high(act, c0 + 11, 3)
            act.wait_ge(pa_done, c0 + 12 - PA_SKIP[c0])
            act.activation(dest[:, 0, 11 * W:12 * W], pa[:, 0], ACT.Copy).then_inc(pa_free, 1)
            act.wait_ge(unit_done, 4 * (c0 + 11) + 6)
            act.activation(dest[:, 1, 11 * W:12 * W], pa[:, 1], ACT.Copy).then_inc(pa_free, 1)

        def ffn_sp(sp, c0, layer, j0=None):
            w_in = ffn_w_in[layer].rearrange("(s i p) (h g w) -> h g s p i w", p=P, i=UK, h=2, w=W)
            w_out = ffn_w_out[layer].rearrange("(g i p) (q w) -> g q p i w", p=P, i=UK, w=W)

            def cond_at(j, n):
                if j0 is not None and n % 2:
                    load_cond(sp, j, n // 2, cond[2, bass.ds(j - j0, 1), n // 2])
            for h in range(2):
                for s in range(4):
                    load_unit(sp, c0 + h, s, w_in[h, 0, s])
                    cond_at(j0, 4 * h + s)
            with sp.Fori(1, FG) as g:
                c = g * 3 + (c0 - 1)
                for h in range(2):
                    for s in range(4):
                        load_unit(sp, c + h, s, w_in[h, bass.ds(g, 1), s])
                        cond_at(g + (j0 or 0), 4 * h + s)
                for q in range(4):
                    load_unit(sp, c + 2, q, w_out[bass.ds(g - 1, 1), q])
            for q in range(4):
                load_unit(sp, c0 + 32, q, w_out[FG - 1, q])
                if j0 is not None:
                    load_cond(sp, j0 + 11, q, cond[2, 11, q])

        def ffn_act(act, c0, f, n_pa):
            def gate_up(c, g):
                for s in range(1, 4):
                    high(act, c, s)
                high(act, c + 1, 0)
                if isinstance(g, int) and g == 0:
                    pass
                else:
                    act.wait_ge(gu_turned, g)
                act.wait_ge(pa_done, g + (n_pa - f + 1))
                act.activation(gu[:, 0], pa[:, 0], ACT.Silu).then_inc(pa_free, 1)
                high(act, c + 1, 1)
                act.wait_ge(unit_done, c * 4 + 6)
                act.activation(gu[:, 1], pa[:, 1], ACT.Silu).then_inc(pa_free, 1)
                high(act, c + 1, 2)
                high(act, c + 1, 3)

            def turned(g):
                act.wait_ge(gu_turned, g + 1)
                act.activation(guh[:, 0:2].rearrange("p k t -> p (k t)"), pt[:, 0], ACT.Copy)
                act.activation(guh[:, 2:4].rearrange("p k t -> p (k t)"), pb[:, 0], ACT.Copy).then_inc(guh_ready, 1)
            high(act, c0, 0)
            gate_up(c0, f)
            high(act, c0 + 2, 0)
            turned(f)
            with act.Fori(1, FG) as g:
                c = g * 3 + (c0 - 1)
                gate_up(c, g + f)
                for q in range(4):
                    high(act, c + 2, q)
                high(act, c + 3, 0)
                turned(g + f)
            for q in range(1, 4):
                high(act, c0 + 32, q)

        def ffn_dve(dve, c0, f, u0, j0=None):
            def cond_at(j, n):
                if j0 is not None and n % 2:
                    cond_unit(dve, j, n // 2)

            def product(i, c, g):
                if i == 0:
                    dve.wait_ge(pb_done, g + 1)
                    dve.wait_ge(pa_free, 2 * g + 2 * (n_of[f] - f) + 3)
                else:
                    dve.wait_ge(unit_done, c * 4 + 10)
                    dve.wait_ge(pa_free, 2 * g + 2 * (n_of[f] - f) + 4)
                dve.tensor_tensor(gu[:, i], gu[:, i], pb[:, i], ALU.mult).then_inc(pb_free, 1)

            def add(c, q, u):
                dve.wait_ge(py_done, u + 1)
                dve.tensor_tensor(ysum[:, 0, q * W:(q + 1) * W], ysum[:, 0, q * W:(q + 1) * W], py[:, 0], ALU.add).then_inc(py_free, 1)
                dve.wait_ge(unit_done, c * 4 + q + 3)
                dve.tensor_tensor(ysum[:, 1, q * W:(q + 1) * W], ysum[:, 1, q * W:(q + 1) * W], py[:, 1], ALU.add).then_inc(py_free, 1)

            def lower(g):
                dve.wait_ge(guh_ready, g + 1)
                dve.tensor_tensor(gul[:, 0:2].rearrange("p k t -> p (k t)"), pt[:, 0],
                                  guh[:, 0:2].rearrange("p k t -> p (k t)").bitcast(F32), ALU.subtract)
                dve.tensor_tensor(gul[:, 2:4].rearrange("p k t -> p (k t)"), pb[:, 0],
                                  guh[:, 2:4].rearrange("p k t -> p (k t)").bitcast(F32), ALU.subtract).then_inc(gul_ready, 1)
            low(dve, c0, 0)
            for n in range(1, 8):
                low(dve, c0 + n // 4, n % 4)
                cond_at(j0, n)
            if j0 is not None:
                cond_sum(dve, j0)
            low(dve, c0 + 2, 0)
            product(0, c0, f)
            product(1, c0, f)
            lower(f)
            if j0 is not None:
                cond_store(dve, j0)
            dve.wait_ge(ysum_zero, 1 if f == 0 else 2)
            with dve.Fori(1, FG) as g:
                c = g * 3 + (c0 - 1)
                for n in range(1, 8):
                    low(dve, c + n // 4, n % 4)
                    cond_at(g + (j0 or 0), n)
                if j0 is not None:
                    cond_sum(dve, g + j0)
                low(dve, c + 2, 0)
                product(0, c, g + f)
                product(1, c, g + f)
                for q in range(1, 4):
                    low(dve, c + 2, q)
                    add(c + 2, q - 1, g * 4 + (u0 - 4 + q - 1))
                low(dve, c + 3, 0)
                add(c + 2, 3, g * 4 + (u0 - 1))
                lower(g + f)
                if j0 is not None:
                    cond_store(dve, g + j0)
            for q in range(1, 4):
                low(dve, c0 + 32, q)
                add(c0 + 32, q - 1, u0 + 40 + q - 1)
                if j0 is not None:
                    cond_unit(dve, j0 + 11, q - 1)
            add(c0 + 32, 3, u0 + 43)
            if j0 is not None:
                cond_unit(dve, j0 + 11, 3)
                cond_sum(dve, j0 + 11)
                cond_store(dve, j0 + 11)

        def ffn_pe(pe, c0, f, u0, j0=None):
            def turn(g):
                pe.wait_ge(pb_free, g * 2 + 4)
                for k in range(UK):
                    bank = pt[:, 0] if k < 2 else pb[:, 0]
                    for i in range(NT):
                        at = (k % 2) * SEQ + i * P
                        mm = pe.transpose(bank[:, at:at + P], gu[:, i, k * P:(k + 1) * P], ident)
                mm.then_inc(gu_turned, 1)

            def output(c, u, g):
                pe.wait_ge(gul_ready, g + 1)
                for q in range(4):
                    pe.wait_ge(py_free, (u + q) * 2 + 2)
                    multiply(pe, c, q, (guh, gul), py, tile0=py_done, k0=0)
            project(pe, c0, n_of[f], (hth, htl), pa_done, pa_free, pa)
            project(pe, c0 + 1, f, (hth, htl), pb_done, pb_free, pb)
            turn(f)
            if j0 is not None:
                cond_cols(pe, j0)
            with pe.Fori(1, FG) as g:
                c = g * 3 + (c0 - 1)
                project(pe, c, g + n_of[f], (hth, htl), pa_done, pa_free, pa)
                pe.wait_ge(gul_ready, g + f)
                project(pe, c + 1, g + f, (hth, htl), pb_done, pb_free, pb)
                output(c + 2, g * 4 + (u0 - 4), g + (f - 1))
                turn(g + f)
                if j0 is not None:
                    cond_cols(pe, g + j0)
            output(c0 + 32, u0 + 40, f + 10)
            if j0 is not None:
                cond_cols(pe, j0 + 11)

        ab_w = ab_w_in[0].rearrange("(s i p) n -> s p i n", p=P, i=UK)
        LASTW = Z - (ABC - 1) * W

        def vectors():
            yield T_LN_G, ln_g.rearrange("a b (k p) -> (a b k) p", p=P)
            yield T_LN_B, ln_b.rearrange("a b (k p) -> (a b k) p", p=P)
            yield T_MU, rwkv_mu[0, 0:3 * RW].rearrange("(k p) -> k p", p=P)
            yield T_MU + 24, rwkv_mu[0:1, Z_WD:Z_AD]
            yield T_MU + 25, rwkv_mu[0:1, Z_AD:Z_GD]
            yield T_MU + 26, rwkv_mu[0, Z_GD:Z_Q].rearrange("(k p) -> k p", p=P)
            yield T_W0, rwkv_w0[0].rearrange("a (k p) -> (a k) p", p=P)
            yield T_A0, rwkv_a0[0].rearrange("(k p) -> k p", p=P)
            yield T_KK, rwkv_k_k[0].rearrange("(k p) -> k p", p=P)
            yield T_KA, rwkv_k_a[0].rearrange("(k p) -> k p", p=P)
            yield T_RK, rwkv_r_k[0].rearrange("(k h) n -> k (h n)", h=2)
            yield T_GNG, rwkv_gn_g[0].rearrange("(k p) -> k p", p=P)
            yield T_GNB, rwkv_gn_b[0].rearrange("(k p) -> k p", p=P)
            yield T_GB, gla_gate_b[0].rearrange("a (k p) -> (a k) p", p=P)
            yield T_NG, gla_norm_g[0].rearrange("(k p) -> k p", p=P)
            yield T_SUB, diff_subln_g[0:1, :]
            yield T_C, c_in[0].rearrange("(k p) -> k p", p=P)
            ab = ada_b.rearrange("a b (k p) -> (a b k) p", p=P)
            yield T_ADA, ab[0:96]
            yield T_ADA + 96, ab[96:192]

        @block.sync
        def _(sp):
            sp.dma_start(cst[:], consts).then_inc(const_in, 16)
            sp.wait_ge(rows_zero, 1)
            for col, src in vectors():
                tile = max(i for i in range(4) if TABS[i] <= col)
                r = col - TABS[tile]
                sp.dma_start(rows[r:r + src.shape[0], tile, 0:src.shape[1]], src).then_inc(rows_in, 16)
            for s in range(4):
                load_cond(sp, 0, s, cond[0, 0, s], first=(s < 2))
            sp.dma_start(xt[:], x_in[0].rearrange("(i p) d -> p i d", p=P)).then_inc(x_in_sem, 16)
            with sp.Fori(1, 8) as j:
                for s in range(4):
                    load_cond(sp, j, s, cond[0, bass.ds(j, 1), s])
            for s in range(4):
                load_unit(sp, 0, s, ab_w[s, :, :, 0:W], first=True)
                load_cond(sp, 8, s, cond[0, 8, s])
            cond_all = cond.rearrange("a j s p i w -> (a j) s p i w") if False else None
            with sp.Fori(1, 4) as c:
                for s in range(4):
                    load_unit(sp, c, s, ab_w[s, :, :, bass.ds(c * W, W)])
                    load_cond(sp, c + 8, s, cond[0, bass.ds(c + 8, 1), s])
            with sp.Fori(4, 12) as c:
                for s in range(4):
                    load_unit(sp, c, s, ab_w[s, :, :, bass.ds(c * W, W)])
                    load_cond(sp, c + 8, s, cond[1, bass.ds(c - 4, 1), s])
            for s in range(4):
                load_unit(sp, 12, s, ab_w[s, :, :, 12 * W:Z], LASTW)
            w_up_v = rwkv_w_up[0].rearrange("a r n -> r a n")
            g_up_v = rwkv_g_up[0].rearrange("(i p) n -> p i n", p=P)
            with sp.Fori(0, PAIRS) as t:
                sp.wait_ge(pair_done, t + 1)
                sp.dma_start(R_up[0:LORA, 0:2, :], w_up_v[:, :, bass.ds(t * P, P)]).then_inc(up_in, 16)
                sp.dma_start(R_up[0:LORA, 2, :], rwkv_a_up[0][:, bass.ds(t * P, P)]).then_inc(up_in, 16)
                sp.dma_start(R_up[:, 3:5, :], g_up_v[:, :, bass.ds(t * P, P)]).then_inc(up_in, 16)
            gup_v = gla_gate_up[0].rearrange("a r n -> r a n")
            sp.wait_ge(pair_done, 1 + PAIRS)
            with sp.Fori(0, GH) as t:
                sp.wait_ge(head_done, t + 1)
                sp.dma_start(L_up[0:GLORA], gup_v[:, :, bass.ds(t * DK, DK)]).then_inc(gla_in, 16)
            sp.wait_ge(head_done, 1 + GH)
            ab_wo = ab_w_out[0].rearrange("(s i p) n -> s p i n", p=P, i=UK)
            out_sp(sp, 13, ab_wo, 20, 1)
            ffn_sp(sp, C_FFN0, 0, 24)
            dw = diff_w_in[0].rearrange("(s i p) n -> s p i n", p=P, i=UK)
            with sp.Fori(0, 12) as t:
                for s in range(4):
                    load_unit(sp, t + C_DIFF, s, dw[s, :, :, bass.ds(t * W, W)])
                    load_cond(sp, t + 36, s, cond[3, bass.ds(t, 1), s])
            out_sp(sp, C_OUT1, diff_w_out[0].rearrange("(s i p) n -> s p i n", p=P, i=UK))
            ffn_sp(sp, C_FFN1, 1)
            out_v = out[0].rearrange("(i p) d -> p i d", p=P)
            for i in range(NT):
                sp.wait_ge(x_ready, 7 + i)
                sp.dma_start(out_v[:, i], xt[:, i]).then_inc(out_sem, 16)
            sp.wait_ge(out_sem, 32)

        @block.gpsimd
        def _(pool):
            pool.memset(rows[:], 0.0).then_inc(rows_zero, 1)
            pool.wait_ge(unit_done, 2 + 4 * ABC)
            for tile in (R_Kbd, R_Rbd, R_Lbd, R_Wbd, R_Qbd):
                pool.memset(tile[:], 0.0)
            pool.memset(R_vp[:], 0.0)
            pool.memset(R_G[:].rearrange("p a b c -> p (a b c)")[:, 0:4 * (SEQ + 2)], 0.0)
            pool.drain().then_inc(bd_zero, 1)
            pool.wait_ge(lora_ready, 3)
            pool.wait_ge(pa_free, 2 + 2 * ABC)
            with pool.Fori(0, PAIRS) as t:
                pool.wait_ge(pair_done, t + 1)
                pool.sem_inc(pool_passed, 1)
                pool.memset(R_zf[:], 0.0)
                for i in range(NT):
                    src = z[:, i, 0:3 * RW].rearrange("p (j n) -> p j n", n=RW)
                    cp = pool.tensor_copy(R_zs[:, i], src[:, :, bass.ds(t * P, P)])
                pool.drain().then_inc(zs_ready, 1)
                pool.memset(R_UV[:], 0.0)
                pool.tensor_copy(R_Wbd[:], ident.unsqueeze(1).to_broadcast((P, NU, P)))
                pool.wait_ge(rkv_mixed, t + 1)
                pool.sem_inc(pool_passed, 1)
                pool.tensor_copy(R_vc[:], cst[:, C_I2:C_I2 + CH].unsqueeze(1).to_broadcast((P, NU, CH)))
                pool.tensor_copy(R_wc[:], cst[:, C_I2:C_I2 + CH].unsqueeze(1).to_broadcast((P, NU, CH)))
                pool.drain().then_inc(init_ready, 1)
                pool.wait_ge(kr_ready, t + 1)
                pool.sem_inc(pool_passed, 1)
                pool.tensor_copy(R_Kbd[0:CH, :, 0:CH], R_KR[0:CH, :, 0:CH])
                pool.tensor_copy(R_Rbd[0:CH, :, 0:CH], R_KR[0:CH, :, CH:P])
                pool.drain()
                pool.tensor_copy(R_Kbd[CH:P, :, CH:P], R_KR[CH:P, :, 0:CH])
                pool.tensor_copy(R_Rbd[CH:P, :, CH:P], R_KR[CH:P, :, CH:P])
                pool.drain().then_inc(krbd_ready, 1)
            pool.wait_ge(pair_done, 1 + PAIRS)
            pool.sem_inc(pool_passed, 1)
            with pool.Fori(0, GH) as t:
                pool.wait_ge(head_done, t + 1)
                pool.sem_inc(pool_passed, 1)
                for i in range(NT):
                    src = z[:, i, Z_Q:Z_V].rearrange("p (j n) -> p j n", n=GH * DK)
                    pool.tensor_copy(L_zs[:, i], src[:, :, bass.ds(t * DK, DK)])
                    pool.tensor_copy(L_v[:, i], z[:, i, bass.ds(t * DV + Z_V, DV)])
                pool.drain().then_inc(gz_ready, 1)
            pool.wait_ge(x_ready, 2)
            pool.memset(ysum[:], 0.0).then_inc(ysum_zero, 1)
            def rotary_pool(t):
                rotate(pool, t, 1)
            with pool.Fori(0, DH) as t:
                pool.wait_ge(at_done, t + 1)
                pool.sem_inc(pool_passed, 1)
                rotate(pool, t, 1)
                pool.drain().then_inc(at_rot1, 1)
            pool.wait_ge(x_ready, 6)
            pool.memset(ysum[:], 0.0).then_inc(ysum_zero, 1)

        @block.scalar
        def _(act):
            act.wait_ge(tab_turned, 1)
            act.activation(tab[:], pa[:, 0, 0:T_N], ACT.Copy).then_inc(tab_copied, 1)
            act.wait_ge(tab_copied, 1)
            act.activation(silu_c[:], tab[:, T_C:T_C + KT], ACT.Silu).then_inc(silu_ready, 1)
            turn_act(act, 0)

            def store_z(c, width=W):
                act.wait_ge(pa_done, c + 1)
                act.activation(z[:, 0, bass.ds(c * W, width)], pa[:, 0, 0:width], ACT.Copy).then_inc(pa_free, 1)
                act.wait_ge(unit_done, c * 4 + 6)
                act.activation(z[:, 1, bass.ds(c * W, width)], pa[:, 1, 0:width], ACT.Copy).then_inc(pa_free, 1)

            high(act, 0, 0)
            high(act, 0, 1)
            with act.Fori(0, 11) as c:
                high(act, c, 2)
                high(act, c, 3)
                act.wait_ge(pa_done, c + 1)
                act.activation(z[:, 0, bass.ds(c * W, W)], pa[:, 0], ACT.Copy).then_inc(pa_free, 1)
                high(act, c + 1, 0)
                act.wait_ge(unit_done, c * 4 + 6)
                act.activation(z[:, 1, bass.ds(c * W, W)], pa[:, 1], ACT.Copy).then_inc(pa_free, 1)
                high(act, c + 1, 1)
            high(act, 11, 2)
            high(act, 11, 3)
            store_z(11)
            for s in range(4):
                high(act, 12, s, LASTW)
            store_z(12, LASTW)
            act.wait_ge(bd_zero, 1)
            act.wait_ge(lora_turned, 1)
            pad4 = R_G[:].rearrange("p a b c -> p (a b c)")[:, 0:4 * (SEQ + 2)].rearrange("p (j t) -> p j t", t=SEQ + 2)
            act.activation(pad4[0:LORA, 0:2, 1:1 + SEQ], py[0:LORA, 0].rearrange("p (j t) -> p j t", t=SEQ), ACT.Copy)
            act.activation(pad4[:, 2:4, 1:1 + SEQ], py[:, 1].rearrange("p (j t) -> p j t", t=SEQ),
                           ACT.Copy).then_inc(lora_padded, 1)
            act.wait_ge(lora_mixed, 1)
            act.activation(R_lora[0:LORA, 0], R_lora[0:LORA, 0], ACT.Tanh).then_inc(lora_ready, 1)
            act.activation(R_lora[:, 2:4], R_lora[:, 2:4], ACT.Sigmoid).then_inc(lora_ready, 1)
            with act.Fori(0, PAIRS) as t:
                act.wait_ge(rk_turned, t + 1)
                act.activation(R_zf[:, 0:2, 1:1 + SEQ], pt[:, 0].rearrange("p (j t) -> p j t", t=SEQ), ACT.Copy)
                act.activation(R_zf[:, 2, 1:1 + SEQ], pt[:, 1, 0:SEQ], ACT.Copy).then_inc(zf_ready, 1)
                act.wait_ge(up_done, t + 1)
                for j in range(3):
                    act.activation(R_lw[:, j], pa[:, j // 2, (j % 2) * SEQ:(j % 2 + 1) * SEQ], ACT.Exp,
                                   bias=neg[:, bass.ds(t + 8 * j, 1)], scale=-1.0)
                act.activation(R_g[:], pa[:, 1, SEQ:W], ACT.Copy).then_inc(up_act, 1)
                act.wait_ge(v_turned, t + 1)
                act.wait_ge(init_ready, t + 1)
                for d in range(2):
                    us = slice(d * NCH, (d + 1) * NCH)
                    act.activation(R_UV[CH:P, 0, us], pt[CH:P, 0].rearrange("p (c n) -> p c n", n=P)[:, :, 0:CH], ACT.Copy)
                    ins = act.activation(R_UV[0:CH, 1, us], pt[0:CH, 1].rearrange("p (c n) -> p c n", n=P)[:, :, CH:P],
                                         ACT.Copy)
                ins.then_inc(uv_ready, 1)
                act.wait_ge(ss_clamped, t + 1)
                act.activation(R_sh[:, 1], R_sh[:, 1], ACT.Ln, scale=65536.0)
                act.drain()
                act.activation(R_sh[:, 1], R_sh[:, 1], ACT.Exp, scale=-0.5).then_inc(rn_ready, 1)
                act.wait_ge(logs_ready, t + 1)
                act.activation(R_e1[:], R_b[:], ACT.Exp)
                act.activation(R_e2[:], R_b[:], ACT.Exp, scale=-1.0)
                act.activation(R_lw[:, 0:2], R_lw[:, 0:2], ACT.Exp).then_inc(exps_ready, 1)
                act.wait_ge(ab_turned, t + 1)
                for d in range(2):
                    ins = act.activation(R_ABt[:, d * NCH:(d + 1) * NCH].rearrange("p u c -> p (u c)"), pt[:, d], ACT.Copy)
                ins.then_inc(abt_ready, 1)
                for lv in range(LEVELS):
                    act.wait_ge(qc_ready, t * LEVELS + lv + 1)
                    act.activation(R_Qbd[0:CH, :, 0:CH], R_qc[0:CH], ACT.Copy)
                    act.activation(R_Qbd[CH:P, :, CH:P], R_qc[CH:P], ACT.Copy).then_inc(qbd_ready, 1)
                    act.wait_ge(wc_ready, t * LEVELS + lv + 1)
                    act.activation(R_Wbd[0:CH, :, 0:CH], R_wc[0:CH], ACT.Copy)
                    act.activation(R_Wbd[CH:P, :, CH:P], R_wc[CH:P], ACT.Copy).then_inc(wbd_ready, 1)
                for i in range(NCH):
                    u = NCH + NCH - 1 - i
                    act.wait_ge(x_done[1], t * NCH + i + 1)
                    act.activation(R_X[:, 1], pb[:, 1, (u % NCH) * CH:(u % NCH + 1) * CH], ACT.Copy).then_inc(xs_ready[1], 1)
                    act.wait_ge(u_done[1], t * NCH + i + 1)
                    act.activation(R_UV[0:CH, 0, u], py[0:CH, 1, 0:CH], ACT.Copy, scale=-1.0)
                    act.activation(R_UV[CH:P, 1, u], py[CH:P, 1, 0:CH], ACT.Copy, scale=-1.0).then_inc(u_ready[1], 1)
                act.wait_ge(y_done[1], t + 1)
                act.activation(R_y[:].rearrange("p c n -> p (c n)"), pt[:, 1, 0:SEQ], ACT.Copy).then_inc(ys1_ready, 1)
                act.wait_ge(ys_var, t + 1)
                act.activation(small[:, 20:24], small[:, 16:20], ACT.Ln)
                act.drain()
                act.activation(small[:, 24:28], small[:, 20:24], ACT.Exp, scale=-0.5).then_inc(ys_rstd, 1)
                act.wait_ge(yn_ready, t + 1)
                act.activation(R_Qbd[0:CH, 0:NCH, 0:CH], R_y[0:CH], ACT.Copy)
                act.activation(R_Qbd[CH:P, 0:NCH, CH:P], R_y[CH:P], ACT.Copy).then_inc(ybd_ready, 1)
            for i in range(NT):
                act.activation(z[:, i, Z_OG:Z], z[:, i, Z_OG:Z], ACT.Silu).then_inc(og_ready, 1)
            act.wait_ge(pair_done, 1 + PAIRS)
            act.wait_ge(gg_turned, 1)
            act.activation(L_gg[0:GLORA], py[0:GLORA, 1, 0:SEQ], ACT.Copy).then_inc(gg_ready, 1)
            with act.Fori(0, GH) as t:
                act.wait_ge(g_turned, t + 1)
                act.activation(L_qk[:].rearrange("p j t -> p (j t)"), pt[:, 0], ACT.Copy).then_inc(g_qk, 1)
                act.wait_ge(g_x, t + 1)
                act.activation(L_t[:], L_t[:], ACT.Exp, scale=-1.0)
                act.drain()
                act.activation(L_t[:], L_t[:], ACT.Ln, bias=1.0).then_inc(g_soft, 1)
                act.wait_ge(g_logs, t + 1)
                act.activation(L_e1[:], L_b[:], ACT.Exp)
                act.activation(L_e2[:], L_b[:], ACT.Exp, scale=-1.0)
                for d in range(2):
                    for c in range(NCH):
                        end = c * CH + (CH - 1 if d == 0 else 0)
                        ins = act.activation(L_e3[:, d, c * CH:(c + 1) * CH], L_b[:, d, c * CH:(c + 1) * CH], ACT.Exp,
                                             scale=-1.0, bias=L_b[:, d, end:end + 1])
                ins.then_inc(g_exps, 1)
                act.wait_ge(g_kdt_done, t + 1)
                act.activation(L_kdt[:].rearrange("p d i n -> p (d i n)"), pt[:, 1], ACT.Copy).then_inc(g_kdt, 1)
                act.wait_ge(g_o, t + 1)
                for i in range(NT):
                    ins = act.activation(L_sq[:, i], pa[:, 1, i * DV:(i + 1) * DV], ACT.Square, accum_out=small[:, 28 + i:29 + i])
                act.drain().then_inc(g_sq, 1)
                act.wait_ge(g_var, t + 1)
                act.activation(small[:, 30:32], small[:, 28:30], ACT.Ln)
                act.drain()
                act.activation(small[:, 32:34], small[:, 30:32], ACT.Exp, scale=-0.5).then_inc(g_rstd, 1)
            act.wait_ge(head_done, 1 + GH)
            split_act(act, 0)
            act.wait_ge(split_lo, 8)
            act.dma_start(xt[:], x_in[0].rearrange("(i p) d -> p i d", p=P)).then_inc(x_in_sem, 16)
            out_act(act, 13, 13)
            end_load(act, 0, 16)
            end_act(act, 0)
            turn_act(act, 1)
            ffn_act(act, C_FFN0, 0, 17)
            end_load(act, 1, C_FFN0 + 32)
            end_act(act, 1)
            turn_act(act, 2)
            in_act(act, C_DIFF, qkv, True)
            act.wait_ge(unit_done, 2 + 4 * C_OUT1)
            act.dma_start(A_lam[0:1, 0:256], diff_lambda.rearrange("a b n -> a (b n)")).then_inc(lam_in, 16)
            act.wait_ge(lam_prod, 1)
            act.activation(A_lam[0:1, 258:260], A_lam[0:1, 256:258], ACT.Exp).then_inc(lam_exp, 1)
            with act.Fori(0, DH) as t:
                act.wait_ge(at_turned, t + 1)
                act.activation(A_qkT[:].rearrange("p j t -> p (j t)"), pt[:, 0], ACT.Copy).then_inc(at_T, 1)
                act.wait_ge(at_bias, t + 1)
                for c in range(2):
                    for i in range(NT):
                        m = 2 * c + i
                        act.activation(A_p[:, c, i], py[:, c, i * SEQ:(i + 1) * SEQ], ACT.Exp, scale=0.125,
                                       bias=small[:, 76 + m:77 + m], accum_out=small[:, 80 + m:81 + m])
                act.drain().then_inc(at_exp, 1)
                act.wait_ge(at_pturned, t + 1)
                act.activation(A_pT[:].rearrange("p k t -> p (k t)"), pt[:, 1], ACT.Copy).then_inc(at_pT, 1)
                act.wait_ge(at_o, t + 1)
                for i in range(NT):
                    act.activation(A_sq[:], pa[:, 0, i * P:(i + 1) * P], ACT.Square, accum_out=small[:, 28 + i:29 + i])
                    act.drain()
                act.drain().then_inc(at_sq, 1)
                act.wait_ge(at_var, t + 1)
                act.activation(small[:, 30:32], small[:, 28:30], ACT.Ln)
                act.drain()
                act.activation(small[:, 32:34], small[:, 30:32], ACT.Exp, scale=-0.5).then_inc(at_rstd, 1)
                act.wait_ge(at_scaled, t + 1)
                act.activation(hth[:, bass.ds(t, 1), :], A_t2[:], ACT.Copy).then_inc(at_hi, 1)
            act.wait_ge(at_done, 1 + DH)
            out_act(act, C_OUT1, 17 + FG + 12)
            end_load(act, 2, C_OUT1 + 3)
            end_act(act, 2)
            turn_act(act, 3)
            ffn_act(act, C_FFN1, FG, n_of[FG])
            end_load(act, 3, C_FFN1 + 32)
            end_act(act, 3)

        @block.vector
        def _(dve):
            dve.sem_inc(lo_done, 4)
            dve.sem_inc(ada_step, 1)
            dve.wait_ge(tab_copied, 1)
            dve.tensor_scalar(hmu[:], tab[:, T_MU:T_MU + 28], 0.5, None, ALU.mult)
            dve.tensor_scalar(omu[:], tab[:, T_MU:T_MU + 28], -1.0, 1.0, ALU.mult, ALU.add)
            dve.tensor_scalar(neg[:, 0:24], tab[:, T_W0:T_W0 + 24], -1.0, None, ALU.mult)
            dve.tensor_scalar(neg[:, 24:32], tab[:, T_KA:T_KA + 8], -1.0, 1.0, ALU.mult, ALU.add)
            dve.wait_ge(silu_ready, 1)
            for s in range(4):
                cond_unit(dve, 0, s)
            cond_sum(dve, 0, first=True)
            with dve.Fori(1, 8) as j:
                cond_unit(dve, j, 0)
                cond_unit(dve, j, 1)
                cond_store(dve, j - 1)
                cond_unit(dve, j, 2)
                cond_unit(dve, j, 3)
                cond_sum(dve, j)
            cond_store(dve, 7)
            dve.drain()
            turn_dve(dve, 0, 0)
            with dve.Fori(0, 12) as c:
                for s in range(4):
                    low(dve, c, s)
                    cond_unit(dve, c + 8, s)
                    if s == 2:
                        cond_store(dve, c + 7) if False else None
                cond_sum(dve, c + 8)
                cond_store(dve, c + 8)
            for s in range(4):
                low(dve, 12, s, LASTW)
            dve.wait_ge(lora_padded, 1)
            pad4 = R_G[:].rearrange("p a b c -> p (a b c)")[:, 0:4 * (SEQ + 2)].rearrange("p (j t) -> p j t", t=SEQ + 2)
            for lo, hi, n in ((0, 2, LORA), (2, 4, P)):
                dve.tensor_tensor(R_lora[0:n, lo:hi], pad4[0:n, lo:hi, 0:SEQ], pad4[0:n, lo:hi, 2:2 + SEQ], ALU.add)
            dve.drain()
            for j in range(4):
                n = LORA if j < 2 else P
                dve.tensor_scalar(R_lora[0:n, j], R_lora[0:n, j], hmu[0:n, 24 + j:25 + j], None, ALU.mult)
            dve.drain()
            for j in range(4):
                n = LORA if j < 2 else P
                ins = dve.scalar_tensor_tensor(R_lora[0:n, j], pad4[0:n, j, 1:1 + SEQ], omu[0:n, 24 + j:25 + j],
                                               R_lora[0:n, j], ALU.mult, ALU.add)
            ins.then_inc(lora_mixed, 1)
            dve.drain().then_inc(lora_ready, 1)
            dve.sem_inc(pair_done, 1)
            with dve.Fori(0, PAIRS) as t:
                dve.wait_ge(zf_ready, t + 1)
                dve.tensor_tensor(R_sh[:], R_zf[:, :, 0:SEQ], R_zf[:, :, 2:2 + SEQ], ALU.add)
                dve.drain()
                for j in range(3):
                    dve.tensor_scalar(R_sh[:, j], R_sh[:, j], hmu[:, bass.ds(t + 8 * j, 1)], None, ALU.mult)
                dve.drain()
                for j in range(3):
                    o = R_rk[:, j] if j < 2 else R_vp[:, CH:CH + SEQ]
                    ins = dve.scalar_tensor_tensor(o, R_zf[:, j, 1:1 + SEQ], omu[:, bass.ds(t + 8 * j, 1)], R_sh[:, j],
                                                   ALU.mult, ALU.add)
                dve.drain().then_inc(rkv_mixed, 1)
                dve.tensor_scalar(R_kk[:], R_rk[:, 1], tab[:, bass.ds(t + T_KK, 1)], None, ALU.mult)
                dve.drain()
                dve.tensor_tensor(R_sh[:, 0], R_kk[:], R_kk[:], ALU.mult).then_inc(sq_ready, 1)
                dve.wait_ge(up_act, t + 1)
                dve.tensor_scalar(R_lw[:], R_lw[:], 1.0, None, ALU.add)
                dve.drain()
                dve.reciprocal(R_lw[:], R_lw[:])
                dve.drain()
                dve.wait_ge(ss_done, t + 1)
                dve.tensor_scalar(R_sh[:, 1], pb[:, 0, 0:SEQ], 1e-24, None, ALU.max).then_inc(ss_clamped, 1)
                dve.tensor_scalar(R_lw[:, 0:2], R_lw[:, 0:2], -DECAY, None, ALU.mult)
                dve.drain()
                reset = cst[:, C_RESET:C_RESET + SEQ]
                dve.tensor_tensor_scan(R_b[:, 0], reset, R_lw[:, 0], 0.0, ALU.mult, ALU.add)
                dve.tensor_tensor_scan(R_b[:, 1][:, ::-1], reset, R_lw[:, 1][:, ::-1], 0.0, ALU.mult, ALU.add)
                dve.drain()
                dve.tensor_tensor(R_lw[:, 0:2], R_b[:], R_lw[:, 0:2], ALU.subtract).then_inc(logs_ready, 1)
                dve.tensor_scalar(R_sh[:, 2], R_lw[:, 2], tab[:, bass.ds(t + T_KA, 1)], neg[:, bass.ds(t + 24, 1)],
                                  ALU.mult, ALU.add)
                dve.drain()
                dve.tensor_tensor(R_rk[:, 1], R_rk[:, 1], R_sh[:, 2], ALU.mult)
                dve.wait_ge(rn_ready, t + 1)
                dve.scalar_tensor_tensor(R_kk[:], R_kk[:], 256.0, R_sh[:, 1], ALU.mult, ALU.mult)
                dve.drain()
                dve.tensor_tensor(R_sh[:, 0], R_kk[:], R_lw[:, 2], ALU.mult)
                dve.scalar_tensor_tensor(R_sh[:, 1], R_rk[:, 0], tab[:, bass.ds(t + T_RK, 1)], R_rk[:, 1],
                                         ALU.mult, ALU.mult).then_inc(q_ready, 1)
                dve.drain()
                dve.wait_ge(exps_ready, t + 1)

                def both(row):
                    return row.unsqueeze(1).to_broadcast((row.shape[0], 2, SEQ))

                def units(tile, rows_, at):
                    return tile[rows_, :, at:at + CH]
                full, top, low_half = slice(0, P), slice(0, CH), slice(CH, P)
                dve.tensor_tensor(units(R_KR, full, 0), both(R_kk[:]), R_lw[:, 0:2], ALU.mult)
                dve.tensor_tensor(units(R_KR, full, CH), both(R_rk[:, 0]), R_e1[:], ALU.mult).then_inc(kr_ready, 1)
                for rows_, at_a, at_b in ((top, 0, CH), (low_half, CH, 0)):
                    dve.tensor_tensor(units(R_AB, rows_, at_a), both(R_sh[rows_, 0]), R_e2[rows_], ALU.mult)
                    ins = dve.tensor_tensor(units(R_AB, rows_, at_b), both(R_rk[rows_, 1]), R_e2[rows_], ALU.mult)
                ins.then_inc(ab_ready, 1)
                dve.drain()
                dve.wait_ge(bonus_done, t + 1)
                dve.tensor_tensor(R_rk[:, 0], pb[:, 0, SEQ:W], R_vp[:, CH:CH + SEQ], ALU.mult)
                for d in range(2):
                    mask = cst[:, C_SCORE + d * P:C_SCORE + (d + 1) * P].unsqueeze(1).to_broadcast((P, NCH, P))
                    for h, bank in enumerate((py, pa)):
                        dve.wait_ge(scores_done, t * 4 + 2 * d + h + 1)
                        dve.tensor_tensor(R_G[:, h, d * NCH:(d + 1) * NCH],
                                          bank[:, d].rearrange("p (c n) -> p c n", n=P), mask, ALU.mult)
                dve.drain().then_inc(g_ready, 1)
                dve.tensor_copy(R_Lbd[0:CH, :, 0:CH], R_G[0:CH, 0, :, 0:CH])
                dve.tensor_copy(R_Lbd[CH:P, :, CH:P], R_G[CH:P, 1, :, 0:CH])
                dve.drain().then_inc(l_ready, 1)
                lv_mask = cst[:, C_LEVEL:C_LEVEL + 2 * LEVELS * CH].rearrange("p (d l n) -> p d l n", d=2, l=LEVELS)
                for lv in range(LEVELS):
                    dve.wait_ge(q_done, t * LEVELS + lv + 1)
                    for d in range(2):
                        ins = dve.tensor_tensor(R_qc[:, d * NCH:(d + 1) * NCH],
                                                py[:, 0, d * SEQ:(d + 1) * SEQ].rearrange("p (c n) -> p c n", n=CH),
                                                lv_mask[:, d, lv].unsqueeze(1).to_broadcast((P, NCH, CH)), ALU.mult)
                    ins.then_inc(qc_ready, 1)
                    if lv < LEVELS - 1:
                        dve.wait_ge(v_done, t * (LEVELS - 1) + lv + 1)
                        dve.tensor_tensor(R_vc[:].rearrange("p u n -> p (u n)"), R_vc[:].rearrange("p u n -> p (u n)"),
                                          py[:, 1], ALU.subtract)
                    dve.wait_ge(w_done, t * LEVELS + lv + 1)
                    dve.tensor_tensor(R_wc[:].rearrange("p u n -> p (u n)"), R_wc[:].rearrange("p u n -> p (u n)"),
                                      pa[:, 0], ALU.subtract).then_inc(wc_ready, 1)
                for i in range(NCH):
                    u = i
                    dve.wait_ge(x_done[0], t * NCH + i + 1)
                    dve.tensor_copy(R_X[:, 0], pb[:, 0, u * CH:(u + 1) * CH]).then_inc(xs_ready[0], 1)
                    dve.wait_ge(u_done[0], t * NCH + i + 1)
                    dve.tensor_scalar(R_UV[0:CH, 0, u], py[0:CH, 0, 0:CH], -1.0, None, ALU.mult)
                    dve.tensor_scalar(R_UV[CH:P, 1, u], py[CH:P, 0, 0:CH], -1.0, None, ALU.mult).then_inc(u_ready[0], 1)
                    if i == NCH - 1:
                        break
                    for d in range(2):
                        c = i if d == 0 else NCH - 1 - i
                        end = c * CH + CH - 1 if d == 0 else c * CH
                        dve.wait_ge(s_done[d], t * (NCH - 1) + i + 1)
                        decay = R_e1[:, d, end:end + 1]
                        if i:
                            dve.tensor_tensor(R_S[:, d], R_S[:, d], pa[:, d, 0:CH], ALU.add)
                            dve.drain()
                            dve.tensor_scalar(R_S[:, d], R_S[:, d], decay, None, ALU.mult).then_inc(s_ready[d], 1)
                        else:
                            dve.tensor_scalar(R_S[:, d], pa[:, d, 0:CH], decay, None, ALU.mult).then_inc(s_ready[d], 1)
                dve.wait_ge(y_done[0], t + 1)
                dve.wait_ge(ys1_ready, t + 1)
                dve.tensor_tensor(R_y[:].rearrange("p c n -> p (c n)"), R_y[:].rearrange("p c n -> p (c n)"),
                                  pt[:, 0, 0:SEQ], ALU.add)
                dve.drain()
                for c in range(NCH):
                    dve.bn_stats(R_st[:, c], R_y[:, c])
                dve.drain()
                for c in range(NCH):
                    dve.bn_aggr(R_mv[:, c], R_st[:, c])
                dve.drain()
                dve.tensor_scalar(small[:, 16:20], R_mv[:, :, 1], GN_EPS, None, ALU.add).then_inc(ys_var, 1)
                dve.wait_ge(ys_rstd, t + 1)
                for c in range(NCH):
                    dve.tensor_scalar(R_y[:, c], R_y[:, c], R_mv[:, c, 0:1], small[:, 24 + c:25 + c],
                                      ALU.subtract, ALU.mult)
                dve.drain().then_inc(yn_ready, 1)
                dve.wait_ge(yt_done, t + 1)
                dve.tensor_scalar(R_sh[:, 0], py[:, 0, 0:SEQ], tab[:, bass.ds(t + T_GNG, 1)], tab[:, bass.ds(t + T_GNB, 1)],
                                  ALU.mult, ALU.add)
                dve.drain()
                dve.tensor_tensor(R_sh[:, 0], R_sh[:, 0], R_rk[:, 0], ALU.add)
                dve.drain()
                dve.tensor_tensor(xf[:, bass.ds(t, 1), :], R_sh[:, 0:1], R_g[:].unsqueeze(1), ALU.mult).then_inc(pair_done, 1)
            dve.sem_inc(head_done, 1)
            dve.wait_ge(og_ready, 2)
            with dve.Fori(0, GH) as t:
                dve.wait_ge(g_gate, t + 1)
                for d in range(2):
                    dve.tensor_scalar(L_x[:, d], pa[:, 0, d * SEQ:(d + 1) * SEQ], tab[:, bass.ds(t + T_GB + d * GH, 1)], None, ALU.add)
                dve.drain()
                xx, tt = (v[:].rearrange("p d t -> p (d t)") for v in (L_x, L_t))
                dve.scalar_tensor_tensor(tt, xx, -1.0, xx, ALU.mult, ALU.max).then_inc(g_x, 1)
                dve.drain()
                dve.tensor_scalar(xx, xx, 0.0, 1.0 / 16, ALU.min, ALU.mult)
                dve.drain()
                dve.wait_ge(g_soft, t + 1)
                dve.scalar_tensor_tensor(xx, tt, -1.0 / 16, xx, ALU.mult, ALU.add)
                dve.drain()
                reset = cst[:, C_RESET:C_RESET + SEQ]
                dve.tensor_tensor_scan(L_b[:, 0], reset, L_x[:, 0], 0.0, ALU.mult, ALU.add)
                dve.tensor_tensor_scan(L_b[:, 1][:, ::-1], reset, L_x[:, 1][:, ::-1], 0.0, ALU.mult, ALU.add).then_inc(g_logs, 1)
                dve.wait_ge(g_qk, t + 1)
                dve.wait_ge(g_exps, t + 1)
                for d in range(2):
                    dve.scalar_tensor_tensor(L_qb[:, d], L_qk[:, 0], float(DK) ** -0.5, L_e1[:, d], ALU.mult, ALU.mult)
                kk2 = L_qk[:, 1:2].to_broadcast((P, 2, SEQ))
                dve.tensor_tensor(L_kb[:], kk2, L_e2[:], ALU.mult)
                dve.tensor_tensor(L_kd[:], kk2, L_e3[:], ALU.mult).then_inc(g_prod, 1)
                dve.wait_ge(g_att, t + 1)
                for d in range(2):
                    ins = dve.scalar_tensor_tensor(
                        L_att[:, d], pb[:, 0, d * SEQ:(d + 1) * SEQ].rearrange("p (i n) -> p i n", n=P), 3e38,
                        cst[:, C_GLA + d * P:C_GLA + (d + 1) * P].unsqueeze(1).to_broadcast((P, NT, P)), ALU.min, ALU.mult)
                ins.then_inc(g_attm, 1)
                dve.wait_ge(g_kv, t + 1)
                place = {(0, 0): py[:, 0, 0:DV], (0, 1): py[:, 1, 0:DV], (0, 2): py[:, 0, DV:2 * DV],
                         (1, 3): py[:, 1, DV:2 * DV], (1, 2): pa[:, 0, 0:DV], (1, 1): pb[:, 1, 0:DV]}
                for i in range(NCH - 1):
                    for d in range(2):
                        c = i if d == 0 else NCH - 1 - i
                        end = c * CH + (CH - 1 if d == 0 else 0)
                        if i == 0:
                            ins = dve.tensor_copy(L_S[:, d, 0], place[d, c])
                        else:
                            ins = dve.scalar_tensor_tensor(L_S[:, d, i], L_S[:, d, i - 1], L_e1[:, d, end:end + 1],
                                                           place[d, c], ALU.mult, ALU.add)
                    dve.drain()
                dve.drain().then_inc(g_states, 1)
                dve.wait_ge(g_sq, t + 1)
                dve.tensor_scalar(small[:, 28:30], small[:, 28:30], 1.0 / DV, EPS, ALU.mult, ALU.add).then_inc(g_var, 1)
                dve.wait_ge(g_rstd, t + 1)
                for i in range(NT):
                    ins = dve.scalar_tensor_tensor(L_o[:, i], pa[:, 1, i * DV:(i + 1) * DV], small[:, 32 + i:33 + i],
                                                   z[:, i, bass.ds(t * DV + Z_OG, DV)], ALU.mult, ALU.mult)
                ins.then_inc(g_on, 1)
                dve.wait_ge(g_oT, t + 1)
                for j in range(2):
                    dve.tensor_scalar(xf[:, bass.ds(t * 2 + 8 + j, 1), :], pt[:, 0:1, j * SEQ:(j + 1) * SEQ],
                                      tab[:, T_NG + j:T_NG + j + 1], None, ALU.mult)
                dve.drain().then_inc(head_done, 1)
            split_dve(dve, 0)
            out_dve(dve, 13, 20)
            dve.wait_ge(pa_free, 2 + 2 * 17)
            dve.wait_ge(x_in_sem, 32)
            end_dve(dve, 0)
            turn_dve(dve, 1, 1)
            ffn_dve(dve, C_FFN0, 0, 0, 24)
            end_dve(dve, 1)
            turn_dve(dve, 2, 2)
            with dve.Fori(0, 12) as t:
                for s in range(4):
                    low(dve, t + C_DIFF, s)
                    cond_unit(dve, t + 36, s)
                cond_sum(dve, t + 36)
                cond_store(dve, t + 36)
            dve.wait_ge(lam_in, 16)
            lam4 = A_lam[0:1, 0:256].rearrange("p (a b n) -> p a b n", a=2, b=2)
            dve.tensor_tensor(lam4[:, :, 0], lam4[:, :, 0], lam4[:, :, 1], ALU.mult)
            dve.drain()
            dve.tensor_reduce(A_lam[0:1, 256:258], lam4[:, :, 0], AX_X, ALU.add).then_inc(lam_prod, 1)
            dve.wait_ge(lam_exp, 1)
            dve.tensor_tensor(A_lam[0:1, 260:261], A_lam[0:1, 259:260], A_lam[0:1, 258:259], ALU.subtract)
            dve.drain()
            dve.tensor_scalar(A_lam[0:1, 261:262], A_lam[0:1, 260:261], LAMBDA_INIT, None, ALU.subtract)
            dve.drain().then_inc(lam_prod, 1)
            dve.wait_ge(lam_mm, 1)
            dve.tensor_copy(small[:, 74:75], pb[:, 1, 0:1])
            dve.tensor_scalar(small[:, 75:76], tab[:, T_SUB:T_SUB + 1], 1.0 - LAMBDA_INIT, None, ALU.mult)
            dve.drain()
            dve.wait_ge(pa_free, 2 + 2 * (17 + FG + 12))
            dve.sem_inc(at_done, 1)
            with dve.Fori(0, DH) as t:
                rotate(dve, t, 0)
                dve.drain().then_inc(at_rot0, 1)
                dve.wait_ge(at_scores, t + 1)
                for c in range(2):
                    dve.tensor_reduce(small[:, 84 + 2 * c:86 + 2 * c], py[:, c].rearrange("p (i k) -> p i k", k=SEQ), AX_X, ALU.max)
                dve.drain()
                dve.tensor_scalar(small[:, 76:80], small[:, 84:88], -0.125, None, ALU.mult).then_inc(at_bias, 1)
                dve.wait_ge(at_exp, t + 1)
                dve.reciprocal(small[:, 80:84], small[:, 80:84])
                dve.drain()
                dve.tensor_scalar(small[:, 82:84], small[:, 82:84], small[:, 74:75], None, ALU.mult)
                for i in range(NT):
                    dve.tensor_scalar(A_p[:, 0, i], A_p[:, 0, i], small[:, 80 + i:81 + i], None, ALU.mult)
                dve.drain()
                for i in range(NT):
                    ins = dve.scalar_tensor_tensor(A_p[:, 0, i], A_p[:, 1, i], small[:, 82 + i:83 + i], A_p[:, 0, i],
                                                   ALU.mult, ALU.add)
                ins.then_inc(at_p, 1)
                dve.wait_ge(at_sq, t + 1)
                dve.tensor_scalar(small[:, 28:30], small[:, 28:30], 1.0 / P, EPS, ALU.mult, ALU.add).then_inc(at_var, 1)
                dve.wait_ge(at_rstd, t + 1)
                for i in range(NT):
                    ins = dve.tensor_scalar(A_o[:, i], pa[:, 0, i * P:(i + 1) * P], small[:, 32 + i:33 + i], None, ALU.mult)
                ins.then_inc(at_on, 1)
                dve.wait_ge(at_oT, t + 1)
                dve.tensor_scalar(A_t2[:, 0], pb[:, 0, 0:SEQ], small[:, 75:76], None, ALU.mult).then_inc(at_scaled, 1)
                dve.wait_ge(at_hi, t + 1)
                dve.tensor_tensor(htl[:, bass.ds(t, 1), :], A_t2[:], hth[:, bass.ds(t, 1), :].bitcast(F32),
                                  ALU.subtract).then_inc(at_done, 1)
            out_dve(dve, C_OUT1)
            dve.wait_ge(pa_free, 2 + 2 * (17 + FG + 16))
            end_dve(dve, 2)
            turn_dve(dve, 3, 3)
            ffn_dve(dve, C_FFN1, FG, 44)
            end_dve(dve, 3)

        @block.tensor
        def _(pe):
            pe.sem_inc(unit_done, 2)
            pe.sem_inc(pa_free, 2)
            pe.wait_ge(const_in, 16)
            pe.wait_ge(rows_in, 16 * len(list(vectors())))
            for i in range(4):
                n = TABS[i + 1] - TABS[i]
                mm = pe.transpose(pa[:, 0, TABS[i]:TABS[i + 1]], rows[0:n, i, :], ident[0:n, 0:n])
            mm.then_inc(tab_turned, 1)
            cond_cols(pe, 0, first=True)
            with pe.Fori(1, 8) as j:
                cond_cols(pe, j)
            pe.wait_ge(x_in_sem, 16)
            turn_pe(pe, 0)
            pe.wait_ge(h_lo, 8)
            with pe.Fori(0, 12) as c:
                project(pe, c, c, (hth, htl), pa_done, pa_free, pa)
                cond_cols(pe, c + 8)
            project(pe, 12, 12, (hth, htl), pa_done, pa_free, pa, LASTW)
            pe.wait_ge(pa_free, 2 + 2 * ABC)
            for j, (a, b) in enumerate(((Z_WD, Z_AD), (Z_AD, Z_GD), (Z_GD, Z_GD + P), (Z_GD + P, Z_Q))):
                for i in range(NT):
                    at = (j % 2) * SEQ + i * P
                    mm = pe.transpose(py[0:b - a, j // 2, at:at + P], z[:, i, a:b], ident)
            mm.then_inc(lora_turned, 1)
            pe.wait_ge(lora_ready, 3)
            with pe.Fori(0, PAIRS) as t:
                pe.wait_ge(zs_ready, t + 1)
                for j in range(3):
                    for i in range(NT):
                        at = (j % 2) * SEQ + i * P
                        mm = pe.transpose(pt[:, j // 2, at:at + P], R_zs[:, i, j], ident)
                mm.then_inc(rk_turned, 1)
                pe.wait_ge(up_in, t * 48 + 48)
                for j in range(3):
                    lora = R_lora[0:LORA, 0 if j < 2 else 1]
                    pe.matmul(pa[:, j // 2, (j % 2) * SEQ:(j % 2 + 1) * SEQ], R_up[0:LORA, j], lora, start=True, stop=True)
                for j in range(2):
                    mm = pe.matmul(pa[:, 1, SEQ:W], R_up[:, 3 + j], R_lora[:, 2 + j], start=(j == 0), stop=(j == 1))
                mm.then_inc(up_done, 1)
                pe.wait_ge(rkv_mixed, t + 1)
                for h in range(2):
                    for c in range(NCH):
                        mm = pe.transpose(pt[:, h, c * P:(c + 1) * P], R_vp[:, (c + h) * CH:(c + h) * CH + P], ident)
                mm.then_inc(v_turned, 1)
                pe.wait_ge(sq_ready, t + 1)
                pe.matmul(pb[:, 0, 0:SEQ], heads1, R_sh[:, 0], start=True, stop=True).then_inc(ss_done, 1)
                pe.wait_ge(q_ready, t + 1)
                pe.matmul(pb[:, 0, SEQ:W], heads1, R_sh[:, 1], start=True, stop=True).then_inc(bonus_done, 1)
                pe.wait_ge(ab_ready, t + 1)
                for d in range(2):
                    for h, bank in enumerate((py, pa)):
                        half = slice(h * CH, (h + 1) * CH)
                        for c in range(NCH):
                            u = d * NCH + c
                            mm = pe.matmul(bank[:, d, c * P:(c + 1) * P], R_AB[half, u], R_KR[half, u], start=True, stop=True)
                        mm.then_inc(scores_done, 1)
                pe.wait_ge(uv_ready, t + 1)
                for u in range(NU):
                    mm = pe.transpose(pt[:, u // NCH, (u % NCH) * P:(u % NCH + 1) * P], R_AB[:, u], ident)
                mm.then_inc(ab_turned, 1)
                pe.wait_ge(g_ready, t + 1)
                for d in range(2):
                    for c in range(NCH):
                        u = d * NCH + c
                        for h in range(2):
                            mm = pe.matmul(pb[h * CH:(h + 1) * CH, d, c * CH:(c + 1) * CH], R_G[:, h, u, 0:CH],
                                           R_UV[:, h, u], start=(c == 0), stop=True, skip_group_check=True)
                    mm.then_inc(x_done[d], 1)
                pe.wait_ge(l_ready, t + 1)
                pe.wait_ge(init_ready, t + 1)
                for lv in range(LEVELS):
                    if lv:
                        pe.wait_ge(wc_ready, t * LEVELS + lv)
                    for u in range(NU):
                        mm = pe.matmul(py[:, 0, u * CH:(u + 1) * CH], R_Lbd[:, u], R_vc[:, u], start=True, stop=True)
                    mm.then_inc(q_done, 1)
                    if lv:
                        pe.wait_ge(wbd_ready, t * LEVELS + lv)
                    if lv < LEVELS - 1:
                        pe.wait_ge(qc_ready, t * LEVELS + lv + 1)
                        for u in range(NU):
                            mm = pe.matmul(py[:, 1, u * CH:(u + 1) * CH], R_Wbd[:, u], R_qc[:, u], start=True, stop=True)
                        mm.then_inc(v_done, 1)
                    pe.wait_ge(qbd_ready, t * LEVELS + lv + 1)
                    for u in range(NU):
                        mm = pe.matmul(pa[:, 0, u * CH:(u + 1) * CH], R_Qbd[:, u], R_wc[:, u], start=True, stop=True)
                    mm.then_inc(w_done, 1)
                pe.wait_ge(wbd_ready, t * LEVELS + LEVELS)
                pe.wait_ge(krbd_ready, t + 1)
                pe.wait_ge(abt_ready, t + 1)
                for i in range(NCH):
                    for d in range(2):
                        c = i if d == 0 else NCH - 1 - i
                        u = d * NCH + c
                        if i:
                            pe.wait_ge(s_ready[d], t * (NCH - 1) + i)
                            pe.matmul(pb[:, d, c * CH:(c + 1) * CH], R_Kbd[:, u], R_S[:, d], start=False, stop=True,
                                      skip_group_check=True).then_inc(x_done[d], 1)
                    for d in range(2):
                        c = i if d == 0 else NCH - 1 - i
                        u = d * NCH + c
                        pe.wait_ge(xs_ready[d], t * NCH + i + 1)
                        pe.matmul(py[:, d, 0:CH], R_Wbd[:, u], R_X[:, d], start=True, stop=True).then_inc(u_done[d], 1)
                    for d in range(2):
                        c = i if d == 0 else NCH - 1 - i
                        u = d * NCH + c
                        pe.wait_ge(u_ready[d], t * NCH + i + 1)
                        if i < NCH - 1:
                            for h in range(2):
                                mm = pe.matmul(pa[h * CH:(h + 1) * CH, d, 0:CH], R_ABt[:, u, h * CH:(h + 1) * CH],
                                               R_UV[:, h, u], start=True, stop=True)
                        at = slice(c * CH, (c + 1) * CH)
                        for h in range(2):
                            mm = pe.matmul(pt[h * CH:(h + 1) * CH, d, at], R_G[:, h, u, CH:P], R_UV[:, h, u],
                                           start=(i == 0), stop=True, skip_group_check=True)
                        if i:
                            mm = pe.matmul(pt[:, d, at], R_Rbd[:, u], R_S[:, d], start=False, stop=True,
                                           skip_group_check=True)
                        mm.then_inc(y_done[d] if i == NCH - 1 else s_done[d], 1)
                pe.wait_ge(ybd_ready, t + 1)
                for c in range(NCH):
                    mm = pe.matmul(py[:, 0, c * CH:(c + 1) * CH], R_Qbd[:, c], cst[:, C_I2:C_I2 + CH], start=True, stop=True)
                mm.then_inc(yt_done, 1)
            pe.wait_ge(pair_done, 1 + PAIRS)
            for i in range(NT):
                mm = pe.transpose(py[0:GLORA, 1, i * P:(i + 1) * P], z[:, i, Z_GG:Z_OG], ident)
            mm.then_inc(gg_turned, 1)
            pe.wait_ge(gg_ready, 1)
            with pe.Fori(0, GH) as t:
                pe.wait_ge(head_done, t + 1)
                pe.wait_ge(gz_ready, t + 1)
                for j in range(2):
                    for i in range(NT):
                        mm = pe.transpose(pt[:, 0, j * SEQ + i * P:j * SEQ + (i + 1) * P], L_zs[:, i, j], ident)
                mm.then_inc(g_turned, 1)
                pe.wait_ge(gla_in, t * 16 + 16)
                for d in range(2):
                    mm = pe.matmul(pa[:, 0, d * SEQ:(d + 1) * SEQ], L_up[0:GLORA, d], L_gg[0:GLORA], start=True, stop=True)
                mm.then_inc(g_gate, 1)
                pe.wait_ge(g_prod, t + 1)
                for d in range(2):
                    for i in range(NT):
                        ts_ = slice(i * P, (i + 1) * P)
                        mm = pe.matmul(pb[:, 0, (d * NT + i) * P:(d * NT + i + 1) * P], L_kb[:, d, ts_], L_qb[:, d, ts_],
                                       start=True, stop=True)
                mm.then_inc(g_att, 1)
                for d in range(2):
                    for i in range(NT):
                        mm = pe.transpose(pt[:, 1, (d * NT + i) * P:(d * NT + i + 1) * P], L_kd[:, d, i * P:(i + 1) * P], ident)
                mm.then_inc(g_kdt_done, 1)
                pe.wait_ge(g_kdt, t + 1)
                place = {(0, 0): py[:, 0, 0:DV], (0, 1): py[:, 1, 0:DV], (0, 2): py[:, 0, DV:2 * DV],
                         (1, 3): py[:, 1, DV:2 * DV], (1, 2): pa[:, 0, 0:DV], (1, 1): pb[:, 1, 0:DV]}
                for (d, c), bank in place.items():
                    r = slice(c % 2 * CH, c % 2 * CH + CH)
                    mm = pe.matmul(bank, L_kdt[r, d, c // 2], L_v[r, c // 2], start=True, stop=True)
                mm.then_inc(g_kv, 1)
                pe.wait_ge(g_attm, t + 1)
                for i in range(NT):
                    for d in range(2):
                        pe.matmul(pa[:, 1, i * DV:(i + 1) * DV], L_att[:, d, i], L_v[:, i], start=(i == 0 and d == 0),
                                  stop=True, skip_group_check=True)
                pe.wait_ge(g_states, t + 1)
                for d in range(2):
                    for i in range(1, NCH):
                        c = i if d == 0 else NCH - 1 - i
                        mm = pe.matmul(pa[c % 2 * CH:c % 2 * CH + CH, 1, c // 2 * DV:c // 2 * DV + DV],
                                       L_qb[:, d, c * CH:(c + 1) * CH], L_S[:, d, i - 1], start=False, stop=True,
                                       skip_group_check=True)
                mm.then_inc(g_o, 1)
                pe.wait_ge(g_on, t + 1)
                for j in range(2):
                    for i in range(NT):
                        mm = pe.transpose(pt[:, 0, j * SEQ + i * P:j * SEQ + (i + 1) * P], L_o[:, i, j * P:(j + 1) * P], ident)
                mm.then_inc(g_oT, 1)
            pe.wait_ge(split_lo, 8)
            out_pe(pe, 13, 13, 20)
            end_pe(pe, 0)
            pe.sem_inc(pb_free, 2)
            pe.sem_inc(py_free, 2)
            turn_pe_at(pe, 1)
            ffn_pe(pe, C_FFN0, 0, 0, 24)
            end_pe(pe, 1)
            turn_pe_at(pe, 2)
            with pe.Fori(0, 12) as t:
                project(pe, t + C_DIFF, t + (17 + FG), (hth, htl), pa_done, pa_free, pa)
                cond_cols(pe, t + 36)
            pe.wait_ge(lam_prod, 2)
            pe.matmul(pb[:, 1, 0:1], ones[0:1, :], A_lam[0:1, 261:262], start=True, stop=True).then_inc(lam_mm, 1)
            with pe.Fori(0, DH) as t:
                pe.wait_ge(at_rot0, t + 1)
                pe.wait_ge(at_rot1, t + 1)
                for j in range(2):
                    for i in range(NT):
                        mm = pe.transpose(pt[:, 0, j * SEQ + i * P:j * SEQ + (i + 1) * P],
                                          A_qk[:, i, j].rearrange("p c f -> p (c f)"), ident)
                mm.then_inc(at_turned, 1)
                pe.wait_ge(at_T, t + 1)
                for c in range(2):
                    r = slice(c * 64, c * 64 + 64)
                    for i in range(NT):
                        mm = pe.matmul(py[:, c, i * SEQ:(i + 1) * SEQ], A_qkT[r, 0, i * P:(i + 1) * P], A_qkT[r, 1],
                                       start=True, stop=True)
                mm.then_inc(at_scores, 1)
                pe.wait_ge(at_p, t + 1)
                for k in range(NT):
                    for i in range(NT):
                        mm = pe.transpose(pt[:, 1, k * SEQ + i * P:k * SEQ + (i + 1) * P], A_p[:, 0, i, k * P:(k + 1) * P], ident)
                mm.then_inc(at_pturned, 1)
                pe.wait_ge(at_pT, t + 1)
                for i in range(NT):
                    for k in range(NT):
                        mm = pe.matmul(pa[:, 0, i * P:(i + 1) * P], A_pT[:, k, i * P:(i + 1) * P],
                                       qkv[:, k, bass.ds(t * P + 2 * D, P)], start=(k == 0), stop=(k == NT - 1))
                mm.then_inc(at_o, 1)
                pe.wait_ge(at_on, t + 1)
                for i in range(NT):
                    mm = pe.transpose(pb[:, 0, i * P:(i + 1) * P], A_o[:, i], ident)
                mm.then_inc(at_oT, 1)
            pe.wait_ge(at_done, 1 + DH)
            out_pe(pe, C_OUT1, 17 + FG + 12)
            end_pe(pe, 2)
            turn_pe_at(pe, 3)
            ffn_pe(pe, C_FFN1, FG, 44)
            end_pe(pe, 3)


INPUTS = ["x", "c", "ada_w", "ada_b", "ln_g", "ln_b", "ffn_w_in", "ffn_w_out", "ab_w_in", "ab_w_out",
          "rwkv_mu", "rwkv_w0", "rwkv_w_up", "rwkv_a0", "rwkv_a_up", "rwkv_g_up", "rwkv_k_k", "rwkv_k_a",
          "rwkv_r_k", "rwkv_gn_g", "rwkv_gn_b", "gla_gate_up", "gla_gate_b", "gla_norm_g",
          "diff_w_in", "diff_w_out", "diff_lambda", "diff_subln_g"]


def kernel(**inputs):
    import concourse.bacc as bacc
    from concourse.bass_utils import run_bass_kernel_spmd

    nc = bacc.Bacc("TRN2", target_bir_lowering=False, num_devices=1)
    arrays, args = {}, []
    for name in INPUTS:
        a = np.ascontiguousarray(inputs[name])
        arrays[f"in_{name}"] = a
        args.append(nc.dram_tensor(f"in_{name}", a.shape, mybir.dt.from_np(a.dtype), kind="ExternalInput").ap())
    arrays["in_constants"] = constants()
    args.append(nc.dram_tensor("in_constants", (P, C_N), F32, kind="ExternalInput").ap())
    out = nc.dram_tensor("out_0", (1, SEQ, D), F32, kind="ExternalOutput").ap()
    build_trunk(nc, *args, out)
    r = run_bass_kernel_spmd(nc, [arrays], core_ids=[0])
    return r.results[0]["out_0"]
```

```python
from contextlib import ExitStack

import numpy as np

import concourse.bass as bass
from concourse import mybir

ALU = mybir.AluOpType
ACT = mybir.ActivationFunctionType
F32 = mybir.dt.float32
F32R = mybir.dt.float32r
AX_X = mybir.AxisListType.X

P = 128
D = 2048
SEQ = 256
NT = SEQ // P
KT = D // P
W = 512
UK = 4
D_FF = 5632
FG = D_FF // W
HN = 64
RW = D // 2
PAIRS = RW // P
LORA = 96
GATE = 256
Z_WD = 3 * RW
Z_AD = Z_WD + LORA
Z_GD = Z_AD + LORA
Z_Q = Z_GD + GATE
GH = 4
DK = 128
DV = 256
Z_K = Z_Q + GH * DK
Z_V = Z_K + GH * DK
Z_GG = Z_V + GH * DV
GLORA = 16
Z_OG = Z_GG + GLORA
Z = Z_OG + GH * DV
ABC = -(-Z // W)
CH = 64
NCH = SEQ // CH
NU = 2 * NCH
LEVELS = 6
DH = 16
ALPHA = (2.0 * 2) ** 0.25
DECAY = 0.606531
LAMBDA_INIT = 0.8 - 0.6 * float(np.exp(-0.3))
EPS = 1e-5
GN_EPS = 64e-5

T_LN_G, T_LN_B = 0, 64
T_MU, T_W0, T_A0, T_KK, T_KA, T_RK, T_GNG, T_GNB = 128, 156, 172, 180, 188, 196, 204, 212
T_GB, T_NG, T_SUB, T_C = 220, 228, 230, 231
T_ADA = 247
T_N = T_ADA + 192
TABS = (0, 128, 247, 343, 439)

C_ID, C_ONES, C_HEADS, C_SCORE, C_GLA, C_LEVEL, C_RESET, C_COS, C_SIN = (
    0, 128, 256, 384, 640, 896, 896 + 2 * LEVELS * CH, 896 + 2 * LEVELS * CH + SEQ, 896 + 2 * LEVELS * CH + SEQ + 64)
C_I2 = C_SIN + 64
C_N = C_I2 + CH


def constants():
    c = np.zeros((P, C_N), np.float32)
    p = np.arange(P)
    c[:, C_ID:C_ID + P] = np.eye(P)
    c[:, C_ONES:C_ONES + P] = 1.0
    c[:, C_HEADS:C_HEADS + P] = (p[:, None] // HN == p[None, :] // HN)
    s, t = (p % CH)[:, None], np.arange(CH)[None, :]
    c[:, C_SCORE:C_SCORE + P] = np.concatenate([s < t, s <= t], 1)
    c[:, C_SCORE + P:C_SCORE + 2 * P] = np.concatenate([s > t, s >= t], 1)
    same = p[:, None] // CH == p[None, :] // CH
    c[:, C_GLA:C_GLA + P] = same & (p[:, None] <= p[None, :])
    c[:, C_GLA + P:C_GLA + 2 * P] = same & (p[:, None] >= p[None, :])
    for d in range(2):
        for lv in range(LEVELS):
            b = 1 << lv
            row, col = (p % CH)[:, None], np.arange(CH)[None, :]
            if d:
                row, col = CH - 1 - row, CH - 1 - col
            m = (row // (2 * b) == col // (2 * b)) & (row // b % 2 == 0) & (col // b % 2 == 1)
            at = C_LEVEL + (d * LEVELS + lv) * CH
            c[:, at:at + CH] = -1.0 * m
    c[:, C_RESET:C_RESET + SEQ] = (np.arange(SEQ) % CH != 0)
    inv = (10000.0 ** (-np.arange(0, 64, 2, dtype=np.float32) / 64)).astype(np.float32)
    for i in range(NT):
        ang = ((i * P + p).astype(np.float32)[:, None] * inv[None, :]).astype(np.float32)
        c[:, C_COS + 32 * i:C_COS + 32 * i + 32] = np.cos(ang)
        c[:, C_SIN + 32 * i:C_SIN + 32 * i + 32] = np.sin(ang)
    c[:, C_I2:C_I2 + CH] = np.eye(CH)[np.arange(P) % CH]
    return c


def build_trunk(nc, x_in, c_in, ada_w, ada_b, ln_g, ln_b, ffn_w_in, ffn_w_out, ab_w_in, ab_w_out,
                rwkv_mu, rwkv_w0, rwkv_w_up, rwkv_a0, rwkv_a_up, rwkv_g_up, rwkv_k_k, rwkv_k_a,
                rwkv_r_k, rwkv_gn_g, rwkv_gn_b, gla_gate_up, gla_gate_b, gla_norm_g,
                diff_w_in, diff_w_out, diff_lambda, diff_subln_g, consts, out):
    with ExitStack() as ctx:
        def sb(name, shape, dt=F32, stack=ctx):
            return stack.enter_context(nc.sbuf_tensor("s_" + name, shape, dt))

        def sem(name):
            return ctx.enter_context(nc.semaphore(name))

        cst = sb("cst", [P, C_N])
        tab = sb("tab", [P, T_N])
        ada = sb("ada", [P, 4, 48])
        silu_c = sb("silu_c", [P, KT])
        hmu = sb("hmu", [P, 28])
        omu = sb("omu", [P, 28])
        neg = sb("neg", [P, 32])
        small = sb("small", [P, 96])
        raw = sb("raw", [P, 4, UK, W])
        adaw = sb("adaw", [P, 2, UK, W])
        acc = sb("acc", [P, 2, W])
        asum = sb("asum", [P, W])
        xt = sb("xt", [P, NT, D])
        xf = xt[:].rearrange("p a d -> p (a d)").rearrange("p (k t) -> p k t", t=SEQ)

        r1 = ExitStack()
        z = sb("z", [P, NT, Z], stack=r1)
        r1.close()
        r1 = ExitStack()
        qkv = sb("qkv", [P, NT, 3 * D], stack=r1)
        r1.close()
        r1 = ExitStack()
        ysum = sb("ysum", [P, NT, D], stack=r1)
        gu = sb("gu", [P, NT, W], stack=r1)
        guh = sb("guh", [P, UK, SEQ], F32R, stack=r1)
        gul = sb("gul", [P, UK, SEQ], F32R, stack=r1)
        r1.close()
        hold = sb("hold", [P, NT, Z])

        r2 = ExitStack()
        wh = sb("wh", [P, 2, UK, W], F32R, stack=r2)
        wl = sb("wl", [P, 2, UK, W], F32R, stack=r2)
        hth = sb("hth", [P, KT, SEQ], F32R, stack=r2)
        htl = sb("htl", [P, KT, SEQ], F32R, stack=r2)
        htmp = sb("htmp", [P, 2, 2, SEQ], stack=r2)
        r2.close()
        r2 = ExitStack()
        rows = sb("rows", [P, 4, P], stack=r2)
        r2.close()
        r2 = ExitStack()
        sb("skip", [P, 2, 2, UK, W], stack=r2)
        lng = sb("lng", [P, D], stack=r2)
        lnb = sb("lnb", [P, D], stack=r2)
        gate_bc = sb("gate_bc", [P, D], stack=r2)
        diag = sb("diag", [P, 4, P], stack=r2)
        r2.close()
        r2 = ExitStack()
        R_zs = sb("R_zs", [P, NT, 3, P], stack=r2)
        R_zf = sb("R_zf", [P, 3, SEQ + 2], stack=r2)
        R_sh = sb("R_sh", [P, 3, SEQ], stack=r2)
        R_bonus = sb("R_bonus", [P, SEQ], stack=r2)
        R_gn = sb("R_gn", [P, SEQ], stack=r2)
        R_dec = sb("R_dec", [P, 2, NCH], stack=r2)
        R_qc = sb("R_qc", [P, NU, CH], stack=r2)
        R_vc = sb("R_vc", [P, NU, CH], stack=r2)
        R_wc = sb("R_wc", [P, NU, CH], stack=r2)
        R_rk = sb("R_rk", [P, 2, SEQ], stack=r2)
        R_vp = sb("R_vp", [P, CH + SEQ + CH], stack=r2)
        R_lw = sb("R_lw", [P, 3, SEQ], stack=r2)
        R_b = sb("R_b", [P, 2, SEQ], stack=r2)
        R_e1 = sb("R_e1", [P, 2, SEQ], stack=r2)
        R_e2 = sb("R_e2", [P, 2, SEQ], stack=r2)
        R_g = sb("R_g", [P, SEQ], stack=r2)
        R_kk = sb("R_kk", [P, SEQ], stack=r2)
        R_Kbd = sb("R_Kbd", [P, NU, P], stack=r2)
        R_Rbd = sb("R_Rbd", [P, NU, P], stack=r2)
        R_ABt = sb("R_ABt", [P, NU, P], stack=r2)
        R_UV = sb("R_UV", [P, 2, NU, CH], stack=r2)
        R_G = sb("R_G", [P, 2, NU, P], stack=r2)
        R_C = sb("R_C", [P, 2, NU, CH], stack=r2)
        R_Wbd = sb("R_Wbd", [P, NU, P], stack=r2)
        R_Qbd = sb("R_Qbd", [P, NCH, P], stack=r2)
        R_S = sb("R_S", [P, 2, CH], stack=r2)
        R_X = sb("R_X", [P, 2, CH], stack=r2)
        R_y = sb("R_y", [P, NCH, CH], stack=r2)
        R_st = sb("R_st", [P, NCH, 6], stack=r2)
        R_mv = sb("R_mv", [P, NCH, 2], stack=r2)
        R_lora = sb("R_lora", [P, 4, SEQ], stack=r2)
        R_up = sb("R_up", [P, 5, P], stack=r2)
        r2.close()
        r2 = ExitStack()
        L_zs = sb("L_zs", [P, NT, 2, P], stack=r2)
        L_v = sb("L_v", [P, NT, DV], stack=r2)
        L_qk = sb("L_qk", [P, 2, SEQ], stack=r2)
        L_up = sb("L_up", [P, 2, P], stack=r2)
        L_gg = sb("L_gg", [P, SEQ], stack=r2)
        L_x = sb("L_x", [P, 2, SEQ], stack=r2)
        L_t = sb("L_t", [P, 2, SEQ], stack=r2)
        L_b = sb("L_b", [P, 2, SEQ], stack=r2)
        L_e1 = sb("L_e1", [P, 2, SEQ], stack=r2)
        L_e2 = sb("L_e2", [P, 2, SEQ], stack=r2)
        L_e3 = sb("L_e3", [P, 2, SEQ], stack=r2)
        L_qb = sb("L_qb", [P, 2, SEQ], stack=r2)
        L_kb = sb("L_kb", [P, 2, SEQ], stack=r2)
        L_kd = sb("L_kd", [P, 2, SEQ], stack=r2)
        L_kdt = sb("L_kdt", [P, 2, NT, P], stack=r2)
        L_att = sb("L_att", [P, 2, NT, P], stack=r2)
        L_S = sb("L_S", [P, 2, NCH - 1, DV], stack=r2)
        L_o = sb("L_o", [P, NT, DV], stack=r2)
        L_sq = sb("L_sq", [P, NT, DV], stack=r2)
        r2.close()
        r2 = ExitStack()
        A_qk = sb("A_qk", [P, 2, NT, 2, 2, 64], stack=r2)
        A_t = sb("A_t", [P, NT, 2, 2, 32], stack=r2)
        A_qkT = sb("A_qkT", [P, 2, SEQ], stack=r2)
        A_p = sb("A_p", [P, 2, 2, NT, SEQ], stack=r2)
        A_pT = sb("A_pT", [P, NT, SEQ], stack=r2)
        A_s = sb("A_s", [P, 2, 12], stack=r2)
        A_sq = sb("A_sq", [P, P], stack=r2)
        A_ss = sb("A_ss", [P, NT, DH], stack=r2)
        A_rs = sb("A_rs", [P, NT, DH], stack=r2)
        A_on = sb("A_on", [P, 2, NT, 2 * P], stack=r2)
        A_t2 = sb("A_t2", [P, 2, 2, SEQ], stack=r2)
        A_lam = sb("A_lam", [P, 4 * 64 + 8], stack=r2)
        r2.close()


        R_KR = xf[:, 8:12].rearrange("p k (u n) -> p (k u) n", n=P)
        R_AB = xf[:, 12:16].rearrange("p k (u n) -> p (k u) n", n=P)

        pa = ctx.enter_context(nc.psum_tensor("pa", [P, 2, W], F32))
        pb = ctx.enter_context(nc.psum_tensor("pb", [P, 2, W], F32))
        py = ctx.enter_context(nc.psum_tensor("py", [P, 2, W], F32))
        pt = ctx.enter_context(nc.psum_tensor("pt", [P, 2, W], F32))
        ident = cst[:, C_ID:C_ID + P]
        ones = cst[:, C_ONES:C_ONES + P]
        heads1 = cst[:, C_HEADS:C_HEADS + P]
        level_masks = cst[:, C_LEVEL:C_LEVEL + 2 * LEVELS * CH].rearrange("p (d l n) -> p d l n", d=2, l=LEVELS)

        def level(eng, lv):
            for h, rows_ in enumerate((slice(0, CH), slice(CH, P))):
                if h and eng is nc.gpsimd:
                    eng.drain()
                ins = eng.tensor_tensor(
                    R_C[rows_, lv % 2].rearrange("p (d c) n -> p d c n", d=2),
                    R_G[rows_, h, :, 0:CH].rearrange("p (d c) n -> p d c n", d=2),
                    level_masks[rows_, :, lv].unsqueeze(2).to_broadcast((CH, 2, NCH, CH)), ALU.mult)
            return ins

        def flat(tile):
            return tile[:].rearrange("p u n -> p (u n)")
        ada_flat = ada[:].rearrange("p a b -> p (a b)")

        n_of = {0: 17, FG: 17 + FG + 12 + 4}
        C_FFN0, C_DIFF, C_OUT1, C_FFN1 = 17, 17 + 33, 17 + 33 + 12, 17 + 33 + 16
        PA_SKIP = {0: 0, C_DIFF: C_DIFF - (17 + FG)}

        ACT_AT = {(1, 2): 1, (2, 0): 2, (3, 2): 3, (4, 0): 4, (4, 1): 5, (4, 2): 6}
        DVE_AT = {(1, 0): 0, (1, 2): 1, (2, 2): 2, (3, 0): 3, (4, 1): 4}
        PE_AT = {1: 1, 2: 2}
        S_AT = (0, 1, 2, 3, 4)
        L_AT = (4, 4, 7, 7, 10, 13, 13, 13, 16, 19, 22, 22, 25, 28, 28, 28)
        X_AT = (28, 29, 30, 31, 32)

        const_in = sem("const_in")
        rows_zero = sem("rows_zero")
        rows_in = sem("rows_in")
        x_in_sem = sem("x_in_sem")
        tab_turned = sem("tab_turned")
        tab_copied = sem("tab_copied")
        silu_ready = sem("silu_ready")
        raw_in = [sem(f"raw_in{s}") for s in range(4)]
        hi_done = sem("hi_done")
        lo_done = sem("lo_done")
        unit_done = sem("unit_done")
        adaw_in = [sem(f"adaw_in{s}") for s in range(2)]
        ada_step = sem("ada_step")
        ada_cols = sem("ada_cols")
        ada_out = sem("ada_out")
        tr_done = sem("tr_done")
        h_scaled = sem("h_scaled")
        h_hi = sem("h_hi")
        h_lo = sem("h_lo")
        pa_done = sem("pa_done")
        pa_free = sem("pa_free")

        lora_turned = sem("lora_turned")
        lora_padded = sem("lora_padded")
        lora_mixed = sem("lora_mixed")
        lora_ready = sem("lora_ready")
        bd_zero = sem("bd_zero")
        pool_passed = sem("pool_passed")
        pe_passed = sem("pe_passed")
        pair_done = sem("pair_done")
        zs_ready = sem("zs_ready")
        up_in = sem("up_in")
        rk_turned = sem("rk_turned")
        zf_ready = sem("zf_ready")
        rkv_mixed = sem("rkv_mixed")
        v_turned = sem("v_turned")
        uv_ready = sem("uv_ready")
        sq_ready = sem("sq_ready")
        ss_done = sem("ss_done")
        ss_clamped = sem("ss_clamped")
        rn_ready = sem("rn_ready")
        q_ready = sem("q_ready")
        bonus_done = sem("bonus_done")
        up_done = sem("up_done")
        up_act = sem("up_act")
        logs_ready = sem("logs_ready")
        exps_ready = sem("exps_ready")
        krbd_ready = sem("krbd_ready")
        ab_ready = sem("ab_ready")
        scores_done = sem("scores_done")
        g_ready = sem("g_ready")
        init_ready = sem("init_ready")
        ab_turned = sem("ab_turned")
        abt_ready = sem("abt_ready")
        q_done = sem("q_done")
        qc_ready = sem("qc_ready")
        first_ready = sem("first_ready")
        c1_ready = sem("c1_ready")
        kept_ready = sem("kept_ready")
        bonus_out = sem("bonus_out")
        c_ready = sem("c_ready")
        vc_ready = sem("vc_ready")
        v_done = sem("v_done")
        w_done = sem("w_done")
        wc_ready = sem("wc_ready")
        wbd_ready = sem("wbd_ready")
        tail_done = sem("tail_done")
        ys_var = sem("ys_var")
        ys_rstd = sem("ys_rstd")
        yn_ready = sem("yn_ready")
        ybd_ready = sem("ybd_ready")
        yt_done = sem("yt_done")
        gg_turned = sem("gg_turned")
        gg_ready = sem("gg_ready")
        og_ready = sem("og_ready")
        gla_in = sem("gla_in")
        head_done = sem("head_done")
        gz_ready = sem("gz_ready")
        g_turned = sem("g_turned")
        g_qk = sem("g_qk")
        g_gate = sem("g_gate")
        g_x = sem("g_x")
        g_soft = sem("g_soft")
        g_logs = sem("g_logs")
        g_exps = sem("g_exps")
        g_prod = sem("g_prod")
        g_att = sem("g_att")
        g_kdt_done = sem("g_kdt_done")
        g_kdt = sem("g_kdt")
        g_attm = sem("g_attm")
        g_kv = sem("g_kv")
        g_states = sem("g_states")
        g_o = sem("g_o")
        g_sq = sem("g_sq")
        g_var = sem("g_var")
        g_rstd = sem("g_rstd")
        g_on = sem("g_on")
        g_oT = sem("g_oT")
        split_hi = sem("split_hi")
        split_lo = sem("split_lo")
        ln_in = sem("ln_in")
        diag_ready = sem("diag_ready")
        gate_mm = sem("gate_mm")
        gate_out = sem("gate_out")
        end_var = sem("end_var")
        end_rstd = sem("end_rstd")
        x_ready = sem("x_ready")
        pb_done = sem("pb_done")
        pb_free = sem("pb_free")
        py_done = sem("py_done")
        py_free = sem("py_free")
        gu_turned = sem("gu_turned")
        guh_ready = sem("guh_ready")
        gul_ready = sem("gul_ready")
        ysum_zero = sem("ysum_zero")
        lam_in = sem("lam_in")
        lam_prod = sem("lam_prod")
        lam_exp = sem("lam_exp")
        lam_mm = sem("lam_mm")
        at_rot = sem("at_rot")
        at_out = sem("at_out")
        at_turned = sem("at_turned")
        at_T = sem("at_T")
        at_scores = sem("at_scores")
        at_bias = sem("at_bias")
        at_exp = sem("at_exp")
        at_p = sem("at_p")
        at_pturned = sem("at_pturned")
        at_pT = sem("at_pT")
        at_o = sem("at_o")
        at_sq = sem("at_sq")
        at_var = sem("at_var")
        at_rstd = sem("at_rstd")
        at_on = sem("at_on")
        at_oT = sem("at_oT")
        at_scaled = sem("at_scaled")
        at_hi = sem("at_hi")
        at_done = sem("at_done")
        out_sem = sem("out_sem")
        x_done = [sem(f"x_done{d}") for d in range(2)]
        xs_ready = [sem(f"xs_ready{d}") for d in range(2)]
        u_ready = [sem(f"u_ready{d}") for d in range(2)]
        s_done = [sem(f"s_done{d}") for d in range(2)]
        s_ready = [sem(f"s_ready{d}") for d in range(2)]
        u_done = [sem(f"u_done{d}") for d in range(2)]
        y_done = [sem(f"y_done{d}") for d in range(2)]

        block = ctx.enter_context(nc.Block())
        cond = ada_w.rearrange("a b (s i p) (j w) -> (a b) j s p i w", p=P, i=UK, w=W)

        def load_unit(sp, c, s, src, width=W, first=False):
            if not first:
                sp.wait_ge(lo_done, c * 4 + s + 1)
            sp.dma_start(raw[:, s, :, 0:width], src).then_inc(raw_in[s], 16)

        def load_cond(sp, j, s, src, first=False):
            if not first:
                sp.wait_ge(ada_step, j * 17 + (5 + 4 * (s - 2) if s >= 2 else 4 * s - 4))
            sp.dma_start(adaw[:, s % 2], src).then_inc(adaw_in[s % 2], 16)

        def high(act, c, s, width=W):
            act.wait_ge(raw_in[s], c * 16 + 16)
            act.wait_ge(unit_done, c * 4 + s + 1)
            act.activation(wh[:, s % 2, :, 0:width], raw[:, s, :, 0:width], ACT.Copy).then_inc(hi_done, 1)

        def low(dve, c, s, width=W):
            dve.wait_ge(hi_done, c * 4 + s + 1)
            dve.tensor_tensor(wl[:, s % 2, :, 0:width], raw[:, s, :, 0:width],
                              wh[:, s % 2, :, 0:width].bitcast(F32), ALU.subtract).then_inc(lo_done, 1)

        def cond_steps(dve, j, a, b):
            for k in range(a, b):
                s, i = k // UK, k % UK
                if i == 0:
                    dve.wait_ge(adaw_in[s % 2], j * 32 + 16 * (s // 2) + 16)
                if k < 2:
                    dve.wait_ge(ada_step, j * 17 + 1)
                    dve.tensor_scalar(acc[:, k % 2], adaw[:, s % 2, i], silu_c[:, k:k + 1], None,
                                      ALU.mult).then_inc(ada_step, 1)
                else:
                    dve.wait_ge(ada_step, j * 17 + k)
                    dve.scalar_tensor_tensor(acc[:, k % 2], adaw[:, s % 2, i], silu_c[:, k:k + 1],
                                             acc[:, k % 2], ALU.mult, ALU.add).then_inc(ada_step, 1)

        def cond_unit(dve, j, s):
            cond_steps(dve, j, UK * s, UK * s + UK)

        def cond_sum(dve, j, first=False):
            dve.wait_ge(ada_step, j * 17 + 17)
            if not first:
                dve.wait_ge(ada_cols, j)
            dve.tensor_tensor(asum[:], acc[:, 0], acc[:, 1], ALU.add).then_inc(ada_step, 1)

        def cond_cols(pe, j, first=False, bank=None):
            pe.wait_ge(ada_step, j * 17 + 18)
            if not first:
                pe.wait_ge(ada_out, j)
            bank = pt[:, 1] if bank is None else bank
            for m in range(4):
                mm = pe.matmul(bank[:, m:m + 1], asum[:, m * P:(m + 1) * P], ones[:, 0:1], start=(m == 0),
                               stop=True, skip_group_check=True)
            mm.then_inc(ada_cols, 1)

        def cond_store(dve, j, bank=None):
            bank = pt[:, 1] if bank is None else bank
            dve.wait_ge(ada_cols, j + 1)
            dve.tensor_tensor(ada_flat[:, bass.ds(j * 4, 4)], bank[:, 0:4], tab[:, bass.ds(j * 4 + T_ADA, 4)],
                              ALU.add).then_inc(ada_out, 1)

        def multiply(pe, c, s, lhs, bank, width=W, start=True, stop=True, tile0=None, k0=None,
                     free=None):
            pe.wait_ge(lo_done, c * 4 + s + 5)
            hi, lo = lhs
            for i in range(NT):
                if free is not None:
                    pe.wait_ge(free[0], free[1] * 2 + 1 + i)
                for k in range(UK):
                    kk = (k0 if k0 is not None else UK * s) + k
                    a_hi, a_lo = hi[:, kk, i * P:(i + 1) * P], lo[:, kk, i * P:(i + 1) * P]
                    w_hi, w_lo = wh[:, s % 2, k, 0:width], wl[:, s % 2, k, 0:width]
                    o = bank[:, i, 0:width]
                    pe.matmul(o, a_hi, w_hi, start=start and k == 0, stop=False)
                    pe.matmul(o, a_hi, w_lo, start=False, stop=False)
                    mm = pe.matmul(o, a_lo, w_hi, start=False, stop=stop and k == UK - 1)
                if i == 0 and tile0 is not None:
                    mm.then_inc(tile0, 1)
            mm.then_inc(unit_done, 1)

        def project(pe, c, n, lhs, done, free, bank, width=W):
            for s in range(4):
                multiply(pe, c, s, lhs, bank, width, start=(s == 0), stop=(s == 3), tile0=done if s == 3 else None,
                         free=(free, n) if s == 0 else None)

        def turn_pe(pe, call):
            for g in range(KT // 2):
                n = call * 8 + g
                if n >= 2:
                    pe.wait_ge(h_scaled, n - 1)
                for j in range(2):
                    for i in range(NT):
                        mm = pe.transpose(py[:, g % 2, j * SEQ + i * P:j * SEQ + (i + 1) * P],
                                          xt[:, i, (2 * g + j) * P:(2 * g + j + 1) * P], ident)
                mm.then_inc(tr_done, 1)

        def turn_act(act, call):
            for g in range(KT // 2):
                n = call * 8 + g
                act.wait_ge(h_scaled, n + 1)
                act.activation(hth[:, 2 * g:2 * g + 2, :], htmp[:, g % 2], ACT.Copy).then_inc(h_hi, 1)

        def turn_dve(dve, call, sub):
            dve.tensor_scalar(small[:, 0:16], ada[:, sub, 16:32], 1.0, None, ALU.add)
            dve.drain()

            def lower(g):
                dve.wait_ge(h_hi, call * 8 + g + 1)
                dve.tensor_tensor(htl[:, 2 * g:2 * g + 2, :], htmp[:, g % 2],
                                  hth[:, 2 * g:2 * g + 2, :].bitcast(F32), ALU.subtract).then_inc(h_lo, 1)
            for g in range(KT // 2):
                dve.wait_ge(tr_done, call * 8 + g + 1)
                if g >= 2:
                    dve.wait_ge(h_lo, call * 8 + g - 1)
                for j in range(2):
                    k = 2 * g + j
                    ins = dve.tensor_scalar(htmp[:, g % 2, j], py[:, g % 2, j * SEQ:(j + 1) * SEQ],
                                            small[:, k:k + 1], ada[:, sub, k:k + 1], ALU.mult, ALU.add)
                ins.then_inc(h_scaled, 1)
                if g:
                    lower(g - 1)
            lower(KT // 2 - 1)

        def split_act(act, call):
            for g in range(KT // 2):
                act.activation(hth[:, 2 * g:2 * g + 2], xf[:, 2 * g:2 * g + 2], ACT.Copy).then_inc(split_hi, 1)

        def split_dve(dve, call):
            for g in range(KT // 2):
                dve.wait_ge(split_hi, call * 8 + g + 1)
                dve.tensor_tensor(htl[:, 2 * g:2 * g + 2], xf[:, 2 * g:2 * g + 2],
                                  hth[:, 2 * g:2 * g + 2].bitcast(F32), ALU.subtract).then_inc(split_lo, 1)

        def end_load(act, n, c):
            act.wait_ge(unit_done, c * 4 + 6)
            act.dma_start(lng[:], ln_g[n // 2, n % 2].partition_broadcast(P)).then_inc(ln_in, 16)
            act.dma_start(lnb[:], ln_b[n // 2, n % 2].partition_broadcast(P)).then_inc(ln_in, 16)

        def end_pe(pe, n):
            for g in range(4):
                pe.wait_ge(diag_ready, n * 4 + g + 1)
                if n * 4 + g >= 2:
                    pe.wait_ge(gate_out, n * 4 + g - 1)
                for m in range(4):
                    mm = pe.matmul(pb[:, g % 2, m * P:(m + 1) * P], ones, diag[:, m], start=True, stop=True)
                mm.then_inc(gate_mm, 1)

        def end_act(act, n):
            for g in range(4):
                act.wait_ge(gate_mm, n * 4 + g + 1)
                act.activation(gate_bc[:, g * W:(g + 1) * W], pb[:, g % 2], ACT.Copy, bias=1.0).then_inc(gate_out, 1)
            for i in range(NT):
                act.wait_ge(end_var, n * NT + i + 1)
                act.activation(small[:, 36 + i:37 + i], small[:, 34 + i:35 + i], ACT.Ln)
                act.drain()
                act.activation(small[:, 38 + i:39 + i], small[:, 36 + i:37 + i], ACT.Exp, scale=-0.5).then_inc(end_rstd, 1)

        def end_dve(dve, n):
            for g in range(4):
                if g or n:
                    dve.wait_ge(gate_mm, n * 4 + g)
                for m in range(4):
                    k = 32 + 4 * g + m
                    ins = dve.tensor_scalar(diag[:, m], ident, ada[:, n, k:k + 1], None, ALU.mult)
                ins.then_inc(diag_ready, 1)
            dve.wait_ge(gate_out, n * 4 + 4)
            stats = small[:, 40:40 + 24].rearrange("p (c s) -> p c s", s=6)
            for i in range(NT):
                dve.tensor_tensor(ysum[:, i], ysum[:, i], gate_bc[:], ALU.mult)
                dve.drain()
                dve.scalar_tensor_tensor(xt[:, i], xt[:, i], ALPHA, ysum[:, i], ALU.mult, ALU.add)
                dve.drain()
                for c in range(4):
                    dve.bn_stats(stats[:, c], xt[:, i, c * W:(c + 1) * W])
                dve.drain()
                dve.bn_aggr(small[:, 64 + 2 * i:66 + 2 * i], stats.rearrange("p c s -> p (c s)"))
                dve.drain()
                dve.tensor_scalar(small[:, 34 + i:35 + i], small[:, 65 + 2 * i:66 + 2 * i], EPS, None, ALU.add).then_inc(end_var, 1)
            dve.wait_ge(ln_in, n * 32 + 32)
            for i in range(NT):
                dve.wait_ge(end_rstd, n * NT + i + 1)
                dve.tensor_scalar(xt[:, i], xt[:, i], small[:, 64 + 2 * i:65 + 2 * i], small[:, 38 + i:39 + i],
                                  ALU.subtract, ALU.mult)
            dve.drain()
            for i in range(NT):
                dve.tensor_tensor(xt[:, i], xt[:, i], lng[:], ALU.mult)
            dve.drain()
            for i in range(NT):
                dve.tensor_tensor(xt[:, i], xt[:, i], lnb[:], ALU.add).then_inc(x_ready, 1)

        def out_sp(sp, c0, wv):
            for q in range(4):
                for s in range(4):
                    load_unit(sp, c0 + q, s, wv[s, :, :, q * W:(q + 1) * W])

        def out_act(act, c0, n0):
            for q in range(4):
                for s in range(4):
                    high(act, c0 + q, s)
                    if q and s == 0:
                        act.wait_ge(pa_done, n0 + q)
                        act.activation(ysum[:, 0, (q - 1) * W:q * W], pa[:, 0], ACT.Copy).then_inc(pa_free, 1)
                        act.wait_ge(unit_done, (c0 + q) * 4 + 2)
                        act.activation(ysum[:, 1, (q - 1) * W:q * W], pa[:, 1], ACT.Copy).then_inc(pa_free, 1)
            act.wait_ge(pa_done, n0 + 4)
            act.activation(ysum[:, 0, 3 * W:], pa[:, 0], ACT.Copy).then_inc(pa_free, 1)
            act.wait_ge(unit_done, (c0 + 4) * 4 + 2)
            act.activation(ysum[:, 1, 3 * W:], pa[:, 1], ACT.Copy).then_inc(pa_free, 1)

        def out_dve(dve, c0):
            for q in range(4):
                for s in range(4):
                    low(dve, c0 + q, s)

        def out_pe(pe, c0, n0):
            for q in range(4):
                project(pe, c0 + q, n0 + q, (hth, htl), pa_done, pa_free, pa)

        def rotate(eng, t, slot):
            def part(i):
                src = qkv[:, i, 0:2 * D].rearrange("p (j n) -> p j n", j=2)[:, :, bass.ds(t * P, P)].rearrange(
                    "p j (c f) -> p j c f", c=2)

                def wave(at):
                    return cst[:, at + 32 * i:at + 32 * i + 32].unsqueeze(1).unsqueeze(1).to_broadcast((P, 2, 2, 32))
                return (src[:, :, :, 0:32], src[:, :, :, 32:64], A_qk[:, slot, i, :, :, 0:32], A_qk[:, slot, i, :, :, 32:64],
                        wave(C_COS), wave(C_SIN))
            for i in range(NT):
                x1, x2, o1, o2, cos, sin = part(i)
                eng.tensor_tensor(o1, x1, cos, ALU.mult)
                eng.tensor_tensor(A_t[:, i], x2, sin, ALU.mult)
                eng.tensor_tensor(o2, x2, cos, ALU.mult)
            eng.drain()
            for i in range(NT):
                x1, x2, o1, o2, cos, sin = part(i)
                eng.tensor_tensor(o1, o1, A_t[:, i], ALU.subtract)
            eng.drain()
            for i in range(NT):
                x1, x2, o1, o2, cos, sin = part(i)
                eng.tensor_tensor(A_t[:, i], x1, sin, ALU.mult)
            eng.drain()
            for i in range(NT):
                x1, x2, o1, o2, cos, sin = part(i)
                eng.tensor_tensor(o2, o2, A_t[:, i], ALU.add)
            eng.drain().then_inc(at_rot, 1)

        def heads(eng, body):
            with eng.Fori(0, DH // 2 - 1) as m:
                body(m * 2, 0, True)
                body(m * 2 + 1, 1, True)
            body(DH - 2, 0, True)
            body(DH - 1, 1, False)

        def turn_pe_at(pe, n):
            pe.wait_ge(x_ready, 2 * n)
            turn_pe(pe, n)
            pe.wait_ge(h_lo, 8 * n + 8)

        def in_act(act, c0, dest, last):
            high(act, c0, 0)
            high(act, c0, 1)
            with act.Fori(0, 11) as t:
                high(act, t + c0, 2)
                high(act, t + c0, 3)
                high(act, t + c0 + 1, 0)
                act.wait_ge(pa_done, t + c0 + 1 - PA_SKIP[c0])
                act.activation(dest[:, 0, bass.ds(t * W, W)], pa[:, 0], ACT.Copy).then_inc(pa_free, 1)
                act.wait_ge(unit_done, t * 4 + 4 * c0 + 6)
                act.activation(dest[:, 1, bass.ds(t * W, W)], pa[:, 1], ACT.Copy).then_inc(pa_free, 1)
                high(act, t + c0 + 1, 1)
            high(act, c0 + 11, 2)
            high(act, c0 + 11, 3)
            act.wait_ge(pa_done, c0 + 12 - PA_SKIP[c0])
            act.activation(dest[:, 0, 11 * W:12 * W], pa[:, 0], ACT.Copy).then_inc(pa_free, 1)
            act.wait_ge(unit_done, 4 * (c0 + 11) + 6)
            act.activation(dest[:, 1, 11 * W:12 * W], pa[:, 1], ACT.Copy).then_inc(pa_free, 1)

        def ffn_sp(sp, c0, layer, j0=None):
            w_in = ffn_w_in[layer].rearrange("(s i p) (h g w) -> h g s p i w", p=P, i=UK, h=2, w=W)
            w_out = ffn_w_out[layer].rearrange("(g i p) (q w) -> g q p i w", p=P, i=UK, w=W)

            def group(g, n, sub):
                load_unit(sp, g * 3 + (c0 - 1) + n // 4 if g is not None else c0 + n // 4, n % 4,
                          w_in[n // 4, bass.ds(g, 1) if g is not None else 0, n % 4])
                if j0 is not None and n:
                    m, u = (n - 1) // 4, (n - 1) % 4
                    if g is None:
                        load_cond(sp, j0 + m, u, cond[sub, m, u])
                    else:
                        j = g * 2 + m
                        load_cond(sp, j + j0, u, cond[sub, bass.ds(j - (12 if sub == 3 else 0), 1), u])
            for n in range(8):
                group(None, n, 2)
            if j0 is not None:
                load_cond(sp, j0 + 1, 3, cond[2, 1, 3])

            def step(g, sub):
                for n in range(8):
                    group(g, n, sub)
                for q in range(4):
                    load_unit(sp, g * 3 + (c0 + 1), q, w_out[bass.ds(g - 1, 1), q])
                    if j0 is not None and q == 2:
                        load_cond(sp, g * 2 + (j0 + 1), 3, cond[sub, bass.ds(g * 2 + (1 if sub == 2 else -11), 1), 3])
            if j0 is not None:
                with sp.Fori(1, 6) as g:
                    step(g, 2)
                with sp.Fori(6, FG) as g:
                    step(g, 3)
            else:
                with sp.Fori(1, FG) as g:
                    step(g, None)
            for q in range(4):
                load_unit(sp, c0 + 32, q, w_out[FG - 1, q])

        def ffn_act(act, c0, f, n_pa):
            def gate_up(c, g):
                for s in range(1, 4):
                    high(act, c, s)
                high(act, c + 1, 0)
                if isinstance(g, int) and g == 0:
                    pass
                else:
                    act.wait_ge(gu_turned, g)
                act.wait_ge(pa_done, g + (n_pa - f + 1))
                act.activation(gu[:, 0], pa[:, 0], ACT.Silu).then_inc(pa_free, 1)
                high(act, c + 1, 1)
                act.wait_ge(unit_done, c * 4 + 6)
                act.activation(gu[:, 1], pa[:, 1], ACT.Silu).then_inc(pa_free, 1)
                high(act, c + 1, 2)
                high(act, c + 1, 3)

            def turned(g):
                act.wait_ge(gu_turned, g + 1)
                act.activation(guh[:, 0:2].rearrange("p k t -> p (k t)"), pt[:, 0], ACT.Copy)
                act.activation(guh[:, 2:4].rearrange("p k t -> p (k t)"), pb[:, 0], ACT.Copy).then_inc(guh_ready, 1)
            high(act, c0, 0)
            gate_up(c0, f)
            high(act, c0 + 2, 0)
            turned(f)
            with act.Fori(1, FG) as g:
                c = g * 3 + (c0 - 1)
                gate_up(c, g + f)
                for q in range(4):
                    high(act, c + 2, q)
                high(act, c + 3, 0)
                turned(g + f)
            for q in range(1, 4):
                high(act, c0 + 32, q)

        def ffn_dve(dve, c0, f, u0, j0=None):
            def cond_at(j, n):
                if j0 is not None:
                    cond_unit(dve, j + (n - 1) // 4, (n - 1) % 4)
                    if n == 4:
                        cond_sum(dve, j)

            def product(i, c, g):
                if i == 0:
                    dve.wait_ge(pb_done, g + 1)
                    dve.wait_ge(pa_free, 2 * g + 2 * (n_of[f] - f) + 3)
                else:
                    dve.wait_ge(unit_done, c * 4 + 10)
                    dve.wait_ge(pa_free, 2 * g + 2 * (n_of[f] - f) + 4)
                dve.tensor_tensor(gu[:, i], gu[:, i], pb[:, i], ALU.mult).then_inc(pb_free, 1)

            def add(c, q, u):
                dve.wait_ge(py_done, u + 1)
                dve.tensor_tensor(ysum[:, 0, q * W:(q + 1) * W], ysum[:, 0, q * W:(q + 1) * W], py[:, 0], ALU.add).then_inc(py_free, 1)
                dve.wait_ge(unit_done, c * 4 + q + 3)
                dve.tensor_tensor(ysum[:, 1, q * W:(q + 1) * W], ysum[:, 1, q * W:(q + 1) * W], py[:, 1], ALU.add).then_inc(py_free, 1)

            def lower(g):
                dve.wait_ge(guh_ready, g + 1)
                dve.tensor_tensor(gul[:, 0:2].rearrange("p k t -> p (k t)"), pt[:, 0],
                                  guh[:, 0:2].rearrange("p k t -> p (k t)").bitcast(F32), ALU.subtract)
                dve.tensor_tensor(gul[:, 2:4].rearrange("p k t -> p (k t)"), pb[:, 0],
                                  guh[:, 2:4].rearrange("p k t -> p (k t)").bitcast(F32), ALU.subtract).then_inc(gul_ready, 1)
            low(dve, c0, 0)
            for n in range(1, 8):
                low(dve, c0 + n // 4, n % 4)
                cond_at(j0, n)
            if j0 is not None:
                cond_unit(dve, j0 + 1, 3)
            low(dve, c0 + 2, 0)
            product(0, c0, f)
            product(1, c0, f)
            if j0 is not None:
                cond_store(dve, j0)
                cond_sum(dve, j0 + 1)
            lower(f)
            if j0 is not None:
                cond_store(dve, j0 + 1)
            dve.wait_ge(ysum_zero, 1 if f == 0 else 2)
            with dve.Fori(1, FG) as g:
                c = g * 3 + (c0 - 1)
                for n in range(1, 8):
                    low(dve, c + n // 4, n % 4)
                    cond_at(g * 2 + (j0 or 0), n)
                low(dve, c + 2, 0)
                product(0, c, g + f)
                product(1, c, g + f)
                if j0 is not None:
                    cond_store(dve, g * 2 + j0)
                for q in range(1, 4):
                    low(dve, c + 2, q)
                    add(c + 2, q - 1, g * 4 + (u0 - 4 + q - 1))
                    if q == 2 and j0 is not None:
                        cond_unit(dve, g * 2 + (j0 + 1), 3)
                if j0 is not None:
                    cond_sum(dve, g * 2 + (j0 + 1))
                low(dve, c + 3, 0)
                add(c + 2, 3, g * 4 + (u0 - 1))
                lower(g + f)
                if j0 is not None:
                    cond_store(dve, g * 2 + (j0 + 1))
            for q in range(1, 4):
                low(dve, c0 + 32, q)
                add(c0 + 32, q - 1, u0 + 40 + q - 1)
            add(c0 + 32, 3, u0 + 43)

        def ffn_pe(pe, c0, f, u0, j0=None):
            def turn(g):
                pe.wait_ge(pb_free, g * 2 + 4)
                for k in range(UK):
                    bank = pt[:, 0] if k < 2 else pb[:, 0]
                    for i in range(NT):
                        at = (k % 2) * SEQ + i * P
                        mm = pe.transpose(bank[:, at:at + P], gu[:, i, k * P:(k + 1) * P], ident)
                mm.then_inc(gu_turned, 1)

            def output(c, u, g):
                pe.wait_ge(gul_ready, g + 1)
                for q in range(4):
                    multiply(pe, c, q, (guh, gul), py, tile0=py_done, k0=0, free=(py_free, u + q))
            project(pe, c0, n_of[f], (hth, htl), pa_done, pa_free, pa)
            project(pe, c0 + 1, f, (hth, htl), pb_done, pb_free, pb)
            if j0 is not None:
                cond_cols(pe, j0)
            turn(f)
            if j0 is not None:
                cond_cols(pe, j0 + 1)
            with pe.Fori(1, FG) as g:
                c = g * 3 + (c0 - 1)
                project(pe, c, g + n_of[f], (hth, htl), pa_done, pa_free, pa)
                pe.wait_ge(gul_ready, g + f)
                project(pe, c + 1, g + f, (hth, htl), pb_done, pb_free, pb)
                if j0 is not None:
                    cond_cols(pe, g * 2 + j0)
                output(c + 2, g * 4 + (u0 - 4), g + (f - 1))
                turn(g + f)
                if j0 is not None:
                    cond_cols(pe, g * 2 + (j0 + 1))
            output(c0 + 32, u0 + 40, f + 10)

        ab_w = ab_w_in[0].rearrange("(s i p) n -> s p i n", p=P, i=UK)
        LASTW = Z - (ABC - 1) * W

        def vectors():
            yield T_LN_G, ln_g.rearrange("a b (k p) -> (a b k) p", p=P)
            yield T_LN_B, ln_b.rearrange("a b (k p) -> (a b k) p", p=P)
            yield T_MU, rwkv_mu[0, 0:3 * RW].rearrange("(k p) -> k p", p=P)
            yield T_MU + 24, rwkv_mu[0:1, Z_WD:Z_AD]
            yield T_MU + 25, rwkv_mu[0:1, Z_AD:Z_GD]
            yield T_MU + 26, rwkv_mu[0, Z_GD:Z_Q].rearrange("(k p) -> k p", p=P)
            yield T_W0, rwkv_w0[0].rearrange("a (k p) -> (a k) p", p=P)
            yield T_A0, rwkv_a0[0].rearrange("(k p) -> k p", p=P)
            yield T_KK, rwkv_k_k[0].rearrange("(k p) -> k p", p=P)
            yield T_KA, rwkv_k_a[0].rearrange("(k p) -> k p", p=P)
            yield T_RK, rwkv_r_k[0].rearrange("(k h) n -> k (h n)", h=2)
            yield T_GNG, rwkv_gn_g[0].rearrange("(k p) -> k p", p=P)
            yield T_GNB, rwkv_gn_b[0].rearrange("(k p) -> k p", p=P)
            yield T_GB, gla_gate_b[0].rearrange("a (k p) -> (a k) p", p=P)
            yield T_NG, gla_norm_g[0].rearrange("(k p) -> k p", p=P)
            yield T_SUB, diff_subln_g[0:1, :]
            yield T_C, c_in[0].rearrange("(k p) -> k p", p=P)
            ab = ada_b.rearrange("a b (k p) -> (a b k) p", p=P)
            yield T_ADA, ab[0:96]
            yield T_ADA + 96, ab[96:192]

        @block.sync
        def _(sp):
            sp.dma_start(cst[:], consts).then_inc(const_in, 16)
            sp.wait_ge(rows_zero, 1)
            for col, src in vectors():
                tile = max(i for i in range(4) if TABS[i] <= col)
                r = col - TABS[tile]
                sp.dma_start(rows[r:r + src.shape[0], tile, 0:src.shape[1]], src).then_inc(rows_in, 16)
            for s in range(4):
                load_cond(sp, 0, s, cond[0, 0, s], first=(s < 2))
            sp.dma_start(xt[:], x_in[0].rearrange("(i p) d -> p i d", p=P)).then_inc(x_in_sem, 16)
            with sp.Fori(1, 8) as j:
                for s in range(4):
                    load_cond(sp, j, s, cond[0, bass.ds(j, 1), s])
            for s in range(4):
                load_unit(sp, 0, s, ab_w[s, :, :, 0:W], first=True)
            with sp.Fori(1, 12) as c:
                for s in range(4):
                    load_unit(sp, c, s, ab_w[s, :, :, bass.ds(c * W, W)])
            for s in range(4):
                load_unit(sp, 12, s, ab_w[s, :, :, 12 * W:Z], LASTW)
            with sp.Fori(0, 2) as t:
                for h in range(2):
                    for s in range(4):
                        load_cond(sp, t * 2 + (8 + h), s, cond[0, bass.ds(t * 2 + (8 + h), 1), s])
            with sp.Fori(2, PAIRS) as t:
                for h in range(2):
                    for s in range(4):
                        load_cond(sp, t * 2 + (8 + h), s, cond[1, bass.ds(t * 2 + (h - 4), 1), s])
            gup_v = gla_gate_up[0].rearrange("a r n -> r a n")
            sp.wait_ge(tail_done, PAIRS)
            with sp.Fori(0, GH) as t:
                sp.wait_ge(head_done, t + 1)
                sp.dma_start(L_up[0:GLORA], gup_v[:, :, bass.ds(t * DK, DK)]).then_inc(gla_in, 16)
            sp.wait_ge(head_done, 1 + GH)
            ab_wo = ab_w_out[0].rearrange("(s i p) n -> s p i n", p=P, i=UK)
            out_sp(sp, 13, ab_wo)
            ffn_sp(sp, C_FFN0, 0, 24)
            dw = diff_w_in[0].rearrange("(s i p) n -> s p i n", p=P, i=UK)
            for t in range(2):
                for s in range(4):
                    load_unit(sp, t + C_DIFF, s, dw[s, :, :, t * W:(t + 1) * W])
                    load_cond(sp, t + 46, s, cond[3, t + 10, s])
            with sp.Fori(2, 12) as t:
                for s in range(4):
                    load_unit(sp, t + C_DIFF, s, dw[s, :, :, bass.ds(t * W, W)])
            out_sp(sp, C_OUT1, diff_w_out[0].rearrange("(s i p) n -> s p i n", p=P, i=UK))
            ffn_sp(sp, C_FFN1, 1)
            out_v = out[0].rearrange("(i p) d -> p i d", p=P)
            for i in range(NT):
                sp.wait_ge(x_ready, 7 + i)
                sp.dma_start(out_v[:, i], xt[:, i]).then_inc(out_sem, 16)
            sp.wait_ge(out_sem, 32)

        @block.gpsimd
        def _(pool):
            pool.memset(rows[:], 0.0).then_inc(rows_zero, 1)
            pool.wait_ge(unit_done, 2 + 4 * ABC)
            for tile in (R_Kbd, R_Rbd, R_Wbd, R_Qbd):
                pool.memset(tile[:], 0.0)
            pool.memset(R_vp[:], 0.0)
            pool.memset(R_zf[:], 0.0)
            pool.memset(R_G[:].rearrange("p a b c -> p (a b c)")[:, 0:4 * (SEQ + 2)], 0.0)
            pool.drain().then_inc(bd_zero, 1)
            pool.wait_ge(lora_ready, 3)
            pool.wait_ge(pa_free, 2 + 2 * ABC)

            def next_z(n):
                for i in range(NT):
                    src = z[:, i, 0:3 * RW].rearrange("p (j n) -> p j n", n=RW)
                    pool.tensor_copy(R_zs[:, i], src[:, :, bass.ds(n * P, P)])
                pool.drain().then_inc(zs_ready, 1)

            def both(row):
                return row.unsqueeze(1).to_broadcast((row.shape[0], 2, SEQ))

            def units(tile, rows_, at):
                return tile[rows_, :, at:at + CH]
            full, top, low_half = slice(0, P), slice(0, CH), slice(CH, P)

            def next_factors(n):
                pool.wait_ge(exps_ready, n + 1)
                pool.wait_ge(q_ready, n + 1)
                pool.sem_inc(pool_passed, 1)
                pool.tensor_tensor(units(R_KR, full, 0), both(R_kk[:]), R_lw[:, 0:2], ALU.mult)
                pool.tensor_tensor(units(R_KR, full, CH), both(R_rk[:, 0]), R_e1[:], ALU.mult)
                for rows_, at_a, at_b in ((top, 0, CH), (low_half, CH, 0)):
                    pool.drain()
                    pool.tensor_tensor(units(R_AB, rows_, at_a), both(R_sh[rows_, 0]), R_e2[rows_], ALU.mult)
                    pool.tensor_tensor(units(R_AB, rows_, at_b), both(R_rk[rows_, 1]), R_e2[rows_], ALU.mult)
                pool.drain().then_inc(ab_ready, 1)

            def pool_pair(t, more):
                pool.wait_ge(pair_done, t + 1)
                pool.sem_inc(pool_passed, 1)
                pool.memset(R_UV[:], 0.0)
                pool.drain().then_inc(init_ready, 1)
                if more:
                    pool.wait_ge(rk_turned, t + 1)
                    pool.sem_inc(pool_passed, 1)
                    next_z(t + 1)
                pool.tensor_copy(R_Kbd[0:CH, :, 0:CH], R_KR[0:CH, :, 0:CH])
                pool.tensor_copy(R_Rbd[0:CH, :, 0:CH], R_KR[0:CH, :, CH:P])
                pool.drain()
                pool.tensor_copy(R_Kbd[CH:P, :, CH:P], R_KR[CH:P, :, 0:CH])
                pool.tensor_copy(R_Rbd[CH:P, :, CH:P], R_KR[CH:P, :, CH:P])
                pool.drain().then_inc(krbd_ready, 1)
                for lv in range(2, LEVELS):
                    pool.wait_ge(first_ready if lv == 2 else q_done, t + 1 if lv == 2 else t * (LEVELS - 1) + lv - 2)
                    pool.sem_inc(pool_passed, 1)
                    level(pool, lv)
                    pool.drain().then_inc(c_ready, 1)
                if more:
                    pool.wait_ge(ab_turned, t + 1)
                    pool.sem_inc(pool_passed, 1)
                    next_factors(t + 1)
            next_z(0)
            next_factors(0)
            with pool.Fori(0, PAIRS - 1) as t:
                pool_pair(t, True)
            pool_pair(PAIRS - 1, False)
            pool.wait_ge(tail_done, PAIRS)
            pool.sem_inc(pool_passed, 1)
            with pool.Fori(0, GH) as t:
                pool.wait_ge(head_done, t + 1)
                pool.sem_inc(pool_passed, 1)
                for i in range(NT):
                    src = z[:, i, Z_Q:Z_V].rearrange("p (j n) -> p j n", n=GH * DK)
                    pool.tensor_copy(L_zs[:, i], src[:, :, bass.ds(t * DK, DK)])
                    pool.tensor_copy(L_v[:, i], z[:, i, bass.ds(t * DV + Z_V, DV)])
                pool.drain().then_inc(gz_ready, 1)
            pool.wait_ge(x_ready, 2)
            pool.memset(ysum[:], 0.0).then_inc(ysum_zero, 1)
            pool.wait_ge(unit_done, 2 + 4 * C_OUT1)
            pool.wait_ge(pa_free, 2 + 2 * (17 + FG + 12))
            pool.sem_inc(pool_passed, 1)
            rotate(pool, 0, 0)
            rotate(pool, 1, 1)
            with pool.Fori(1, DH // 2) as m:
                for slot in range(2):
                    pool.wait_ge(at_turned, m * 2 + (slot - 1))
                    pool.sem_inc(pool_passed, 1)
                    rotate(pool, m * 2 + slot, slot)
            pool.wait_ge(x_ready, 6)
            pool.memset(ysum[:], 0.0).then_inc(ysum_zero, 1)

        @block.scalar
        def _(act):
            act.wait_ge(tab_turned, 1)
            act.activation(tab[:], pa[:, 0, 0:T_N], ACT.Copy).then_inc(tab_copied, 1)
            act.wait_ge(tab_copied, 1)
            act.activation(silu_c[:], tab[:, T_C:T_C + KT], ACT.Silu).then_inc(silu_ready, 1)
            turn_act(act, 0)

            def store_z(c, width=W):
                act.wait_ge(pa_done, c + 1)
                act.activation(z[:, 0, bass.ds(c * W, width)], pa[:, 0, 0:width], ACT.Copy).then_inc(pa_free, 1)
                act.wait_ge(unit_done, c * 4 + 6)
                act.activation(z[:, 1, bass.ds(c * W, width)], pa[:, 1, 0:width], ACT.Copy).then_inc(pa_free, 1)

            high(act, 0, 0)
            high(act, 0, 1)
            with act.Fori(0, 11) as c:
                high(act, c, 2)
                high(act, c, 3)
                high(act, c + 1, 0)
                act.wait_ge(pa_done, c + 1)
                act.activation(z[:, 0, bass.ds(c * W, W)], pa[:, 0], ACT.Copy).then_inc(pa_free, 1)
                act.wait_ge(unit_done, c * 4 + 6)
                act.activation(z[:, 1, bass.ds(c * W, W)], pa[:, 1], ACT.Copy).then_inc(pa_free, 1)
                high(act, c + 1, 1)
            high(act, 11, 2)
            high(act, 11, 3)
            store_z(11)
            for s in range(4):
                high(act, 12, s, LASTW)
            store_z(12, LASTW)
            act.wait_ge(bd_zero, 1)
            act.wait_ge(lora_turned, 1)
            pad4 = R_G[:].rearrange("p a b c -> p (a b c)")[:, 0:4 * (SEQ + 2)].rearrange("p (j t) -> p j t", t=SEQ + 2)
            act.activation(pad4[0:LORA, 0:2, 1:1 + SEQ], py[0:LORA, 0].rearrange("p (j t) -> p j t", t=SEQ), ACT.Copy)
            act.activation(pad4[:, 2:4, 1:1 + SEQ], py[:, 1].rearrange("p (j t) -> p j t", t=SEQ),
                           ACT.Copy).then_inc(lora_padded, 1)
            act.wait_ge(lora_mixed, 1)
            act.activation(R_lora[0:LORA, 0], R_lora[0:LORA, 0], ACT.Tanh).then_inc(lora_ready, 1)
            act.activation(R_lora[:, 2:4], R_lora[:, 2:4], ACT.Sigmoid).then_inc(lora_ready, 1)

            w_up_v = rwkv_w_up[0].rearrange("a r n -> r a n")
            g_up_v = rwkv_g_up[0].rearrange("(i p) n -> p i n", p=P)

            def next_act(n, piece):
                if piece == 0:
                    if not (isinstance(n, int) and n == 0):
                        act.wait_ge(up_done, n)
                    act.dma_start(R_up[0:LORA, 0:2, :], w_up_v[:, :, bass.ds(n * P, P)]).then_inc(up_in, 16)
                    act.dma_start(R_up[0:LORA, 2, :], rwkv_a_up[0][:, bass.ds(n * P, P)]).then_inc(up_in, 16)
                    act.dma_start(R_up[:, 3:5, :], g_up_v[:, :, bass.ds(n * P, P)]).then_inc(up_in, 16)
                    act.wait_ge(rk_turned, n + 1)
                    if not (isinstance(n, int) and n == 0):
                        act.wait_ge(rkv_mixed, n)
                    act.activation(R_zf[:, 0:2, 1:1 + SEQ], pb[:, 0].rearrange("p (j t) -> p j t", t=SEQ), ACT.Copy)
                    act.activation(R_zf[:, 2, 1:1 + SEQ], pb[:, 1, 0:SEQ], ACT.Copy).then_inc(zf_ready, 1)
                elif piece == 1:
                    act.wait_ge(up_done, n + 1)
                    if not (isinstance(n, int) and n == 0):
                        act.wait_ge(ab_ready, n)
                    for j in range(2):
                        act.activation(R_lw[:, j], pb[:, 0, j * SEQ:(j + 1) * SEQ], ACT.Sigmoid,
                                       bias=tab[:, bass.ds(n + (T_W0 + 8 * j), 1)])
                elif piece == 2:
                    act.activation(R_lw[:, 2], pb[:, 1, 0:SEQ], ACT.Sigmoid, bias=tab[:, bass.ds(n + (T_W0 + 16), 1)])
                    act.activation(R_gn[:], pb[:, 1, SEQ:W], ACT.Copy).then_inc(up_act, 1)
                elif piece == 3:
                    act.wait_ge(ss_clamped, n + 1)
                    act.activation(R_sh[:, 1], R_sh[:, 1], ACT.Ln, scale=65536.0)
                    act.drain()
                elif piece == 4:
                    act.activation(R_sh[:, 1], R_sh[:, 1], ACT.Exp, scale=-0.5).then_inc(rn_ready, 1)
                elif piece == 5:
                    act.wait_ge(logs_ready, n + 1)
                    act.activation(R_e1[:], R_b[:], ACT.Exp)
                    act.activation(R_e2[:], R_b[:], ACT.Exp, scale=-1.0)
                else:
                    act.activation(R_lw[:, 0:2], R_lw[:, 0:2], ACT.Exp).then_inc(exps_ready, 1)

            def act_tail(t):
                act.wait_ge(ys_var, t + 1)
                act.activation(small[:, 20:24], small[:, 16:20], ACT.Ln)
                act.drain()
                act.activation(small[:, 24:28], small[:, 20:24], ACT.Exp, scale=-0.5).then_inc(ys_rstd, 1)

            def act_pair(t, more, tail=True):
                if tail:
                    act_tail(t - 1)
                act.wait_ge(pair_done, t + 1)
                act.wait_ge(exps_ready, t + 1)
                act.activation(R_dec[:, 0], R_e1[:, 0].rearrange("p (c n) -> p c n", n=CH)[:, :, CH - 1], ACT.Copy)
                act.activation(R_dec[:, 1], R_e1[:, 1].rearrange("p (c n) -> p c n", n=CH)[:, :, 0], ACT.Copy)
                act.wait_ge(v_turned, t + 1)
                act.wait_ge(init_ready, t + 1)
                for d in range(2):
                    us = slice(d * NCH, (d + 1) * NCH)
                    act.activation(R_UV[CH:P, 0, us], pt[CH:P, 0].rearrange("p (c n) -> p c n", n=P)[:, :, 0:CH], ACT.Copy)
                    ins = act.activation(R_UV[0:CH, 1, us], pt[0:CH, 1].rearrange("p (c n) -> p c n", n=P)[:, :, CH:P],
                                         ACT.Copy)
                ins.then_inc(uv_ready, 1)
                act.wait_ge(ab_turned, t + 1)
                for d in range(2):
                    ins = act.activation(R_ABt[:, d * NCH:(d + 1) * NCH].rearrange("p u c -> p (u c)"), pt[:, d], ACT.Copy)
                ins.then_inc(abt_ready, 1)

                def ahead(lv, point):
                    if more and (lv, point) in ACT_AT:
                        next_act(t + 1, ACT_AT[lv, point])
                for lv in range(1, LEVELS):
                    if lv == 1:
                        act.wait_ge(v_done, t * (LEVELS - 1) + 1)
                        act.activation(flat(R_vc)[0:CH], pt[0:CH, 0], ACT.Copy).then_inc(vc_ready, 1)
                        if tail:
                            act.wait_ge(tail_done, t)
                        act.activation(R_g[:], R_gn[:], ACT.Copy).then_inc(kept_ready, 1)
                        if more:
                            next_act(t + 1, 0)
                    act.wait_ge(q_done, t * (LEVELS - 1) + lv)
                    act.activation(flat(R_qc)[0:CH], py[0:CH, 0], ACT.Copy).then_inc(qc_ready, 1)
                    ahead(lv, 0)
                    if lv < LEVELS - 1:
                        act.wait_ge(v_done, t * (LEVELS - 1) + lv + 1)
                        act.activation(flat(R_vc)[0:CH], pt[0:CH, 0], ACT.Copy).then_inc(vc_ready, 1)
                        ahead(lv, 1)
                    act.wait_ge(w_done, t * (LEVELS - 1) + lv)
                    if lv < LEVELS - 1:
                        act.activation(flat(R_wc)[0:CH], pa[0:CH, 0], ACT.Copy).then_inc(wc_ready, 1)
                    else:
                        act.activation(R_Wbd[0:CH, :, 0:CH], pa[0:CH, 0].rearrange("p (u n) -> p u n", n=CH),
                                       ACT.Copy).then_inc(wbd_ready, 1)
                    ahead(lv, 2)
                for i in range(NCH):
                    u = NCH + NCH - 1 - i
                    act.wait_ge(x_done[1], t * NCH + i + 1)
                    act.activation(R_X[:, 1], pb[:, 1, (u % NCH) * CH:(u % NCH + 1) * CH], ACT.Copy).then_inc(xs_ready[1], 1)
                    act.wait_ge(u_done[1], t * NCH + i + 1)
                    act.activation(R_UV[0:CH, 0, u], py[0:CH, 1, 0:CH], ACT.Copy, scale=-1.0)
                    act.activation(R_UV[CH:P, 1, u], py[CH:P, 1, 0:CH], ACT.Copy, scale=-1.0).then_inc(u_ready[1], 1)
            for piece in range(7):
                next_act(0, piece)
            act_pair(0, True, False)
            with act.Fori(1, PAIRS - 1) as t:
                act_pair(t, True)
            act_pair(PAIRS - 1, False)
            act_tail(PAIRS - 1)
            for i in range(NT):
                act.activation(z[:, i, Z_OG:Z], z[:, i, Z_OG:Z], ACT.Silu).then_inc(og_ready, 1)
            act.wait_ge(tail_done, PAIRS)
            act.wait_ge(gg_turned, 1)
            act.activation(L_gg[0:GLORA], py[0:GLORA, 1, 0:SEQ], ACT.Copy).then_inc(gg_ready, 1)
            with act.Fori(0, GH) as t:
                act.wait_ge(g_turned, t + 1)
                act.activation(L_qk[:].rearrange("p j t -> p (j t)"), pt[:, 0], ACT.Copy).then_inc(g_qk, 1)
                act.wait_ge(g_x, t + 1)
                act.activation(L_t[:], L_t[:], ACT.Exp, scale=-1.0)
                act.drain()
                act.activation(L_t[:], L_t[:], ACT.Ln, bias=1.0).then_inc(g_soft, 1)
                act.wait_ge(g_logs, t + 1)
                act.activation(L_e1[:], L_b[:], ACT.Exp)
                act.activation(L_e2[:], L_b[:], ACT.Exp, scale=-1.0)
                for d in range(2):
                    for c in range(NCH):
                        end = c * CH + (CH - 1 if d == 0 else 0)
                        ins = act.activation(L_e3[:, d, c * CH:(c + 1) * CH], L_b[:, d, c * CH:(c + 1) * CH], ACT.Exp,
                                             scale=-1.0, bias=L_b[:, d, end:end + 1])
                ins.then_inc(g_exps, 1)
                act.wait_ge(g_kdt_done, t + 1)
                act.activation(L_kdt[:].rearrange("p d i n -> p (d i n)"), pt[:, 1], ACT.Copy).then_inc(g_kdt, 1)
                act.wait_ge(g_o, t + 1)
                for i in range(NT):
                    ins = act.activation(L_sq[:, i], pa[:, 1, i * DV:(i + 1) * DV], ACT.Square, accum_out=small[:, 28 + i:29 + i])
                act.drain().then_inc(g_sq, 1)
                act.wait_ge(g_var, t + 1)
                act.activation(small[:, 30:32], small[:, 28:30], ACT.Ln)
                act.drain()
                act.activation(small[:, 32:34], small[:, 30:32], ACT.Exp, scale=-0.5).then_inc(g_rstd, 1)
            act.wait_ge(head_done, 1 + GH)
            split_act(act, 0)
            act.wait_ge(split_lo, 8)
            act.dma_start(xt[:], x_in[0].rearrange("(i p) d -> p i d", p=P)).then_inc(x_in_sem, 16)
            out_act(act, 13, 13)
            end_load(act, 0, 16)
            end_act(act, 0)
            turn_act(act, 1)
            ffn_act(act, C_FFN0, 0, 17)
            end_load(act, 1, C_FFN0 + 32)
            end_act(act, 1)
            turn_act(act, 2)
            in_act(act, C_DIFF, qkv, True)
            act.wait_ge(unit_done, 2 + 4 * C_OUT1)
            act.dma_start(A_lam[0:1, 0:256], diff_lambda.rearrange("a b n -> a (b n)")).then_inc(lam_in, 16)
            act.wait_ge(lam_prod, 1)
            act.activation(A_lam[0:1, 258:260], A_lam[0:1, 256:258], ACT.Exp).then_inc(lam_exp, 1)

            def exps(h, slot, first=False):
                if not first:
                    act.wait_ge(at_pturned, h)
                act.wait_ge(at_bias, h + 1)
                for c in range(2):
                    for i in range(NT):
                        m = 2 * c + i
                        act.activation(A_p[:, slot, c, i], py[:, c, i * SEQ:(i + 1) * SEQ], ACT.Exp, scale=0.125,
                                       bias=A_s[:, slot, 4 + m:5 + m], accum_out=A_s[:, slot, 8 + m:9 + m])
                act.drain().then_inc(at_exp, 1)

            def turned_qk(h, first=False):
                if not first:
                    act.wait_ge(at_scores, h)
                act.wait_ge(at_turned, h + 1)
                act.activation(A_qkT[:].rearrange("p j t -> p (j t)"), pt[:, 0], ACT.Copy).then_inc(at_T, 1)

            def act_head(h, slot, more):
                if more:
                    turned_qk(h + 1)
                act.wait_ge(at_pturned, h + 1)
                act.activation(A_pT[:].rearrange("p k t -> p (k t)"), pt[:, 1], ACT.Copy).then_inc(at_pT, 1)
                if more:
                    exps(h + 1, 1 - slot)
                act.drain()
                act.wait_ge(at_out, h + 1)
                for i in range(NT):
                    if i:
                        act.drain()
                    act.activation(A_sq[:], qkv[:, i, bass.ds(h * P, P)], ACT.Square,
                                   accum_out=A_ss[:, i, bass.ds(h, 1)])
            turned_qk(0, first=True)
            exps(0, 0, first=True)
            heads(act, act_head)
            act.drain().then_inc(at_sq, 1)
            act.wait_ge(at_var, 1)
            act.activation(A_ss[:], A_ss[:], ACT.Ln)
            act.drain()
            act.activation(A_rs[:], A_ss[:], ACT.Exp, scale=-0.5).then_inc(at_rstd, 1)
            for m in range(DH // 2):
                act.wait_ge(at_scaled, m + 1)
                act.activation(hth[:, 2 * m:2 * m + 2], A_t2[:, m % 2], ACT.Copy).then_inc(at_hi, 1)
            out_act(act, C_OUT1, 17 + FG + 12)
            end_load(act, 2, C_OUT1 + 3)
            end_act(act, 2)
            turn_act(act, 3)
            ffn_act(act, C_FFN1, FG, n_of[FG])
            end_load(act, 3, C_FFN1 + 32)
            end_act(act, 3)

        @block.vector
        def _(dve):
            dve.sem_inc(lo_done, 4)
            dve.sem_inc(ada_step, 1)
            dve.wait_ge(tab_copied, 1)
            dve.tensor_scalar(hmu[:], tab[:, T_MU:T_MU + 28], 0.5, None, ALU.mult)
            dve.tensor_scalar(omu[:], tab[:, T_MU:T_MU + 28], -1.0, 1.0, ALU.mult, ALU.add)
            dve.tensor_scalar(neg[:, 0:24], tab[:, T_W0:T_W0 + 24], -1.0, None, ALU.mult)
            dve.tensor_scalar(neg[:, 24:32], tab[:, T_KA:T_KA + 8], -1.0, 1.0, ALU.mult, ALU.add)
            dve.wait_ge(silu_ready, 1)
            for s in range(4):
                cond_unit(dve, 0, s)
            cond_sum(dve, 0, first=True)
            with dve.Fori(1, 8) as j:
                cond_unit(dve, j, 0)
                cond_unit(dve, j, 1)
                cond_store(dve, j - 1)
                cond_unit(dve, j, 2)
                cond_unit(dve, j, 3)
                cond_sum(dve, j)
            cond_store(dve, 7)
            dve.drain()
            turn_dve(dve, 0, 0)
            with dve.Fori(0, 12) as c:
                for s in range(4):
                    low(dve, c, s)
            for s in range(4):
                low(dve, 12, s, LASTW)
            dve.wait_ge(lora_padded, 1)
            pad4 = R_G[:].rearrange("p a b c -> p (a b c)")[:, 0:4 * (SEQ + 2)].rearrange("p (j t) -> p j t", t=SEQ + 2)
            for lo, hi, n in ((0, 2, LORA), (2, 4, P)):
                dve.tensor_tensor(R_lora[0:n, lo:hi], pad4[0:n, lo:hi, 0:SEQ], pad4[0:n, lo:hi, 2:2 + SEQ], ALU.add)
            dve.drain()
            for j in range(4):
                n = LORA if j < 2 else P
                dve.tensor_scalar(R_lora[0:n, j], R_lora[0:n, j], hmu[0:n, 24 + j:25 + j], None, ALU.mult)
            dve.drain()
            for j in range(4):
                n = LORA if j < 2 else P
                ins = dve.scalar_tensor_tensor(R_lora[0:n, j], pad4[0:n, j, 1:1 + SEQ], omu[0:n, 24 + j:25 + j],
                                               R_lora[0:n, j], ALU.mult, ALU.add)
            ins.then_inc(lora_mixed, 1)
            dve.drain().then_inc(lora_ready, 1)
            dve.sem_inc(pair_done, 1)
            top, low_half = slice(0, CH), slice(CH, P)

            def next_dve(n, piece):
                if piece == 0:
                    dve.wait_ge(zf_ready, n + 1)
                    if not (isinstance(n, int) and n == 0):
                        dve.wait_ge(ab_ready, n)
                    dve.tensor_tensor(R_sh[:], R_zf[:, :, 0:SEQ], R_zf[:, :, 2:2 + SEQ], ALU.add)
                    dve.drain()
                    for j in range(3):
                        dve.tensor_scalar(R_sh[:, j], R_sh[:, j], hmu[:, bass.ds(n + 8 * j, 1)], None, ALU.mult)
                    dve.drain()
                elif piece == 1:
                    if not (isinstance(n, int) and n == 0):
                        dve.wait_ge(v_turned, n)
                    for j in range(3):
                        o = R_rk[:, j] if j < 2 else R_vp[:, CH:CH + SEQ]
                        dve.scalar_tensor_tensor(o, R_zf[:, j, 1:1 + SEQ], omu[:, bass.ds(n + 8 * j, 1)], R_sh[:, j],
                                                 ALU.mult, ALU.add)
                    dve.drain().then_inc(rkv_mixed, 1)
                    dve.tensor_scalar(R_kk[:], R_rk[:, 1], tab[:, bass.ds(n + T_KK, 1)], None, ALU.mult)
                    dve.drain()
                    dve.tensor_tensor(R_sh[:, 0], R_kk[:], R_kk[:], ALU.mult).then_inc(sq_ready, 1)
                elif piece == 2:
                    dve.wait_ge(up_act, n + 1)
                    dve.tensor_scalar(R_lw[:, 0:2], R_lw[:, 0:2], -DECAY, None, ALU.mult)
                    dve.drain()
                    reset = cst[:, C_RESET:C_RESET + SEQ]
                    dve.tensor_tensor_scan(R_b[:, 0], reset, R_lw[:, 0], 0.0, ALU.mult, ALU.add)
                    dve.tensor_tensor_scan(R_b[:, 1][:, ::-1], reset, R_lw[:, 1][:, ::-1], 0.0, ALU.mult, ALU.add)
                elif piece == 3:
                    dve.wait_ge(ss_done, n + 1)
                    dve.tensor_scalar(R_sh[:, 1], pb[:, 0, 0:SEQ], 1e-24, None, ALU.max).then_inc(ss_clamped, 1)
                    dve.drain()
                    dve.tensor_tensor(R_lw[:, 0:2], R_b[:], R_lw[:, 0:2], ALU.subtract).then_inc(logs_ready, 1)
                elif piece == 4:
                    dve.tensor_scalar(R_sh[:, 2], R_lw[:, 2], tab[:, bass.ds(n + T_KA, 1)], neg[:, bass.ds(n + 24, 1)],
                                      ALU.mult, ALU.add)
                    dve.drain()
                    dve.tensor_tensor(R_rk[:, 1], R_rk[:, 1], R_sh[:, 2], ALU.mult)
                    dve.wait_ge(rn_ready, n + 1)
                    dve.scalar_tensor_tensor(R_kk[:], R_kk[:], 256.0, R_sh[:, 1], ALU.mult, ALU.mult)
                    dve.drain()
                    dve.tensor_tensor(R_sh[:, 0], R_kk[:], R_lw[:, 2], ALU.mult)
                    dve.scalar_tensor_tensor(R_sh[:, 1], R_rk[:, 0], tab[:, bass.ds(n + T_RK, 1)], R_rk[:, 1],
                                             ALU.mult, ALU.mult)
                    dve.drain().then_inc(q_ready, 1)

            def normed(t):
                cond_store(dve, t * 2 + 9, pb[:, 1, SEQ:SEQ + 4])
                dve.wait_ge(ys_rstd, t + 1)
                for h, r in enumerate((top, low_half)):
                    for c in range(NCH):
                        dve.tensor_scalar(R_Qbd[r, c, h * CH:(h + 1) * CH], R_y[r, c], R_mv[r, c, 0:1], small[r, 24 + c:25 + c],
                                          ALU.subtract, ALU.mult)
                dve.drain().then_inc(ybd_ready, 1)

            def finish(t):
                dve.wait_ge(yt_done, t + 1)
                dve.tensor_scalar(flat(R_y), pb[:, 1, 0:SEQ], tab[:, bass.ds(t + T_GNG, 1)], tab[:, bass.ds(t + T_GNB, 1)],
                                  ALU.mult, ALU.add)
                dve.drain()
                dve.tensor_tensor(flat(R_y), flat(R_y), R_bonus[:], ALU.add)
                dve.drain()
                dve.tensor_tensor(xf[:, bass.ds(t, 1), :], flat(R_y).unsqueeze(1), R_g[:].unsqueeze(1), ALU.mult)
                dve.drain().then_inc(tail_done, 1)

            def dve_pair(t, more, tail=True):
                if tail:
                    normed(t - 1)

                def cond_pair(a, b):
                    for j in range(2):
                        lo, hi = max(a - 17 * j, 0), min(b - 17 * j, 17)
                        cond_steps(dve, t * 2 + (8 + j), lo, min(hi, 16))
                        if lo <= 16 < hi:
                            cond_sum(dve, t * 2 + (8 + j))
                for d in range(2):
                    mask = cst[:, C_SCORE + d * P:C_SCORE + (d + 1) * P].unsqueeze(1).to_broadcast((P, NCH, P))
                    for h, bank in enumerate((py, pa)):
                        k = 2 * d + h
                        cond_pair(S_AT[k], S_AT[k + 1])
                        dve.wait_ge(scores_done, t * 4 + 2 * d + h + 1)
                        dve.tensor_tensor(R_G[:, h, d * NCH:(d + 1) * NCH],
                                          bank[:, d].rearrange("p (c n) -> p c n", n=P), mask, ALU.mult)
                dve.drain().then_inc(g_ready, 1)

                level(dve, 0)
                dve.drain()
                dve.tensor_tensor(R_wc[:], R_C[:, 0], cst[:, C_I2:C_I2 + CH].unsqueeze(1).to_broadcast((P, NU, CH)),
                                  ALU.add).then_inc(first_ready, 1)
                if tail:
                    finish(t - 1)
                dve.wait_ge(bonus_done, t + 1)
                dve.tensor_tensor(R_bonus[:], pb[:, 0, SEQ:W], R_vp[:, CH:CH + SEQ], ALU.mult).then_inc(bonus_out, 1)
                level(dve, 1).then_inc(c1_ready, 1)

                def ahead(lv, point):
                    k = 3 * (lv - 1) + point
                    cond_pair(L_AT[k], L_AT[k + 1])
                    if more and (lv, point) in DVE_AT:
                        next_dve(t + 1, DVE_AT[lv, point])
                for lv in range(1, LEVELS):
                    if lv == 1:
                        dve.wait_ge(v_done, t * (LEVELS - 1) + 1)
                        dve.tensor_copy(flat(R_vc)[low_half], pt[low_half, 1]).then_inc(vc_ready, 1)
                    dve.wait_ge(q_done, t * (LEVELS - 1) + lv)
                    dve.tensor_copy(flat(R_qc)[low_half], py[low_half, 1]).then_inc(qc_ready, 1)
                    ahead(lv, 0)
                    if lv < LEVELS - 1:
                        dve.wait_ge(v_done, t * (LEVELS - 1) + lv + 1)
                        dve.tensor_copy(flat(R_vc)[low_half], pt[low_half, 1]).then_inc(vc_ready, 1)
                        ahead(lv, 1)
                    dve.wait_ge(w_done, t * (LEVELS - 1) + lv)
                    if lv < LEVELS - 1:
                        dve.tensor_copy(flat(R_wc)[low_half], pa[low_half, 1]).then_inc(wc_ready, 1)
                    else:
                        dve.tensor_copy(R_Wbd[CH:P, :, CH:P], pa[CH:P, 1].rearrange("p (u n) -> p u n", n=CH)).then_inc(wbd_ready, 1)
                    ahead(lv, 2)
                dve.wait_ge(kept_ready, t + 1)
                for i in range(NCH):
                    u = i
                    dve.wait_ge(x_done[0], t * NCH + i + 1)
                    dve.tensor_copy(R_X[:, 0], pb[:, 0, u * CH:(u + 1) * CH]).then_inc(xs_ready[0], 1)
                    cond_pair(X_AT[i], X_AT[i + 1])
                    dve.wait_ge(u_done[0], t * NCH + i + 1)
                    dve.tensor_scalar(R_UV[0:CH, 0, u], py[0:CH, 0, 0:CH], -1.0, None, ALU.mult)
                    dve.tensor_scalar(R_UV[CH:P, 1, u], py[CH:P, 0, 0:CH], -1.0, None, ALU.mult).then_inc(u_ready[0], 1)
                    if i == NCH - 1:
                        break
                    for d in range(2):
                        c = i if d == 0 else NCH - 1 - i
                        dve.wait_ge(s_done[d], t * (NCH - 1) + i + 1)
                        decay = R_dec[:, d, c:c + 1]
                        if i:
                            dve.tensor_tensor(R_S[:, d], R_S[:, d], pa[:, d, 0:CH], ALU.add)
                            dve.drain()
                            dve.tensor_scalar(R_S[:, d], R_S[:, d], decay, None, ALU.mult).then_inc(s_ready[d], 1)
                        else:
                            dve.tensor_scalar(R_S[:, d], pa[:, d, 0:CH], decay, None, ALU.mult).then_inc(s_ready[d], 1)
                dve.wait_ge(y_done[0], t + 1)
                dve.wait_ge(y_done[1], t + 1)
                dve.tensor_copy(flat(R_y), pt[:, 0, 0:SEQ]).then_inc(pair_done, 1)
                dve.drain()
                for c in range(NCH):
                    dve.bn_stats(R_st[:, c], R_y[:, c])
                dve.drain()
                for c in range(NCH):
                    dve.bn_aggr(R_mv[:, c], R_st[:, c])
                dve.drain()
                dve.tensor_scalar(small[:, 16:20], R_mv[:, :, 1], GN_EPS, None, ALU.add).then_inc(ys_var, 1)
                cond_store(dve, t * 2 + 8, pb[:, 1, SEQ:SEQ + 4])
                cond_pair(X_AT[NCH], 34)
            for piece in range(5):
                next_dve(0, piece)
            dve_pair(0, True, False)
            with dve.Fori(1, PAIRS - 1) as t:
                dve_pair(t, True)
            dve_pair(PAIRS - 1, False)
            normed(PAIRS - 1)
            finish(PAIRS - 1)
            dve.sem_inc(head_done, 1)
            dve.wait_ge(og_ready, 2)
            with dve.Fori(0, GH) as t:
                dve.wait_ge(g_gate, t + 1)
                for d in range(2):
                    dve.tensor_scalar(L_x[:, d], pa[:, 0, d * SEQ:(d + 1) * SEQ], tab[:, bass.ds(t + T_GB + d * GH, 1)], None, ALU.add)
                dve.drain()
                xx, tt = (v[:].rearrange("p d t -> p (d t)") for v in (L_x, L_t))
                dve.scalar_tensor_tensor(tt, xx, -1.0, xx, ALU.mult, ALU.max).then_inc(g_x, 1)
                dve.drain()
                dve.tensor_scalar(xx, xx, 0.0, 1.0 / 16, ALU.min, ALU.mult)
                dve.drain()
                dve.wait_ge(g_soft, t + 1)
                dve.scalar_tensor_tensor(xx, tt, -1.0 / 16, xx, ALU.mult, ALU.add)
                dve.drain()
                reset = cst[:, C_RESET:C_RESET + SEQ]
                dve.tensor_tensor_scan(L_b[:, 0], reset, L_x[:, 0], 0.0, ALU.mult, ALU.add)
                dve.tensor_tensor_scan(L_b[:, 1][:, ::-1], reset, L_x[:, 1][:, ::-1], 0.0, ALU.mult, ALU.add).then_inc(g_logs, 1)
                dve.wait_ge(g_qk, t + 1)
                dve.wait_ge(g_exps, t + 1)
                for d in range(2):
                    dve.scalar_tensor_tensor(L_qb[:, d], L_qk[:, 0], float(DK) ** -0.5, L_e1[:, d], ALU.mult, ALU.mult)
                kk2 = L_qk[:, 1:2].to_broadcast((P, 2, SEQ))
                dve.tensor_tensor(L_kb[:], kk2, L_e2[:], ALU.mult)
                dve.tensor_tensor(L_kd[:], kk2, L_e3[:], ALU.mult).then_inc(g_prod, 1)
                dve.wait_ge(g_att, t + 1)
                for d in range(2):
                    ins = dve.scalar_tensor_tensor(
                        L_att[:, d], pb[:, 0, d * SEQ:(d + 1) * SEQ].rearrange("p (i n) -> p i n", n=P), 3e38,
                        cst[:, C_GLA + d * P:C_GLA + (d + 1) * P].unsqueeze(1).to_broadcast((P, NT, P)), ALU.min, ALU.mult)
                ins.then_inc(g_attm, 1)
                dve.wait_ge(g_kv, t + 1)
                place = {(0, 0): py[:, 0, 0:DV], (0, 1): py[:, 1, 0:DV], (0, 2): py[:, 0, DV:2 * DV],
                         (1, 3): py[:, 1, DV:2 * DV], (1, 2): pa[:, 0, 0:DV], (1, 1): pb[:, 1, 0:DV]}
                for i in range(NCH - 1):
                    for d in range(2):
                        c = i if d == 0 else NCH - 1 - i
                        end = c * CH + (CH - 1 if d == 0 else 0)
                        if i == 0:
                            ins = dve.tensor_copy(L_S[:, d, 0], place[d, c])
                        else:
                            ins = dve.scalar_tensor_tensor(L_S[:, d, i], L_S[:, d, i - 1], L_e1[:, d, end:end + 1],
                                                           place[d, c], ALU.mult, ALU.add)
                    dve.drain()
                dve.drain().then_inc(g_states, 1)
                dve.wait_ge(g_sq, t + 1)
                dve.tensor_scalar(small[:, 28:30], small[:, 28:30], 1.0 / DV, EPS, ALU.mult, ALU.add).then_inc(g_var, 1)
                dve.wait_ge(g_rstd, t + 1)
                for i in range(NT):
                    ins = dve.scalar_tensor_tensor(L_o[:, i], pa[:, 1, i * DV:(i + 1) * DV], small[:, 32 + i:33 + i],
                                                   z[:, i, bass.ds(t * DV + Z_OG, DV)], ALU.mult, ALU.mult)
                ins.then_inc(g_on, 1)
                dve.wait_ge(g_oT, t + 1)
                for j in range(2):
                    dve.tensor_scalar(xf[:, bass.ds(t * 2 + 8 + j, 1), :], pt[:, 0:1, j * SEQ:(j + 1) * SEQ],
                                      tab[:, T_NG + j:T_NG + j + 1], None, ALU.mult)
                dve.drain().then_inc(head_done, 1)
            split_dve(dve, 0)
            out_dve(dve, 13)
            dve.wait_ge(pa_free, 2 + 2 * 17)
            dve.wait_ge(x_in_sem, 32)
            end_dve(dve, 0)
            turn_dve(dve, 1, 1)
            ffn_dve(dve, C_FFN0, 0, 0, 24)
            end_dve(dve, 1)
            turn_dve(dve, 2, 2)
            for t in range(2):
                for s in range(4):
                    low(dve, t + C_DIFF, s)
                    cond_unit(dve, t + 46, s)
                    if t and s == 1:
                        cond_store(dve, 46)
                cond_sum(dve, t + 46)
            low(dve, 2 + C_DIFF, 0)
            cond_store(dve, 47)
            for s in range(1, 4):
                low(dve, 2 + C_DIFF, s)
            with dve.Fori(3, 12) as t:
                for s in range(4):
                    low(dve, t + C_DIFF, s)
            dve.wait_ge(lam_in, 16)
            lam4 = A_lam[0:1, 0:256].rearrange("p (a b n) -> p a b n", a=2, b=2)
            dve.tensor_tensor(lam4[:, :, 0], lam4[:, :, 0], lam4[:, :, 1], ALU.mult)
            dve.drain()
            dve.tensor_reduce(A_lam[0:1, 256:258], lam4[:, :, 0], AX_X, ALU.add).then_inc(lam_prod, 1)
            dve.wait_ge(lam_exp, 1)
            dve.tensor_tensor(A_lam[0:1, 260:261], A_lam[0:1, 259:260], A_lam[0:1, 258:259], ALU.subtract)
            dve.drain()
            dve.tensor_scalar(A_lam[0:1, 261:262], A_lam[0:1, 260:261], LAMBDA_INIT, None, ALU.subtract)
            dve.drain().then_inc(lam_prod, 1)
            dve.wait_ge(lam_mm, 1)
            dve.tensor_copy(small[:, 74:75], pb[:, 1, 0:1])
            dve.tensor_scalar(small[:, 75:76], tab[:, T_SUB:T_SUB + 1], 1.0 - LAMBDA_INIT, None, ALU.mult)
            dve.drain()
            dve.wait_ge(pa_free, 2 + 2 * (17 + FG + 12))

            def maxima(h, slot):
                dve.wait_ge(at_scores, h + 1)
                for c in range(2):
                    dve.tensor_reduce(A_s[:, slot, 2 * c:2 * c + 2], py[:, c].rearrange("p (i k) -> p i k", k=SEQ), AX_X, ALU.max)
                dve.drain()
                dve.tensor_scalar(A_s[:, slot, 4:8], A_s[:, slot, 0:4], -0.125, None, ALU.mult).then_inc(at_bias, 1)

            def dve_head(h, slot, more):
                dve.wait_ge(at_exp, h + 1)
                dve.reciprocal(A_s[:, slot, 8:12], A_s[:, slot, 8:12])
                dve.drain()
                dve.tensor_scalar(A_s[:, slot, 10:12], A_s[:, slot, 10:12], small[:, 74:75], None, ALU.mult)
                for i in range(NT):
                    dve.tensor_scalar(A_p[:, slot, 0, i], A_p[:, slot, 0, i], A_s[:, slot, 8 + i:9 + i], None, ALU.mult)
                dve.drain()
                for i in range(NT):
                    ins = dve.scalar_tensor_tensor(A_p[:, slot, 0, i], A_p[:, slot, 1, i], A_s[:, slot, 10 + i:11 + i],
                                                   A_p[:, slot, 0, i], ALU.mult, ALU.add)
                ins.then_inc(at_p, 1)
                if more:
                    maxima(h + 1, 1 - slot)
                dve.wait_ge(at_o, h + 1)
                dve.tensor_copy(qkv[:, :, bass.ds(h * P, P)], pa[:, 0, 0:NT * P].rearrange("p (i n) -> p i n", n=P)).then_inc(at_out, 1)
            maxima(0, 0)
            heads(dve, dve_head)
            dve.wait_ge(at_sq, 1)
            dve.tensor_scalar(A_ss[:], A_ss[:], 1.0 / P, EPS, ALU.mult, ALU.add).then_inc(at_var, 1)
            dve.wait_ge(at_rstd, 1)

            def normed(m):
                if m >= 2:
                    dve.wait_ge(at_oT, m - 1)
                for h in range(2):
                    for i in range(NT):
                        ins = dve.tensor_scalar(A_on[:, m % 2, i, h * P:(h + 1) * P], qkv[:, i, (2 * m + h) * P:(2 * m + h + 1) * P],
                                                A_rs[:, i, 2 * m + h:2 * m + h + 1], None, ALU.mult)
                ins.then_inc(at_on, 1)

            def lower(m):
                dve.wait_ge(at_hi, m + 1)
                dve.tensor_tensor(htl[:, 2 * m:2 * m + 2], A_t2[:, m % 2], hth[:, 2 * m:2 * m + 2].bitcast(F32),
                                  ALU.subtract).then_inc(at_done, 1)
            normed(0)
            for m in range(DH // 2):
                if m + 1 < DH // 2:
                    normed(m + 1)
                dve.wait_ge(at_oT, m + 1)
                if m >= 2:
                    dve.wait_ge(at_done, m - 1)
                dve.tensor_scalar(A_t2[:, m % 2].rearrange("p h t -> p (h t)"), pb[:, m % 2], small[:, 75:76], None,
                                  ALU.mult).then_inc(at_scaled, 1)
                if m:
                    lower(m - 1)
            lower(DH // 2 - 1)
            dve.drain()
            dve.wait_ge(at_done, DH // 2)
            out_dve(dve, C_OUT1)
            dve.wait_ge(pa_free, 2 + 2 * (17 + FG + 16))
            end_dve(dve, 2)
            turn_dve(dve, 3, 3)
            ffn_dve(dve, C_FFN1, FG, 44)
            end_dve(dve, 3)

        @block.tensor
        def _(pe):
            pe.sem_inc(unit_done, 2)
            pe.sem_inc(pa_free, 2)
            pe.wait_ge(const_in, 16)
            pe.wait_ge(rows_in, 16 * len(list(vectors())))
            for i in range(4):
                n = TABS[i + 1] - TABS[i]
                mm = pe.transpose(pa[:, 0, TABS[i]:TABS[i + 1]], rows[0:n, i, :], ident[0:n, 0:n])
            mm.then_inc(tab_turned, 1)
            cond_cols(pe, 0, first=True)
            with pe.Fori(1, 8) as j:
                cond_cols(pe, j)
            pe.wait_ge(x_in_sem, 16)
            turn_pe(pe, 0)
            pe.wait_ge(h_lo, 8)
            with pe.Fori(0, 12) as c:
                project(pe, c, c, (hth, htl), pa_done, pa_free, pa)
            project(pe, 12, 12, (hth, htl), pa_done, pa_free, pa, LASTW)
            pe.wait_ge(pa_free, 2 + 2 * ABC)
            for j, (a, b) in enumerate(((Z_WD, Z_AD), (Z_AD, Z_GD), (Z_GD, Z_GD + P), (Z_GD + P, Z_Q))):
                for i in range(NT):
                    at = (j % 2) * SEQ + i * P
                    mm = pe.transpose(py[0:b - a, j // 2, at:at + P], z[:, i, a:b], ident)
            mm.then_inc(lora_turned, 1)
            pe.wait_ge(lora_ready, 3)
            def next_pe(n, piece):
                if piece == 0:
                    pe.wait_ge(zs_ready, n + 1)
                    if not (isinstance(n, int) and n == 0):
                        pe.wait_ge(bonus_out, n)
                    for j in range(3):
                        for i in range(NT):
                            at = (j % 2) * SEQ + i * P
                            mm = pe.transpose(pb[:, j // 2, at:at + P], R_zs[:, i, j], ident)
                    mm.then_inc(rk_turned, 1)
                elif piece == 1:
                    pe.wait_ge(up_in, n * 48 + 48)
                    pe.wait_ge(zf_ready, n + 1)
                    for j in range(3):
                        lora = R_lora[0:LORA, 0 if j < 2 else 1]
                        pe.matmul(pb[:, j // 2, (j % 2) * SEQ:(j % 2 + 1) * SEQ], R_up[0:LORA, j], lora, start=True, stop=True)
                    for j in range(2):
                        mm = pe.matmul(pb[:, 1, SEQ:W], R_up[:, 3 + j], R_lora[:, 2 + j], start=(j == 0), stop=(j == 1))
                    mm.then_inc(up_done, 1)
                else:
                    pe.wait_ge(sq_ready, n + 1)
                    pe.wait_ge(up_act, n + 1)
                    pe.matmul(pb[:, 0, 0:SEQ], heads1, R_sh[:, 0], start=True, stop=True).then_inc(ss_done, 1)

            def pe_cols(t):
                cond_cols(pe, t * 2 + 9, bank=pb[:, 1, SEQ:SEQ + 4])

            def pe_tail(t):
                pe.wait_ge(ybd_ready, t + 1)
                for c in range(NCH):
                    mm = pe.matmul(pb[:, 1, c * CH:(c + 1) * CH], R_Qbd[:, c], cst[:, C_I2:C_I2 + CH], start=True, stop=True)
                mm.then_inc(yt_done, 1)

            def pe_pair(t, more, tail=True):
                pe.wait_ge(pair_done, t + 1)
                pe.wait_ge(rkv_mixed, t + 1)
                for h in range(2):
                    for c in range(NCH):
                        mm = pe.transpose(pt[:, h, c * P:(c + 1) * P], R_vp[:, (c + h) * CH:(c + h) * CH + P], ident)
                mm.then_inc(v_turned, 1)
                pe.wait_ge(q_ready, t + 1)
                pe.wait_ge(ss_clamped, t + 1)
                pe.matmul(pb[:, 0, SEQ:W], heads1, R_sh[:, 1], start=True, stop=True).then_inc(bonus_done, 1)
                if tail:
                    pe_cols(t - 1)
                pe.wait_ge(ab_ready, t + 1)
                for d in range(2):
                    for h, bank in enumerate((py, pa)):
                        half = slice(h * CH, (h + 1) * CH)
                        for c in range(NCH):
                            u = d * NCH + c
                            mm = pe.matmul(bank[:, d, c * P:(c + 1) * P], R_AB[half, u], R_KR[half, u], start=True, stop=True)
                        mm.then_inc(scores_done, 1)
                if tail:
                    pe_tail(t - 1)
                pe.wait_ge(uv_ready, t + 1)
                for u in range(NU):
                    mm = pe.transpose(pt[:, u // NCH, (u % NCH) * P:(u % NCH + 1) * P], R_AB[:, u], ident)
                mm.then_inc(ab_turned, 1)
                def products(bank, lhs, rhs, start):
                    pe.sem_inc(pe_passed, 1)
                    for u in range(NU):
                        for h in range(2):
                            r = slice(h * CH, (h + 1) * CH)
                            mm = pe.matmul(bank[r, h, u * CH:(u + 1) * CH], lhs(u)[r], rhs(u)[r],
                                           start=(start or (start is None and u == 0)), stop=True,
                                           skip_group_check=True)
                    return mm

                def unit_of(tile):
                    return lambda u: tile[:, u]
                eye = cst[:, C_I2:C_I2 + CH]
                pe.wait_ge(first_ready, t + 1)
                pe.wait_ge(abt_ready, t + 1)
                products(pt, unit_of(R_wc), lambda u: eye, None).then_inc(v_done, 1)
                products(pa, lambda u: eye, unit_of(R_wc), None)
                if more:
                    if tail:
                        pe.wait_ge(tail_done, t)
                    next_pe(t + 1, 0)
                for lv in range(1, LEVELS):
                    done = t * (LEVELS - 1) + lv
                    pe.wait_ge(c1_ready if lv == 1 else c_ready, t + 1 if lv == 1 else t * (LEVELS - 2) + lv - 1)
                    pe.wait_ge(vc_ready, 2 * done)
                    products(py, unit_of(R_C[:, lv % 2]), unit_of(R_vc), True).then_inc(q_done, 1)
                    if lv > 1:
                        pe.wait_ge(wc_ready, t * 2 * (LEVELS - 2) + 2 * (lv - 1))
                    pe.wait_ge(qc_ready, 2 * done)
                    if lv < LEVELS - 1:
                        products(pt, unit_of(R_wc), unit_of(R_qc), False).then_inc(v_done, 1)
                    products(pa, unit_of(R_qc), unit_of(R_wc), False).then_inc(w_done, 1)
                    if more and lv in PE_AT:
                        next_pe(t + 1, PE_AT[lv])
                pe.wait_ge(wbd_ready, (t + 1) * 2)
                pe.wait_ge(krbd_ready, t + 1)
                pe.wait_ge(abt_ready, t + 1)
                if more:
                    pe.wait_ge(ss_clamped, t + 2)
                for i in range(NCH):
                    for d in range(2):
                        c = i if d == 0 else NCH - 1 - i
                        u = d * NCH + c
                        for h in range(2):
                            mm = pe.matmul(pb[h * CH:(h + 1) * CH, d, c * CH:(c + 1) * CH], R_G[:, h, u, 0:CH],
                                           R_UV[:, h, u], start=(i == 0), stop=True, skip_group_check=True)
                        if i == 0:
                            mm.then_inc(x_done[d], 1)
                    for d in range(2):
                        c = i if d == 0 else NCH - 1 - i
                        u = d * NCH + c
                        if i:
                            pe.wait_ge(s_ready[d], t * (NCH - 1) + i)
                            pe.matmul(pb[:, d, c * CH:(c + 1) * CH], R_Kbd[:, u], R_S[:, d], start=False, stop=True,
                                      skip_group_check=True).then_inc(x_done[d], 1)
                    for d in range(2):
                        c = i if d == 0 else NCH - 1 - i
                        u = d * NCH + c
                        pe.wait_ge(xs_ready[d], t * NCH + i + 1)
                        pe.matmul(py[:, d, 0:CH], R_Wbd[:, u], R_X[:, d], start=True, stop=True).then_inc(u_done[d], 1)
                    for d in range(2):
                        c = i if d == 0 else NCH - 1 - i
                        u = d * NCH + c
                        pe.wait_ge(u_ready[d], t * NCH + i + 1)
                        if i < NCH - 1:
                            for h in range(2):
                                mm = pe.matmul(pa[h * CH:(h + 1) * CH, d, 0:CH], R_ABt[:, u, h * CH:(h + 1) * CH],
                                               R_UV[:, h, u], start=True, stop=True)
                        at = slice(c * CH, (c + 1) * CH)
                        for h in range(2):
                            mm = pe.matmul(pt[h * CH:(h + 1) * CH, 0, at], R_G[:, h, u, CH:P], R_UV[:, h, u],
                                           start=(i == 0 and d == 0), stop=True, skip_group_check=True)
                        if i:
                            mm = pe.matmul(pt[:, 0, at], R_Rbd[:, u], R_S[:, d], start=False, stop=True,
                                           skip_group_check=True)
                        mm.then_inc(y_done[d] if i == NCH - 1 else s_done[d], 1)
                cond_cols(pe, t * 2 + 8, bank=pb[:, 1, SEQ:SEQ + 4])
            for piece in range(3):
                next_pe(0, piece)
            pe_pair(0, True, False)
            with pe.Fori(1, PAIRS - 1) as t:
                pe_pair(t, True)
            pe_pair(PAIRS - 1, False)
            pe_cols(PAIRS - 1)
            pe_tail(PAIRS - 1)
            pe.wait_ge(tail_done, PAIRS)
            for i in range(NT):
                mm = pe.transpose(py[0:GLORA, 1, i * P:(i + 1) * P], z[:, i, Z_GG:Z_OG], ident)
            mm.then_inc(gg_turned, 1)
            pe.wait_ge(gg_ready, 1)
            with pe.Fori(0, GH) as t:
                pe.wait_ge(head_done, t + 1)
                pe.wait_ge(gz_ready, t + 1)
                for j in range(2):
                    for i in range(NT):
                        mm = pe.transpose(pt[:, 0, j * SEQ + i * P:j * SEQ + (i + 1) * P], L_zs[:, i, j], ident)
                mm.then_inc(g_turned, 1)
                pe.wait_ge(gla_in, t * 16 + 16)
                for d in range(2):
                    mm = pe.matmul(pa[:, 0, d * SEQ:(d + 1) * SEQ], L_up[0:GLORA, d], L_gg[0:GLORA], start=True, stop=True)
                mm.then_inc(g_gate, 1)
                pe.wait_ge(g_prod, t + 1)
                for d in range(2):
                    for i in range(NT):
                        ts_ = slice(i * P, (i + 1) * P)
                        mm = pe.matmul(pb[:, 0, (d * NT + i) * P:(d * NT + i + 1) * P], L_kb[:, d, ts_], L_qb[:, d, ts_],
                                       start=True, stop=True)
                mm.then_inc(g_att, 1)
                for d in range(2):
                    for i in range(NT):
                        mm = pe.transpose(pt[:, 1, (d * NT + i) * P:(d * NT + i + 1) * P], L_kd[:, d, i * P:(i + 1) * P], ident)
                mm.then_inc(g_kdt_done, 1)
                pe.wait_ge(g_kdt, t + 1)
                place = {(0, 0): py[:, 0, 0:DV], (0, 1): py[:, 1, 0:DV], (0, 2): py[:, 0, DV:2 * DV],
                         (1, 3): py[:, 1, DV:2 * DV], (1, 2): pa[:, 0, 0:DV], (1, 1): pb[:, 1, 0:DV]}
                for (d, c), bank in place.items():
                    r = slice(c % 2 * CH, c % 2 * CH + CH)
                    mm = pe.matmul(bank, L_kdt[r, d, c // 2], L_v[r, c // 2], start=True, stop=True)
                mm.then_inc(g_kv, 1)
                pe.wait_ge(g_attm, t + 1)
                for i in range(NT):
                    for d in range(2):
                        pe.matmul(pa[:, 1, i * DV:(i + 1) * DV], L_att[:, d, i], L_v[:, i], start=(i == 0 and d == 0),
                                  stop=True, skip_group_check=True)
                pe.wait_ge(g_states, t + 1)
                for d in range(2):
                    for i in range(1, NCH):
                        c = i if d == 0 else NCH - 1 - i
                        mm = pe.matmul(pa[c % 2 * CH:c % 2 * CH + CH, 1, c // 2 * DV:c // 2 * DV + DV],
                                       L_qb[:, d, c * CH:(c + 1) * CH], L_S[:, d, i - 1], start=False, stop=True,
                                       skip_group_check=True)
                mm.then_inc(g_o, 1)
                pe.wait_ge(g_on, t + 1)
                for j in range(2):
                    for i in range(NT):
                        mm = pe.transpose(pt[:, 0, j * SEQ + i * P:j * SEQ + (i + 1) * P], L_o[:, i, j * P:(j + 1) * P], ident)
                mm.then_inc(g_oT, 1)
            pe.wait_ge(split_lo, 8)
            out_pe(pe, 13, 13)
            end_pe(pe, 0)
            pe.sem_inc(pb_free, 2)
            pe.sem_inc(py_free, 2)
            turn_pe_at(pe, 1)
            ffn_pe(pe, C_FFN0, 0, 0, 24)
            end_pe(pe, 1)
            turn_pe_at(pe, 2)
            for t in range(2):
                project(pe, t + C_DIFF, t + (17 + FG), (hth, htl), pa_done, pa_free, pa)
                cond_cols(pe, t + 46)
            with pe.Fori(2, 12) as t:
                project(pe, t + C_DIFF, t + (17 + FG), (hth, htl), pa_done, pa_free, pa)
            pe.wait_ge(lam_prod, 2)
            pe.matmul(pb[:, 1, 0:1], ones[0:1, :], A_lam[0:1, 261:262], start=True, stop=True).then_inc(lam_mm, 1)

            def turn_qk(h, slot, first=False):
                if not first:
                    pe.wait_ge(at_T, h)
                pe.wait_ge(at_rot, h + 1)
                for j in range(2):
                    for i in range(NT):
                        mm = pe.transpose(pt[:, 0, j * SEQ + i * P:j * SEQ + (i + 1) * P],
                                          A_qk[:, slot, i, j].rearrange("p c f -> p (c f)"), ident)
                mm.then_inc(at_turned, 1)

            def scores(h, first=False):
                if not first:
                    pe.wait_ge(at_exp, h)
                pe.wait_ge(at_T, h + 1)
                pe.sem_inc(pe_passed, 1)
                for c in range(2):
                    r = slice(c * 64, c * 64 + 64)
                    for i in range(NT):
                        mm = pe.matmul(py[:, c, i * SEQ:(i + 1) * SEQ], A_qkT[r, 0, i * P:(i + 1) * P], A_qkT[r, 1],
                                       start=True, stop=True)
                mm.then_inc(at_scores, 1)

            def pe_head(h, slot, more):
                if more:
                    turn_qk(h + 1, 1 - slot)
                pe.wait_ge(at_p, h + 1)
                for k in range(NT):
                    for i in range(NT):
                        mm = pe.transpose(pt[:, 1, k * SEQ + i * P:k * SEQ + (i + 1) * P],
                                          A_p[:, slot, 0, i, k * P:(k + 1) * P], ident)
                mm.then_inc(at_pturned, 1)
                if more:
                    scores(h + 1)
                pe.wait_ge(at_pT, h + 1)
                for i in range(NT):
                    for k in range(NT):
                        mm = pe.matmul(pa[:, 0, i * P:(i + 1) * P], A_pT[:, k, i * P:(i + 1) * P],
                                       qkv[:, k, bass.ds(h * P + 2 * D, P)], start=(k == 0), stop=(k == NT - 1))
                mm.then_inc(at_o, 1)
            turn_qk(0, 0, first=True)
            scores(0, first=True)
            heads(pe, pe_head)
            for m in range(DH // 2):
                pe.wait_ge(at_on, m + 1)
                if m >= 2:
                    pe.wait_ge(at_scaled, m - 1)
                for h in range(2):
                    for i in range(NT):
                        mm = pe.transpose(pb[:, m % 2, h * SEQ + i * P:h * SEQ + (i + 1) * P],
                                          A_on[:, m % 2, i, h * P:(h + 1) * P], ident)
                mm.then_inc(at_oT, 1)
            pe.wait_ge(at_done, DH // 2)
            out_pe(pe, C_OUT1, 17 + FG + 12)
            end_pe(pe, 2)
            turn_pe_at(pe, 3)
            ffn_pe(pe, C_FFN1, FG, 44)
            end_pe(pe, 3)


INPUTS = ["x", "c", "ada_w", "ada_b", "ln_g", "ln_b", "ffn_w_in", "ffn_w_out", "ab_w_in", "ab_w_out",
          "rwkv_mu", "rwkv_w0", "rwkv_w_up", "rwkv_a0", "rwkv_a_up", "rwkv_g_up", "rwkv_k_k", "rwkv_k_a",
          "rwkv_r_k", "rwkv_gn_g", "rwkv_gn_b", "gla_gate_up", "gla_gate_b", "gla_norm_g",
          "diff_w_in", "diff_w_out", "diff_lambda", "diff_subln_g"]


def kernel(**inputs):
    import concourse.bacc as bacc
    from concourse.bass_utils import run_bass_kernel_spmd

    nc = bacc.Bacc("TRN2", target_bir_lowering=False, num_devices=1)
    arrays, args = {}, []
    for name in INPUTS:
        a = np.ascontiguousarray(inputs[name])
        arrays[f"in_{name}"] = a
        args.append(nc.dram_tensor(f"in_{name}", a.shape, mybir.dt.from_np(a.dtype), kind="ExternalInput").ap())
    arrays["in_constants"] = constants()
    args.append(nc.dram_tensor("in_constants", (P, C_N), F32, kind="ExternalInput").ap())
    out = nc.dram_tensor("out_0", (1, SEQ, D), F32, kind="ExternalOutput").ap()
    build_trunk(nc, *args, out)
    r = run_bass_kernel_spmd(nc, [arrays], core_ids=[0])
    return r.results[0]["out_0"]
```

```python
from contextlib import ExitStack

import numpy as np

import concourse.bass as bass
from concourse import mybir

ALU = mybir.AluOpType
ACT = mybir.ActivationFunctionType
F32 = mybir.dt.float32
F32R = mybir.dt.float32r
AX_X = mybir.AxisListType.X

P = 128
D = 2048
SEQ = 256
NT = SEQ // P
KT = D // P
W = 512
UK = 4
D_FF = 5632
FG = D_FF // W
HN = 64
RW = D // 2
PAIRS = RW // P
LORA = 96
GATE = 256
Z_WD = 3 * RW
Z_AD = Z_WD + LORA
Z_GD = Z_AD + LORA
Z_Q = Z_GD + GATE
GH = 4
DK = 128
DV = 256
Z_K = Z_Q + GH * DK
Z_V = Z_K + GH * DK
Z_GG = Z_V + GH * DV
GLORA = 16
Z_OG = Z_GG + GLORA
Z = Z_OG + GH * DV
ABC = -(-Z // W)
CH = 64
NCH = SEQ // CH
NU = 2 * NCH
LEVELS = 6
DH = 16
ALPHA = (2.0 * 2) ** 0.25
DECAY = 0.606531
LAMBDA_INIT = 0.8 - 0.6 * float(np.exp(-0.3))
EPS = 1e-5
GN_EPS = 64e-5

T_LN_G, T_LN_B = 0, 64
T_MU, T_W0, T_A0, T_KK, T_KA, T_RK, T_GNG, T_GNB = 128, 156, 172, 180, 188, 196, 204, 212
T_GB, T_NG, T_SUB, T_C = 220, 228, 230, 231
T_ADA = 247
T_N = T_ADA + 192
TABS = (0, 128, 247, 343, 439)

C_ID, C_ONES, C_HEADS, C_SCORE, C_GLA, C_LEVEL, C_RESET, C_COS, C_SIN = (
    0, 128, 256, 384, 640, 896, 896 + 2 * LEVELS * CH, 896 + 2 * LEVELS * CH + SEQ, 896 + 2 * LEVELS * CH + SEQ + 64)
C_I2 = C_SIN + 64
C_N = C_I2 + CH


def constants():
    c = np.zeros((P, C_N), np.float32)
    p = np.arange(P)
    c[:, C_ID:C_ID + P] = np.eye(P)
    c[:, C_ONES:C_ONES + P] = 1.0
    c[:, C_HEADS:C_HEADS + P] = (p[:, None] // HN == p[None, :] // HN)
    s, t = (p % CH)[:, None], np.arange(CH)[None, :]
    c[:, C_SCORE:C_SCORE + P] = np.concatenate([s < t, s <= t], 1)
    c[:, C_SCORE + P:C_SCORE + 2 * P] = np.concatenate([s > t, s >= t], 1)
    same = p[:, None] // CH == p[None, :] // CH
    c[:, C_GLA:C_GLA + P] = same & (p[:, None] <= p[None, :])
    c[:, C_GLA + P:C_GLA + 2 * P] = same & (p[:, None] >= p[None, :])
    for d in range(2):
        for lv in range(LEVELS):
            b = 1 << lv
            row, col = (p % CH)[:, None], np.arange(CH)[None, :]
            if d:
                row, col = CH - 1 - row, CH - 1 - col
            m = (row // (2 * b) == col // (2 * b)) & (row // b % 2 == 0) & (col // b % 2 == 1)
            at = C_LEVEL + (d * LEVELS + lv) * CH
            c[:, at:at + CH] = -1.0 * m
    c[:, C_RESET:C_RESET + SEQ] = (np.arange(SEQ) % CH != 0)
    inv = (10000.0 ** (-np.arange(0, 64, 2, dtype=np.float32) / 64)).astype(np.float32)
    for i in range(NT):
        ang = ((i * P + p).astype(np.float32)[:, None] * inv[None, :]).astype(np.float32)
        c[:, C_COS + 32 * i:C_COS + 32 * i + 32] = np.cos(ang)
        c[:, C_SIN + 32 * i:C_SIN + 32 * i + 32] = np.sin(ang)
    c[:, C_I2:C_I2 + CH] = np.eye(CH)[np.arange(P) % CH]
    return c


def build_trunk(nc, x_in, c_in, ada_w, ada_b, ln_g, ln_b, ffn_w_in, ffn_w_out, ab_w_in, ab_w_out,
                rwkv_mu, rwkv_w0, rwkv_w_up, rwkv_a0, rwkv_a_up, rwkv_g_up, rwkv_k_k, rwkv_k_a,
                rwkv_r_k, rwkv_gn_g, rwkv_gn_b, gla_gate_up, gla_gate_b, gla_norm_g,
                diff_w_in, diff_w_out, diff_lambda, diff_subln_g, consts, out):
    with ExitStack() as ctx:
        def sb(name, shape, dt=F32, stack=ctx):
            return stack.enter_context(nc.sbuf_tensor("s_" + name, shape, dt))

        def sem(name):
            return ctx.enter_context(nc.semaphore(name))

        cst = sb("cst", [P, C_N])
        tab = sb("tab", [P, T_N])
        ada = sb("ada", [P, 4, 48])
        silu_c = sb("silu_c", [P, KT])
        hmu = sb("hmu", [P, 28])
        omu = sb("omu", [P, 28])
        neg = sb("neg", [P, 32])
        small = sb("small", [P, 96])
        raw = sb("raw", [P, 4, UK, W])
        adaw = sb("adaw", [P, 2, UK, W])
        acc = sb("acc", [P, 2, W])
        asum = sb("asum", [P, W])
        xt = sb("xt", [P, NT, D])
        xf = xt[:].rearrange("p a d -> p (a d)").rearrange("p (k t) -> p k t", t=SEQ)

        r1 = ExitStack()
        z = sb("z", [P, NT, Z], stack=r1)
        r1.close()
        r1 = ExitStack()
        qkv = sb("qkv", [P, NT, 3 * D], stack=r1)
        r1.close()
        r1 = ExitStack()
        ysum = sb("ysum", [P, NT, D], stack=r1)
        gu = sb("gu", [P, NT, W], stack=r1)
        guh = sb("guh", [P, UK, SEQ], F32R, stack=r1)
        gul = sb("gul", [P, UK, SEQ], F32R, stack=r1)
        lng = sb("lng", [P, D], stack=r1)
        lnb = sb("lnb", [P, D], stack=r1)
        gate_bc = sb("gate_bc", [P, D], stack=r1)
        r1.close()
        hold = sb("hold", [P, max(NT * Z, NT * D + NT * W + 2 * UK * SEQ + 3 * D)])

        r2 = ExitStack()
        wh = sb("wh", [P, 2, UK, W], F32R, stack=r2)
        wl = sb("wl", [P, 2, UK, W], F32R, stack=r2)
        hth = sb("hth", [P, KT, SEQ], F32R, stack=r2)
        htl = sb("htl", [P, KT, SEQ], F32R, stack=r2)
        htmp = sb("htmp", [P, 2, 2, SEQ], stack=r2)
        r2.close()
        r2 = ExitStack()
        rows = sb("rows", [P, 4, P], stack=r2)
        r2.close()
        diag = htmp[:].rearrange("p a b t -> p (a b t)").rearrange("p (m n) -> p m n", n=P)
        r2 = ExitStack()
        R_zs = sb("R_zs", [P, NT, 3, P], stack=r2)
        R_zf = sb("R_zf", [P, 3, SEQ + 2], stack=r2)
        R_sh = sb("R_sh", [P, 3, SEQ], stack=r2)
        R_bonus = sb("R_bonus", [P, SEQ], stack=r2)
        R_gn = sb("R_gn", [P, SEQ], stack=r2)
        R_dec = sb("R_dec", [P, 2, NCH], stack=r2)
        R_wc = sb("R_wc", [P, NU, CH], stack=r2)
        R_rk = sb("R_rk", [P, 2, SEQ], stack=r2)
        R_vp = sb("R_vp", [P, CH + SEQ + CH], stack=r2)
        R_lw = sb("R_lw", [P, 3, SEQ], stack=r2)
        R_b = sb("R_b", [P, 2, SEQ], stack=r2)
        R_e1 = sb("R_e1", [P, 2, SEQ], stack=r2)
        R_e2 = sb("R_e2", [P, 2, SEQ], stack=r2)
        R_g = sb("R_g", [P, SEQ], stack=r2)
        R_kk = sb("R_kk", [P, SEQ], stack=r2)
        R_Kbd = sb("R_Kbd", [P, NU, P], stack=r2)
        R_Rbd = sb("R_Rbd", [P, NU, P], stack=r2)
        R_ABt = sb("R_ABt", [P, NU, P], stack=r2)
        R_UV = sb("R_UV", [P, 2, NU, CH], stack=r2)
        R_G = sb("R_G", [P, 2, NU, P], stack=r2)
        R_C = sb("R_C", [P, 2, NU, CH], stack=r2)
        R_Wbd = sb("R_Wbd", [P, NU, P], stack=r2)
        R_Qbd = sb("R_Qbd", [P, NU, P], stack=r2)
        R_Vbd = sb("R_Vbd", [P, NU, P], stack=r2)
        R_S = sb("R_S", [P, 2, CH], stack=r2)
        R_X = sb("R_X", [P, 2, CH], stack=r2)
        R_y = sb("R_y", [P, NCH, CH], stack=r2)
        R_st = sb("R_st", [P, NCH, 6], stack=r2)
        R_mv = sb("R_mv", [P, NCH, 2], stack=r2)
        R_lora = sb("R_lora", [P, 4, SEQ], stack=r2)
        r2.close()
        r2 = ExitStack()
        L_zs = sb("L_zs", [P, NT, 2, P], stack=r2)
        L_v = sb("L_v", [P, NT, DV], stack=r2)
        L_qk = sb("L_qk", [P, 2, SEQ], stack=r2)
        L_up = sb("L_up", [P, 2, P], stack=r2)
        L_gg = sb("L_gg", [P, SEQ], stack=r2)
        L_x = sb("L_x", [P, 2, SEQ], stack=r2)
        L_t = sb("L_t", [P, 2, SEQ], stack=r2)
        L_b = sb("L_b", [P, 2, SEQ], stack=r2)
        L_e1 = sb("L_e1", [P, 2, SEQ], stack=r2)
        L_e2 = sb("L_e2", [P, 2, SEQ], stack=r2)
        L_e3 = sb("L_e3", [P, 2, SEQ], stack=r2)
        L_qb = sb("L_qb", [P, 2, SEQ], stack=r2)
        L_kb = sb("L_kb", [P, 2, SEQ], stack=r2)
        L_kd = sb("L_kd", [P, 2, SEQ], stack=r2)
        L_kdt = sb("L_kdt", [P, 2, NT, P], stack=r2)
        L_att = sb("L_att", [P, 2, NT, P], stack=r2)
        L_S = sb("L_S", [P, 2, NCH - 1, DV], stack=r2)
        L_o = sb("L_o", [P, NT, DV], stack=r2)
        L_sq = sb("L_sq", [P, NT, DV], stack=r2)
        r2.close()
        r2 = ExitStack()
        A_qkT = sb("A_qkT", [P, 2, SEQ], stack=r2)
        A_p = sb("A_p", [P, 2, 2, NT, SEQ], stack=r2)
        A_pT = sb("A_pT", [P, NT, SEQ], stack=r2)
        A_s = sb("A_s", [P, 2, 12], stack=r2)
        A_sq = sb("A_sq", [P, P], stack=r2)
        A_ss = sb("A_ss", [P, NT, DH], stack=r2)
        A_rs = sb("A_rs", [P, NT, DH], stack=r2)
        A_on = sb("A_on", [P, 2, NT, 2 * P], stack=r2)
        A_t2 = sb("A_t2", [P, 2, 2, SEQ], stack=r2)
        A_lam = sb("A_lam", [P, 4 * 64 + 8], stack=r2)
        r2.close()


        A_qk = acc[:].rearrange("p s (i j c f) -> p s i j c f", i=NT, j=2, c=2)
        A_t = asum[:, 0:NT * P].rearrange("p (i j c f) -> p i j c f", i=NT, j=2, c=2)
        R_up = raw[:, 3].rearrange("p k w -> p (k w)")[:, 0:5 * P].rearrange("p (a n) -> p a n", n=P)
        R_KR = xf[:, 8:12].rearrange("p k (u n) -> p (k u) n", n=P)
        R_AB = xf[:, 12:16].rearrange("p k (u n) -> p (k u) n", n=P)

        pa = ctx.enter_context(nc.psum_tensor("pa", [P, 2, W], F32))
        pb = ctx.enter_context(nc.psum_tensor("pb", [P, 2, W], F32))
        py = ctx.enter_context(nc.psum_tensor("py", [P, 2, W], F32))
        pt = ctx.enter_context(nc.psum_tensor("pt", [P, 2, W], F32))
        ident = cst[:, C_ID:C_ID + P]
        ones = cst[:, C_ONES:C_ONES + P]
        heads1 = cst[:, C_HEADS:C_HEADS + P]
        level_masks = cst[:, C_LEVEL:C_LEVEL + 2 * LEVELS * CH].rearrange("p (d l n) -> p d l n", d=2, l=LEVELS)

        def level(eng, lv):
            for h, rows_ in enumerate((slice(0, CH), slice(CH, P))):
                if h and eng is nc.gpsimd:
                    eng.drain()
                ins = eng.tensor_tensor(
                    R_C[rows_, lv % 2].rearrange("p (d c) n -> p d c n", d=2),
                    R_G[rows_, h, :, 0:CH].rearrange("p (d c) n -> p d c n", d=2),
                    level_masks[rows_, :, lv].unsqueeze(2).to_broadcast((CH, 2, NCH, CH)), ALU.mult)
            return ins

        def tiles(bank, h):
            return bank[h * CH:(h + 1) * CH, h].rearrange("p (u n) -> p u n", n=CH)

        def flat(tile):
            return tile[:].rearrange("p u n -> p (u n)")
        ada_flat = ada[:].rearrange("p a b -> p (a b)")

        n_of = {0: 17, FG: 17 + FG + 12 + 4}
        C_FFN0, C_DIFF, C_OUT1, C_FFN1 = 17, 17 + 33, 17 + 33 + 12, 17 + 33 + 16
        PA_SKIP = {0: 0, C_DIFF: C_DIFF - (17 + FG)}

        FIRST_JOBS = 8
        ACT_AT = {(1, 2): 1, (2, 0): 2, (3, 2): 3, (4, 0): 4, (4, 1): 5, (4, 2): 6}
        DVE_AT = {(1, 0): 0, (1, 2): 1, (2, 2): 2, (3, 0): 3, (4, 1): 4}
        PE_AT = {1: 1, 2: 2}
        S_AT = (0, 2, 4, 6, 8)
        L_AT = (8, 8, 10, 10, 12, 14, 14, 14, 16, 18, 20, 20, 22, 24, 24, 24)
        X_AT = (24, 26, 28, 30, 32)

        const_in = sem("const_in")
        rows_zero = sem("rows_zero")
        rows_in = sem("rows_in")
        x_in_sem = sem("x_in_sem")
        tab_turned = sem("tab_turned")
        tab_copied = sem("tab_copied")
        silu_ready = sem("silu_ready")
        raw_in = [sem(f"raw_in{s}") for s in range(4)]
        hi_done = sem("hi_done")
        lo_done = sem("lo_done")
        unit_done = sem("unit_done")
        adaw_in = [sem(f"adaw_in{s}") for s in range(2)]
        ada_step = sem("ada_step")
        ada_cols = sem("ada_cols")
        ada_out = sem("ada_out")
        tr_done = sem("tr_done")
        h_scaled = sem("h_scaled")
        h_hi = sem("h_hi")
        h_lo = sem("h_lo")
        pa_done = sem("pa_done")
        pa_free = sem("pa_free")

        lora_turned = sem("lora_turned")
        lora_padded = sem("lora_padded")
        lora_mixed = sem("lora_mixed")
        lora_ready = sem("lora_ready")
        bd_zero = sem("bd_zero")
        passed = sem("passed")
        pair_done = sem("pair_done")
        zs_ready = sem("zs_ready")
        up_in = sem("up_in")
        rk_turned = sem("rk_turned")
        zf_ready = sem("zf_ready")
        rkv_mixed = sem("rkv_mixed")
        v_turned = sem("v_turned")
        uv_ready = sem("uv_ready")
        sq_ready = sem("sq_ready")
        ss_done = sem("ss_done")
        ss_clamped = sem("ss_clamped")
        rn_ready = sem("rn_ready")
        q_ready = sem("q_ready")
        bonus_done = sem("bonus_done")
        up_done = sem("up_done")
        up_act = sem("up_act")
        logs_ready = sem("logs_ready")
        exps_ready = sem("exps_ready")
        krbd_ready = sem("krbd_ready")
        ab_ready = sem("ab_ready")
        scores_done = sem("scores_done")
        g_ready = sem("g_ready")
        init_ready = sem("init_ready")
        ab_turned = sem("ab_turned")
        abt_ready = sem("abt_ready")
        q_done = sem("q_done")
        qc_ready = sem("qc_ready")
        first_ready = sem("first_ready")
        c1_ready = sem("c1_ready")
        kept_ready = sem("kept_ready")
        bonus_out = sem("bonus_out")
        c_ready = sem("c_ready")
        vc_ready = sem("vc_ready")
        v_done = sem("v_done")
        w_done = sem("w_done")
        wc_ready = sem("wc_ready")
        wbd_ready = sem("wbd_ready")
        tail_done = sem("tail_done")
        ys_var = sem("ys_var")
        ys_rstd = sem("ys_rstd")
        ybd_ready = sem("ybd_ready")
        yt_done = sem("yt_done")
        gg_turned = sem("gg_turned")
        gg_ready = sem("gg_ready")
        og_ready = sem("og_ready")
        gla_in = sem("gla_in")
        head_done = sem("head_done")
        gz_ready = sem("gz_ready")
        gv_ready = sem("gv_ready")
        g_turned = sem("g_turned")
        g_qk = sem("g_qk")
        g_gate = sem("g_gate")
        g_x = sem("g_x")
        g_soft = sem("g_soft")
        g_logs = sem("g_logs")
        g_exps = sem("g_exps")
        g_prod = sem("g_prod")
        g_att = sem("g_att")
        g_kdt_done = sem("g_kdt_done")
        g_kdt = sem("g_kdt")
        g_attm = sem("g_attm")
        g_kv = sem("g_kv")
        g_states = sem("g_states")
        g_o = sem("g_o")
        g_sq = sem("g_sq")
        g_var = sem("g_var")
        g_rstd = sem("g_rstd")
        g_on = sem("g_on")
        g_oT = sem("g_oT")
        split_hi = sem("split_hi")
        split_lo = sem("split_lo")
        ln_in = sem("ln_in")
        diag_ready = sem("diag_ready")
        gate_mm = sem("gate_mm")
        gate_out = sem("gate_out")
        end_var = sem("end_var")
        end_rstd = sem("end_rstd")
        x_ready = sem("x_ready")
        x_scaled = sem("x_scaled")
        out_ready = sem("out_ready")
        pb_done = sem("pb_done")
        pb_free = sem("pb_free")
        py_done = sem("py_done")
        py_free = sem("py_free")
        gu_turned = sem("gu_turned")
        guh_ready = sem("guh_ready")
        gul_ready = sem("gul_ready")
        ysum_zero = sem("ysum_zero")
        lam_in = sem("lam_in")
        lam_prod = sem("lam_prod")
        lam_exp = sem("lam_exp")
        lam_mm = sem("lam_mm")
        at_rot = sem("at_rot")
        at_out = sem("at_out")
        at_turned = sem("at_turned")
        at_T = sem("at_T")
        at_scores = sem("at_scores")
        at_bias = sem("at_bias")
        at_exp = sem("at_exp")
        at_p = sem("at_p")
        at_pturned = sem("at_pturned")
        at_pT = sem("at_pT")
        at_o = sem("at_o")
        at_sq = sem("at_sq")
        at_var = sem("at_var")
        at_rstd = sem("at_rstd")
        at_on = sem("at_on")
        at_oT = sem("at_oT")
        at_scaled = sem("at_scaled")
        at_hi = sem("at_hi")
        at_done = sem("at_done")
        out_sem = sem("out_sem")
        x_done = [sem(f"x_done{d}") for d in range(2)]
        xs_ready = [sem(f"xs_ready{d}") for d in range(2)]
        u_ready = [sem(f"u_ready{d}") for d in range(2)]
        s_done = [sem(f"s_done{d}") for d in range(2)]
        s_ready = [sem(f"s_ready{d}") for d in range(2)]
        u_done = [sem(f"u_done{d}") for d in range(2)]
        y_done = [sem(f"y_done{d}") for d in range(2)]

        block = ctx.enter_context(nc.Block())
        cond = ada_w.rearrange("a b (s i p) (j w) -> (a b) j s p i w", p=P, i=UK, w=W)

        def load_unit(sp, c, s, src, width=W, first=False):
            if not first:
                sp.wait_ge(lo_done, c * 4 + s + 1)
            sp.dma_start(raw[:, s, :, 0:width], src).then_inc(raw_in[s], 16)

        def load_cond(sp, j, s, src):
            sp.wait_ge(ada_step, j * 17 + (5 + 4 * (s - 2) if s >= 2 else 4 * s - 4))
            sp.dma_start(adaw[:, s % 2], src).then_inc(adaw_in[s % 2], 16)

        def high(act, c, s, width=W):
            act.wait_ge(raw_in[s], c * 16 + (16 * FIRST_JOBS + 16))
            act.wait_ge(unit_done, c * 4 + s + 1)
            act.activation(wh[:, s % 2, :, 0:width], raw[:, s, :, 0:width], ACT.Copy).then_inc(hi_done, 1)

        def low(dve, c, s, width=W):
            dve.wait_ge(hi_done, c * 4 + s + 1)
            dve.tensor_tensor(wl[:, s % 2, :, 0:width], raw[:, s, :, 0:width],
                              wh[:, s % 2, :, 0:width].bitcast(F32), ALU.subtract).then_inc(lo_done, 1)

        def load_first(sp, j, s, src):
            if not (isinstance(j, int) and j == 0):
                sp.wait_ge(ada_step, j * 17 + (4 * s - 12))
            sp.dma_start(raw[:, s], src).then_inc(raw_in[s], 16)

        def cond_steps(dve, j, a, b, ring=adaw):
            for k in range(a, b):
                s, i = k // UK, k % UK
                slot = s if ring is raw else s % 2
                if i == 0 and ring is raw:
                    dve.wait_ge(raw_in[s], j * 16 + 16)
                elif i == 0:
                    dve.wait_ge(adaw_in[slot], (j - FIRST_JOBS) * 32 + (16 * (s // 2) + 16))
                if k < 2:
                    dve.wait_ge(ada_step, j * 17 + 1)
                    dve.tensor_scalar(acc[:, k % 2], ring[:, slot, i], silu_c[:, k:k + 1], None,
                                      ALU.mult).then_inc(ada_step, 1)
                else:
                    dve.wait_ge(ada_step, j * 17 + k)
                    dve.scalar_tensor_tensor(acc[:, k % 2], ring[:, slot, i], silu_c[:, k:k + 1],
                                             acc[:, k % 2], ALU.mult, ALU.add).then_inc(ada_step, 1)

        def cond_unit(dve, j, s, ring=adaw):
            cond_steps(dve, j, UK * s, UK * s + UK, ring)

        def cond_sum(dve, j, first=False):
            dve.wait_ge(ada_step, j * 17 + 17)
            if not first:
                dve.wait_ge(ada_cols, j)
            dve.tensor_tensor(asum[:], acc[:, 0], acc[:, 1], ALU.add).then_inc(ada_step, 1)

        def cond_cols(pe, j, first=False, bank=None):
            pe.wait_ge(ada_step, j * 17 + 18)
            if not first:
                pe.wait_ge(ada_out, j)
            bank = pt[:, 1] if bank is None else bank
            for m in range(4):
                mm = pe.matmul(bank[:, m:m + 1], asum[:, m * P:(m + 1) * P], ones[:, 0:1], start=(m == 0),
                               stop=True, skip_group_check=True)
            mm.then_inc(ada_cols, 1)

        def cond_store(dve, j, bank=None):
            bank = pt[:, 1] if bank is None else bank
            dve.wait_ge(ada_cols, j + 1)
            dve.tensor_tensor(ada_flat[:, bass.ds(j * 4, 4)], bank[:, 0:4], tab[:, bass.ds(j * 4 + T_ADA, 4)],
                              ALU.add).then_inc(ada_out, 1)

        def multiply(pe, c, s, lhs, bank, width=W, start=True, stop=True, tile0=None, k0=None,
                     free=None):
            pe.wait_ge(lo_done, c * 4 + s + 5)
            hi, lo = lhs
            for i in range(NT):
                if free is not None:
                    pe.wait_ge(free[0], free[1] * 2 + 1 + i)
                for k in range(UK):
                    kk = (k0 if k0 is not None else UK * s) + k
                    a_hi, a_lo = hi[:, kk, i * P:(i + 1) * P], lo[:, kk, i * P:(i + 1) * P]
                    w_hi, w_lo = wh[:, s % 2, k, 0:width], wl[:, s % 2, k, 0:width]
                    o = bank[:, i, 0:width]
                    pe.matmul(o, a_hi, w_hi, start=start and k == 0, stop=False)
                    pe.matmul(o, a_hi, w_lo, start=False, stop=False)
                    mm = pe.matmul(o, a_lo, w_hi, start=False, stop=stop and k == UK - 1)
                if i == 0 and tile0 is not None:
                    mm.then_inc(tile0, 1)
            mm.then_inc(unit_done, 1)

        def project(pe, c, n, lhs, done, free, bank, width=W, call=None, between=None):
            for s in range(4):
                if call is not None:
                    pe.wait_ge(h_lo, 8 * call + 2 * s + 2)
                multiply(pe, c, s, lhs, bank, width, start=(s == 0), stop=(s == 3), tile0=done if s == 3 else None,
                         free=(free, n) if s == 0 else None)
                if between is not None:
                    between(s)

        def turn_pe(pe, call):
            for g in range(KT // 2):
                n = call * 8 + g
                if n >= 2:
                    pe.wait_ge(h_scaled, n - 1)
                if call and g % 4 == 0:
                    pe.wait_ge(x_ready, 2 * call - 1 + g // 4)
                for j in range(2):
                    for i in range(NT):
                        mm = pe.transpose(py[:, g % 2, j * SEQ + i * P:j * SEQ + (i + 1) * P],
                                          xt[:, i, (2 * g + j) * P:(2 * g + j + 1) * P], ident)
                mm.then_inc(tr_done, 1)

        def turn_act(act, call):
            for g in range(KT // 2):
                n = call * 8 + g
                act.wait_ge(h_scaled, n + 1)
                act.activation(hth[:, 2 * g:2 * g + 2, :], htmp[:, g % 2], ACT.Copy).then_inc(h_hi, 1)

        def factors_dve(dve, sub):
            dve.tensor_scalar(small[:, 0:16], ada[:, sub, 16:32], 1.0, None, ALU.add)
            dve.drain()
            if sub:
                g, b = T_LN_G + 16 * (sub - 1), T_LN_B + 16 * (sub - 1)
                dve.tensor_tensor(small[:, 16:32], small[:, 0:16], tab[:, b:b + 16], ALU.mult)
                dve.drain()
                dve.tensor_tensor(small[:, 16:32], small[:, 16:32], ada[:, sub, 0:16], ALU.add)
                dve.tensor_tensor(small[:, 0:16], small[:, 0:16], tab[:, g:g + 16], ALU.mult)
                dve.drain()

        def turn_dve(dve, call):
            shift = small[:, 16:32] if call else ada[:, 0, 0:16]

            def lower(g):
                dve.wait_ge(h_hi, call * 8 + g + 1)
                dve.tensor_tensor(htl[:, 2 * g:2 * g + 2, :], htmp[:, g % 2],
                                  hth[:, 2 * g:2 * g + 2, :].bitcast(F32), ALU.subtract).then_inc(h_lo, 1)
            for g in range(KT // 2):
                dve.wait_ge(tr_done, call * 8 + g + 1)
                if g >= 2:
                    dve.wait_ge(h_lo, call * 8 + g - 1)
                for j in range(2):
                    k = 2 * g + j
                    ins = dve.tensor_scalar(htmp[:, g % 2, j], py[:, g % 2, j * SEQ:(j + 1) * SEQ],
                                            small[:, k:k + 1], shift[:, k:k + 1], ALU.mult, ALU.add)
                ins.then_inc(h_scaled, 1)
                if g:
                    lower(g - 1)
            lower(KT // 2 - 1)

        def split_act(act, call):
            for g in range(KT // 2):
                act.activation(hth[:, 2 * g:2 * g + 2], xf[:, 2 * g:2 * g + 2], ACT.Copy).then_inc(split_hi, 1)

        def split_dve(dve, call):
            for g in range(KT // 2):
                dve.wait_ge(split_hi, call * 8 + g + 1)
                dve.tensor_tensor(htl[:, 2 * g:2 * g + 2], xf[:, 2 * g:2 * g + 2],
                                  hth[:, 2 * g:2 * g + 2].bitcast(F32), ALU.subtract).then_inc(split_lo, 1)

        def gate_dve(dve, n, g):
            if g == 0:
                dve.drain()
            if n * 4 + g >= 2:
                dve.wait_ge(gate_mm, n * 4 + g - 1)
            for m in range(4):
                k = 32 + 4 * g + m
                ins = dve.tensor_scalar(diag[:, g % 2 * 4 + m], ident, ada[:, n, k:k + 1], None, ALU.mult)
            ins.then_inc(diag_ready, 1)

        def gate_pe(pe, n, g, bank):
            pe.wait_ge(diag_ready, n * 4 + g + 1)
            if n * 4 + g >= 2:
                pe.wait_ge(gate_out, n * 4 + g - 1)
            for m in range(4):
                mm = pe.matmul(bank[:, g % 2, m * P:(m + 1) * P], ones, diag[:, g % 2 * 4 + m], start=True, stop=True)
            mm.then_inc(gate_mm, 1)

        def gate_act(act, n, g, bank):
            act.wait_ge(gate_mm, n * 4 + g + 1)
            act.activation(gate_bc[:, g * W:(g + 1) * W], bank[:, g % 2], ACT.Copy, bias=1.0).then_inc(gate_out, 1)

        def end_load(act, n):
            if n:
                act.wait_ge(x_scaled, n)
            act.dma_start(lng[:], ln_g[n // 2, n % 2].partition_broadcast(P)).then_inc(ln_in, 16)
            act.dma_start(lnb[:], ln_b[n // 2, n % 2].partition_broadcast(P)).then_inc(ln_in, 16)

        def end_act(act, n):
            act.wait_ge(end_var, n + 1)
            act.activation(small[:, 36:38], small[:, 34:36], ACT.Ln)
            act.drain()
            act.activation(small[:, 38:40], small[:, 36:38], ACT.Exp, scale=-0.5).then_inc(end_rstd, 1)

        stats = small[:, 40:88].rearrange("p (i c s) -> p i c s", i=NT, s=6)

        def end_block(dve, n, q):
            cols = slice(q * W, (q + 1) * W)
            if q == 0:
                dve.wait_ge(gate_out, n * 4 + 4)
                if n:
                    dve.wait_ge(x_scaled, n)
            dve.drain()
            for i in range(NT):
                dve.tensor_tensor(ysum[:, i, cols], ysum[:, i, cols], gate_bc[:, cols], ALU.mult)
            dve.drain()
            for i in range(NT):
                dve.scalar_tensor_tensor(xt[:, i, cols], xt[:, i, cols], ALPHA, ysum[:, i, cols], ALU.mult, ALU.add)
            dve.drain()
            for i in range(NT):
                dve.bn_stats(stats[:, i, q], xt[:, i, cols])

        def end_dve(dve, n, c=None):
            dve.drain()
            for i in range(NT):
                dve.bn_aggr(small[:, 88 + 2 * i:90 + 2 * i], stats[:, i].rearrange("p c s -> p (c s)"))
            dve.drain()
            for i in range(NT):
                ins = dve.tensor_scalar(small[:, 34 + i:35 + i], small[:, 89 + 2 * i:90 + 2 * i], EPS, None, ALU.add)
            ins.then_inc(end_var, 1)
            if n < 3:
                factors_dve(dve, n + 1)
                low(dve, c, 0)
                low(dve, c, 1)
            dve.wait_ge(end_rstd, n + 1)
            for half in range(2):
                cols = slice(half * D // 2, (half + 1) * D // 2)
                for i in range(NT):
                    ins = dve.tensor_scalar(xt[:, i, cols], xt[:, i, cols], small[:, 88 + 2 * i:89 + 2 * i],
                                            small[:, 38 + i:39 + i], ALU.subtract, ALU.mult)
                ins.then_inc(x_ready, 1)

        def end_pool(pool, n):
            pool.wait_ge(ln_in, n * 32 + 32)
            pool.wait_ge(tr_done, 8 * n + 16)
            pool.sem_inc(passed, 1)
            for i in range(NT):
                pool.tensor_tensor(xt[:, i], xt[:, i], lng[:], ALU.mult)
            pool.drain()
            for i in range(NT):
                pool.tensor_tensor(xt[:, i], xt[:, i], lnb[:], ALU.add)
            pool.drain().then_inc(x_scaled, 1)

        def out_sp(sp, c0, wv, first=0):
            for q in range(first, 4):
                for s in range(4):
                    load_unit(sp, c0 + q, s, wv[s, :, :, q * W:(q + 1) * W])

        def out_act(act, c0, n0, n):
            end_load(act, n)
            for q in range(4):
                for s in range(4):
                    high(act, c0 + q, s)
                    if q and s == 0:
                        act.wait_ge(pa_done, n0 + q)
                        act.activation(ysum[:, 0, (q - 1) * W:q * W], pa[:, 0], ACT.Copy).then_inc(pa_free, 1)
                        act.wait_ge(unit_done, (c0 + q) * 4 + 2)
                        act.activation(ysum[:, 1, (q - 1) * W:q * W], pa[:, 1], ACT.Copy).then_inc(pa_free, 1)
                    g = 4 * q + s - 3
                    if 0 <= g < 4:
                        gate_act(act, n, g, pb)
            act.wait_ge(pa_done, n0 + 4)
            act.activation(ysum[:, 0, 3 * W:], pa[:, 0], ACT.Copy).then_inc(pa_free, 1)
            act.wait_ge(unit_done, (c0 + 4) * 4 + 2)
            act.activation(ysum[:, 1, 3 * W:], pa[:, 1], ACT.Copy).then_inc(pa_free, 1)

        def out_dve(dve, c0, n0, n):
            for q in range(4):
                for s in range(4):
                    low(dve, c0 + q, s)
                    if q == 0:
                        gate_dve(dve, n, s)
                    if q and s == 2:
                        dve.wait_ge(pa_free, 2 + 2 * (n0 + q))
                        end_block(dve, n, q - 1)
            dve.wait_ge(pa_free, 2 + 2 * (n0 + 4))
            end_block(dve, n, 3)

        def out_pe(pe, c0, n0, n):
            for q in range(4):
                project(pe, c0 + q, n0 + q, (hth, htl), pa_done, pa_free, pa,
                        between=lambda s, q=q: gate_pe(pe, n, 4 * q + s - 1, pb) if 0 <= 4 * q + s - 1 < 4 else None)

        def rotate(eng, t, slot):
            def part(i):
                src = qkv[:, i, 0:2 * D].rearrange("p (j n) -> p j n", j=2)[:, :, bass.ds(t * P, P)].rearrange(
                    "p j (c f) -> p j c f", c=2)

                def wave(at):
                    return cst[:, at + 32 * i:at + 32 * i + 32].unsqueeze(1).unsqueeze(1).to_broadcast((P, 2, 2, 32))
                return (src[:, :, :, 0:32], src[:, :, :, 32:64], A_qk[:, slot, i, :, :, 0:32], A_qk[:, slot, i, :, :, 32:64],
                        wave(C_COS), wave(C_SIN))
            for i in range(NT):
                x1, x2, o1, o2, cos, sin = part(i)
                eng.tensor_tensor(o1, x1, cos, ALU.mult)
                eng.tensor_tensor(A_t[:, i], x2, sin, ALU.mult)
                eng.tensor_tensor(o2, x2, cos, ALU.mult)
            eng.drain()
            for i in range(NT):
                x1, x2, o1, o2, cos, sin = part(i)
                eng.tensor_tensor(o1, o1, A_t[:, i], ALU.subtract)
            eng.drain()
            for i in range(NT):
                x1, x2, o1, o2, cos, sin = part(i)
                eng.tensor_tensor(A_t[:, i], x1, sin, ALU.mult)
            eng.drain()
            for i in range(NT):
                x1, x2, o1, o2, cos, sin = part(i)
                eng.tensor_tensor(o2, o2, A_t[:, i], ALU.add)
            eng.drain().then_inc(at_rot, 1)

        def heads(eng, body):
            with eng.Fori(0, DH // 2 - 1) as m:
                body(m * 2, 0, 2)
                body(m * 2 + 1, 1, 2)
            body(DH - 2, 0, 1)
            body(DH - 1, 1, 0)

        def in_act(act, c0, dest):
            with act.Fori(0, 11) as t:
                high(act, t + c0, 2)
                high(act, t + c0, 3)
                high(act, t + c0 + 1, 0)
                act.wait_ge(pa_done, t + c0 + 1 - PA_SKIP[c0])
                act.activation(dest[:, 0, bass.ds(t * W, W)], pa[:, 0], ACT.Copy).then_inc(pa_free, 1)
                act.wait_ge(unit_done, t * 4 + 4 * c0 + 6)
                act.wait_ge(x_scaled, 2)
                act.activation(dest[:, 1, bass.ds(t * W, W)], pa[:, 1], ACT.Copy).then_inc(pa_free, 1)
                high(act, t + c0 + 1, 1)
            high(act, c0 + 11, 2)
            high(act, c0 + 11, 3)
            act.wait_ge(pa_done, c0 + 12 - PA_SKIP[c0])
            act.activation(dest[:, 0, 11 * W:12 * W], pa[:, 0], ACT.Copy).then_inc(pa_free, 1)
            act.wait_ge(unit_done, 4 * (c0 + 11) + 6)
            act.activation(dest[:, 1, 11 * W:12 * W], pa[:, 1], ACT.Copy).then_inc(pa_free, 1)

        def ffn_sp(sp, c0, layer, j0=None):
            w_in = ffn_w_in[layer].rearrange("(s i p) (h g w) -> h g s p i w", p=P, i=UK, h=2, w=W)
            w_out = ffn_w_out[layer].rearrange("(g i p) (q w) -> g q p i w", p=P, i=UK, w=W)

            for n in range(8):
                if j0 is not None and n >= 4:
                    load_cond(sp, j0, n - 4, cond[2, 0, n - 4])
                load_unit(sp, c0 + n // 4, n % 4, w_in[n // 4, 0, n % 4])
            if j0 is not None:
                for u in range(4):
                    load_cond(sp, j0 + 1, u, cond[2, 1, u])

            def group(g, n, sub):
                load_unit(sp, g * 3 + (c0 - 1) + n // 4, n % 4, w_in[n // 4, bass.ds(g, 1), n % 4])
                if j0 is not None and n:
                    m, u = (n - 1) // 4, (n - 1) % 4
                    load_cond(sp, g * 2 + (m + j0), u, cond[sub, bass.ds(g * 2 + (m - (12 if sub == 3 else 0)), 1), u])

            def step(g, sub):
                for n in range(8):
                    group(g, n, sub)
                for q in range(4):
                    load_unit(sp, g * 3 + (c0 + 1), q, w_out[bass.ds(g - 1, 1), q])
                    if j0 is not None and q == 2:
                        load_cond(sp, g * 2 + (j0 + 1), 3, cond[sub, bass.ds(g * 2 + (1 if sub == 2 else -11), 1), 3])
            if j0 is not None:
                with sp.Fori(1, 6) as g:
                    step(g, 2)
                with sp.Fori(6, FG) as g:
                    step(g, 3)
            else:
                with sp.Fori(1, FG) as g:
                    step(g, None)
            for q in range(4):
                load_unit(sp, c0 + 32, q, w_out[FG - 1, q])

        def ffn_act(act, c0, f, n_pa, n):
            def gate_up(c, g, first=False):
                for s in range(2 if first else 1, 4):
                    high(act, c, s)
                high(act, c + 1, 0)
                if first:
                    gate_act(act, n, 0, py)
                if not (first and f == 0):
                    act.wait_ge(gu_turned, g)
                act.wait_ge(pa_done, g + (n_pa - f + 1))
                act.activation(gu[:, 0], pa[:, 0], ACT.Silu).then_inc(pa_free, 1)
                high(act, c + 1, 1)
                if first:
                    gate_act(act, n, 1, py)
                act.wait_ge(unit_done, c * 4 + 6)
                act.activation(gu[:, 1], pa[:, 1], ACT.Silu).then_inc(pa_free, 1)
                high(act, c + 1, 2)
                if first:
                    gate_act(act, n, 2, py)
                high(act, c + 1, 3)
                if first:
                    gate_act(act, n, 3, py)

            def turned(g):
                act.wait_ge(gu_turned, g + 1)
                act.activation(guh[:, 0:2].rearrange("p k t -> p (k t)"), pt[:, 0], ACT.Copy)
                act.activation(guh[:, 2:4].rearrange("p k t -> p (k t)"), pb[:, 0], ACT.Copy).then_inc(guh_ready, 1)
            gate_up(c0, f, first=True)
            high(act, c0 + 2, 0)
            turned(f)
            end_load(act, n)
            with act.Fori(1, FG) as g:
                c = g * 3 + (c0 - 1)
                gate_up(c, g + f)
                for q in range(4):
                    high(act, c + 2, q)
                high(act, c + 3, 0)
                turned(g + f)
            for q in range(1, 4):
                high(act, c0 + 32, q)

        def ffn_dve(dve, c0, f, u0, n_end, j0=None):
            def cond_at(j, n):
                if j0 is not None:
                    cond_unit(dve, j + (n - 1) // 4, (n - 1) % 4)
                    if n == 4:
                        cond_sum(dve, j)

            def product(i, c, g):
                if i == 0:
                    dve.wait_ge(pb_done, g + 1)
                    dve.wait_ge(pa_free, 2 * g + 2 * (n_of[f] - f) + 3)
                else:
                    dve.wait_ge(unit_done, c * 4 + 10)
                    dve.wait_ge(pa_free, 2 * g + 2 * (n_of[f] - f) + 4)
                dve.tensor_tensor(gu[:, i], gu[:, i], pb[:, i], ALU.mult).then_inc(pb_free, 1)

            def add(c, q, u):
                dve.wait_ge(py_done, u + 1)
                dve.tensor_tensor(ysum[:, 0, q * W:(q + 1) * W], ysum[:, 0, q * W:(q + 1) * W], py[:, 0], ALU.add).then_inc(py_free, 1)
                dve.wait_ge(unit_done, c * 4 + q + 3)
                dve.tensor_tensor(ysum[:, 1, q * W:(q + 1) * W], ysum[:, 1, q * W:(q + 1) * W], py[:, 1], ALU.add).then_inc(py_free, 1)

            def lower(g):
                dve.wait_ge(guh_ready, g + 1)
                dve.tensor_tensor(gul[:, 0:2].rearrange("p k t -> p (k t)"), pt[:, 0],
                                  guh[:, 0:2].rearrange("p k t -> p (k t)").bitcast(F32), ALU.subtract)
                dve.tensor_tensor(gul[:, 2:4].rearrange("p k t -> p (k t)"), pb[:, 0],
                                  guh[:, 2:4].rearrange("p k t -> p (k t)").bitcast(F32), ALU.subtract).then_inc(gul_ready, 1)
            for n in range(2, 8):
                low(dve, c0 + n // 4, n % 4)
                if n < 6:
                    gate_dve(dve, n_end, n - 2)
                cond_at(j0, n - 1)
            cond_at(j0, 7)
            if j0 is not None:
                cond_unit(dve, j0 + 1, 3)
            low(dve, c0 + 2, 0)
            product(0, c0, f)
            product(1, c0, f)
            if j0 is not None:
                cond_store(dve, j0)
                cond_sum(dve, j0 + 1)
            lower(f)
            if j0 is not None:
                cond_store(dve, j0 + 1)
            dve.wait_ge(ysum_zero, 1 if f == 0 else 2)
            with dve.Fori(1, FG) as g:
                c = g * 3 + (c0 - 1)
                for n in range(1, 8):
                    low(dve, c + n // 4, n % 4)
                    cond_at(g * 2 + (j0 or 0), n)
                low(dve, c + 2, 0)
                product(0, c, g + f)
                product(1, c, g + f)
                if j0 is not None:
                    cond_store(dve, g * 2 + j0)
                for q in range(1, 4):
                    low(dve, c + 2, q)
                    add(c + 2, q - 1, g * 4 + (u0 - 4 + q - 1))
                    if q == 2 and j0 is not None:
                        cond_unit(dve, g * 2 + (j0 + 1), 3)
                if j0 is not None:
                    cond_sum(dve, g * 2 + (j0 + 1))
                low(dve, c + 3, 0)
                add(c + 2, 3, g * 4 + (u0 - 1))
                lower(g + f)
                if j0 is not None:
                    cond_store(dve, g * 2 + (j0 + 1))
            for q in range(1, 4):
                low(dve, c0 + 32, q)
                add(c0 + 32, q - 1, u0 + 40 + q - 1)
                end_block(dve, n_end, q - 1)
            add(c0 + 32, 3, u0 + 43)
            end_block(dve, n_end, 3)

        def ffn_pe(pe, c0, f, u0, n, j0=None):
            def turn(g):
                pe.wait_ge(pb_free, g * 2 + 4)
                for k in range(UK):
                    bank = pt[:, 0] if k < 2 else pb[:, 0]
                    for i in range(NT):
                        at = (k % 2) * SEQ + i * P
                        mm = pe.transpose(bank[:, at:at + P], gu[:, i, k * P:(k + 1) * P], ident)
                mm.then_inc(gu_turned, 1)

            def output(c, u, g):
                pe.wait_ge(gul_ready, g + 1)
                for q in range(4):
                    multiply(pe, c, q, (guh, gul), py, tile0=py_done, k0=0, free=(py_free, u + q))
            project(pe, c0, n_of[f], (hth, htl), pa_done, pa_free, pa, call=n,
                    between=lambda s: gate_pe(pe, n, s - 2, py) if s >= 2 else None)
            project(pe, c0 + 1, f, (hth, htl), pb_done, pb_free, pb,
                    between=lambda s: gate_pe(pe, n, s + 2, py) if s < 2 else None)
            if j0 is not None:
                cond_cols(pe, j0)
            turn(f)
            if j0 is not None:
                cond_cols(pe, j0 + 1)
            with pe.Fori(1, FG) as g:
                c = g * 3 + (c0 - 1)
                project(pe, c, g + n_of[f], (hth, htl), pa_done, pa_free, pa)
                pe.wait_ge(gul_ready, g + f)
                project(pe, c + 1, g + f, (hth, htl), pb_done, pb_free, pb)
                if j0 is not None:
                    cond_cols(pe, g * 2 + j0)
                output(c + 2, g * 4 + (u0 - 4), g + (f - 1))
                turn(g + f)
                if j0 is not None:
                    cond_cols(pe, g * 2 + (j0 + 1))
            output(c0 + 32, u0 + 40, f + 10)

        ab_w = ab_w_in[0].rearrange("(s i p) n -> s p i n", p=P, i=UK)
        LASTW = Z - (ABC - 1) * W

        def vectors():
            yield T_LN_G, ln_g.rearrange("a b (k p) -> (a b k) p", p=P)
            yield T_LN_B, ln_b.rearrange("a b (k p) -> (a b k) p", p=P)
            yield T_MU, rwkv_mu[0, 0:3 * RW].rearrange("(k p) -> k p", p=P)
            yield T_MU + 24, rwkv_mu[0:1, Z_WD:Z_AD]
            yield T_MU + 25, rwkv_mu[0:1, Z_AD:Z_GD]
            yield T_MU + 26, rwkv_mu[0, Z_GD:Z_Q].rearrange("(k p) -> k p", p=P)
            yield T_W0, rwkv_w0[0].rearrange("a (k p) -> (a k) p", p=P)
            yield T_A0, rwkv_a0[0].rearrange("(k p) -> k p", p=P)
            yield T_KK, rwkv_k_k[0].rearrange("(k p) -> k p", p=P)
            yield T_KA, rwkv_k_a[0].rearrange("(k p) -> k p", p=P)
            yield T_RK, rwkv_r_k[0].rearrange("(k h) n -> k (h n)", h=2)
            yield T_GNG, rwkv_gn_g[0].rearrange("(k p) -> k p", p=P)
            yield T_GNB, rwkv_gn_b[0].rearrange("(k p) -> k p", p=P)
            yield T_GB, gla_gate_b[0].rearrange("a (k p) -> (a k) p", p=P)
            yield T_NG, gla_norm_g[0].rearrange("(k p) -> k p", p=P)
            yield T_SUB, diff_subln_g[0:1, :]
            yield T_C, c_in[0].rearrange("(k p) -> k p", p=P)
            ab = ada_b.rearrange("a b (k p) -> (a b k) p", p=P)
            yield T_ADA, ab[0:96]
            yield T_ADA + 96, ab[96:192]

        @block.sync
        def _(sp):
            sp.dma_start(cst[:], consts).then_inc(const_in, 16)
            sp.wait_ge(rows_zero, 1)
            for col, src in vectors():
                tile = max(i for i in range(4) if TABS[i] <= col)
                r = col - TABS[tile]
                sp.dma_start(rows[r:r + src.shape[0], tile, 0:src.shape[1]], src).then_inc(rows_in, 16)
            for s in range(4):
                load_first(sp, 0, s, cond[0, 0, s])
            sp.dma_start(xt[:], x_in[0].rearrange("(i p) d -> p i d", p=P)).then_inc(x_in_sem, 16)
            with sp.Fori(1, 8) as j:
                for s in range(4):
                    load_first(sp, j, s, cond[0, bass.ds(j, 1), s])
            for s in range(4):
                sp.wait_ge(ada_step, FIRST_JOBS * 17 + (4 * s - 12))
                load_unit(sp, 0, s, ab_w[s, :, :, 0:W], first=True)
            with sp.Fori(1, 12) as c:
                for s in range(4):
                    load_unit(sp, c, s, ab_w[s, :, :, bass.ds(c * W, W)])
            for s in range(4):
                load_unit(sp, 12, s, ab_w[s, :, :, 12 * W:Z], LASTW)
            with sp.Fori(0, 2) as t:
                for h in range(2):
                    for s in range(4):
                        load_cond(sp, t * 2 + (8 + h), s, cond[0, bass.ds(t * 2 + (8 + h), 1), s])
            with sp.Fori(2, PAIRS) as t:
                for h in range(2):
                    for s in range(4):
                        load_cond(sp, t * 2 + (8 + h), s, cond[1, bass.ds(t * 2 + (h - 4), 1), s])
            ab_wo = ab_w_out[0].rearrange("(s i p) n -> s p i n", p=P, i=UK)
            sp.wait_ge(tail_done, PAIRS)
            for s in range(4):
                load_unit(sp, 13, s, ab_wo[s, :, :, 0:W])
            gup_v = gla_gate_up[0].rearrange("a r n -> r a n")
            sp.wait_ge(tail_done, PAIRS)
            sp.dma_start(L_up[0:GLORA], gup_v[:, :, 0:DK]).then_inc(gla_in, 16)
            with sp.Fori(1, GH) as t:
                sp.wait_ge(g_gate, t)
                sp.dma_start(L_up[0:GLORA], gup_v[:, :, bass.ds(t * DK, DK)]).then_inc(gla_in, 16)
            sp.wait_ge(head_done, 1 + GH)
            out_sp(sp, 13, ab_wo, first=1)
            ffn_sp(sp, C_FFN0, 0, 24)
            dw = diff_w_in[0].rearrange("(s i p) n -> s p i n", p=P, i=UK)
            for u in range(12):
                if u >= 4:
                    load_cond(sp, 45 + u // 4, u % 4, cond[3, 9 + u // 4, u % 4])
                load_unit(sp, u // 4 + C_DIFF, u % 4, dw[u % 4, :, :, u // 4 * W:(u // 4 + 1) * W])
            with sp.Fori(3, 12) as t:
                for s in range(4):
                    load_unit(sp, t + C_DIFF, s, dw[s, :, :, bass.ds(t * W, W)])
            out_sp(sp, C_OUT1, diff_w_out[0].rearrange("(s i p) n -> s p i n", p=P, i=UK))
            ffn_sp(sp, C_FFN1, 1)
            out_v = out[0].rearrange("(i p) d -> p i d", p=P)
            for i in range(NT):
                sp.wait_ge(out_ready, i + 1)
                if i:
                    sp.wait_ge(x_scaled, 4)
                sp.dma_start(out_v[:, i], xt[:, i]).then_inc(out_sem, 16)
            sp.wait_ge(out_sem, 32)

        @block.gpsimd
        def _(pool):
            pool.memset(rows[:], 0.0).then_inc(rows_zero, 1)
            pool.wait_ge(unit_done, 2 + 4 * ABC)
            for tile in (R_Kbd, R_Rbd, R_Wbd, R_Qbd, R_Vbd):
                pool.memset(tile[:], 0.0)
            pool.memset(R_vp[:], 0.0)
            pool.memset(R_zf[:], 0.0)
            pool.memset(R_G[:].rearrange("p a b c -> p (a b c)")[:, 0:4 * (SEQ + 2)], 0.0)
            pool.drain().then_inc(bd_zero, 1)
            pool.wait_ge(lora_ready, 3)
            pool.wait_ge(pa_free, 2 + 2 * ABC)

            def next_z(n):
                for i in range(NT):
                    src = z[:, i, 0:3 * RW].rearrange("p (j n) -> p j n", n=RW)
                    pool.tensor_copy(R_zs[:, i], src[:, :, bass.ds(n * P, P)])
                pool.drain().then_inc(zs_ready, 1)

            def both(row):
                return row.unsqueeze(1).to_broadcast((row.shape[0], 2, SEQ))

            def units(tile, rows_, at):
                return tile[rows_, :, at:at + CH]
            full, top, low_half = slice(0, P), slice(0, CH), slice(CH, P)

            def next_factors(n):
                pool.wait_ge(exps_ready, n + 1)
                pool.wait_ge(q_ready, n + 1)
                pool.sem_inc(passed, 1)
                pool.tensor_tensor(units(R_KR, full, 0), both(R_kk[:]), R_lw[:, 0:2], ALU.mult)
                pool.tensor_tensor(units(R_KR, full, CH), both(R_rk[:, 0]), R_e1[:], ALU.mult)
                for rows_, at_a, at_b in ((top, 0, CH), (low_half, CH, 0)):
                    pool.drain()
                    pool.tensor_tensor(units(R_AB, rows_, at_a), both(R_sh[rows_, 0]), R_e2[rows_], ALU.mult)
                    pool.tensor_tensor(units(R_AB, rows_, at_b), both(R_rk[rows_, 1]), R_e2[rows_], ALU.mult)
                pool.drain().then_inc(ab_ready, 1)

            def pool_pair(t, more):
                pool.wait_ge(pair_done, t + 1)
                pool.sem_inc(passed, 1)
                pool.memset(R_UV[:], 0.0)
                pool.drain().then_inc(init_ready, 1)
                if more:
                    pool.wait_ge(rk_turned, t + 1)
                    pool.sem_inc(passed, 1)
                    next_z(t + 1)
                pool.tensor_copy(R_Kbd[0:CH, :, 0:CH], R_KR[0:CH, :, 0:CH])
                pool.tensor_copy(R_Rbd[0:CH, :, 0:CH], R_KR[0:CH, :, CH:P])
                pool.drain()
                pool.tensor_copy(R_Kbd[CH:P, :, CH:P], R_KR[CH:P, :, 0:CH])
                pool.tensor_copy(R_Rbd[CH:P, :, CH:P], R_KR[CH:P, :, CH:P])
                pool.drain().then_inc(krbd_ready, 1)
                for lv in range(2, LEVELS):
                    pool.wait_ge(first_ready if lv == 2 else q_done, t + 1 if lv == 2 else t * (LEVELS - 1) + lv - 2)
                    pool.sem_inc(passed, 1)
                    level(pool, lv)
                    pool.drain().then_inc(c_ready, 1)
                if more:
                    pool.wait_ge(ab_turned, t + 1)
                    pool.sem_inc(passed, 1)
                    next_factors(t + 1)
            next_z(0)
            next_factors(0)
            with pool.Fori(0, PAIRS - 1) as t:
                pool_pair(t, True)
            pool_pair(PAIRS - 1, False)
            pool.wait_ge(tail_done, PAIRS)
            pool.sem_inc(passed, 1)

            def gla_qk(n):
                for i in range(NT):
                    src = z[:, i, Z_Q:Z_V].rearrange("p (j n) -> p j n", n=GH * DK)
                    pool.tensor_copy(L_zs[:, i], src[:, :, bass.ds(n * DK, DK)])
                pool.drain().then_inc(gz_ready, 1)

            def gla_v(n):
                for i in range(NT):
                    pool.tensor_copy(L_v[:, i], z[:, i, bass.ds(n * DV + Z_V, DV)])
                pool.drain().then_inc(gv_ready, 1)
            gla_qk(0)
            gla_v(0)
            with pool.Fori(1, GH) as n:
                pool.wait_ge(g_turned, n)
                pool.sem_inc(passed, 1)
                gla_qk(n)
                pool.wait_ge(g_o, n)
                pool.sem_inc(passed, 1)
                gla_v(n)
            pool.wait_ge(x_ready, 2)
            pool.memset(ysum[:], 0.0).then_inc(ysum_zero, 1)
            end_pool(pool, 0)
            end_pool(pool, 1)
            pool.wait_ge(pa_free, 2 + 2 * (17 + FG + 8))
            pool.sem_inc(passed, 1)
            rotate(pool, 0, 0)
            rotate(pool, 1, 1)
            with pool.Fori(1, DH // 2) as m:
                for slot in range(2):
                    pool.wait_ge(at_turned, m * 2 + (slot - 1))
                    pool.sem_inc(passed, 1)
                    rotate(pool, m * 2 + slot, slot)
            pool.wait_ge(x_ready, 6)
            pool.memset(ysum[:], 0.0).then_inc(ysum_zero, 1)
            end_pool(pool, 2)
            pool.wait_ge(ln_in, 4 * 32)
            pool.wait_ge(x_ready, 8)
            pool.sem_inc(passed, 1)
            pool.tensor_tensor(xt[:, 1, D // 2:], xt[:, 1, D // 2:], lng[:, D // 2:], ALU.mult)
            pool.drain()
            pool.tensor_tensor(xt[:, 1, D // 2:], xt[:, 1, D // 2:], lnb[:, D // 2:], ALU.add)
            pool.drain().then_inc(x_scaled, 1)

        @block.scalar
        def _(act):
            act.wait_ge(tab_turned, 1)
            act.activation(tab[:], pa[:, 0, 0:T_N], ACT.Copy).then_inc(tab_copied, 1)
            act.wait_ge(tab_copied, 1)
            act.activation(silu_c[:], tab[:, T_C:T_C + KT], ACT.Silu).then_inc(silu_ready, 1)
            high(act, 0, 0)
            high(act, 0, 1)
            turn_act(act, 0)

            def store_z(c, width=W):
                act.wait_ge(pa_done, c + 1)
                act.activation(z[:, 0, bass.ds(c * W, width)], pa[:, 0, 0:width], ACT.Copy).then_inc(pa_free, 1)
                act.wait_ge(unit_done, c * 4 + 6)
                act.activation(z[:, 1, bass.ds(c * W, width)], pa[:, 1, 0:width], ACT.Copy).then_inc(pa_free, 1)

            with act.Fori(0, 11) as c:
                high(act, c, 2)
                high(act, c, 3)
                high(act, c + 1, 0)
                act.wait_ge(pa_done, c + 1)
                act.activation(z[:, 0, bass.ds(c * W, W)], pa[:, 0], ACT.Copy).then_inc(pa_free, 1)
                act.wait_ge(unit_done, c * 4 + 6)
                act.activation(z[:, 1, bass.ds(c * W, W)], pa[:, 1], ACT.Copy).then_inc(pa_free, 1)
                high(act, c + 1, 1)
            high(act, 11, 2)
            high(act, 11, 3)
            store_z(11)
            for s in range(4):
                high(act, 12, s, LASTW)
            store_z(12, LASTW)
            act.wait_ge(bd_zero, 1)
            act.wait_ge(lora_turned, 1)
            pad4 = R_G[:].rearrange("p a b c -> p (a b c)")[:, 0:4 * (SEQ + 2)].rearrange("p (j t) -> p j t", t=SEQ + 2)
            act.activation(pad4[0:LORA, 0:2, 1:1 + SEQ], py[0:LORA, 0].rearrange("p (j t) -> p j t", t=SEQ), ACT.Copy)
            act.activation(pad4[:, 2:4, 1:1 + SEQ], py[:, 1].rearrange("p (j t) -> p j t", t=SEQ),
                           ACT.Copy).then_inc(lora_padded, 1)
            act.wait_ge(lora_mixed, 1)
            act.activation(R_lora[0:LORA, 0], R_lora[0:LORA, 0], ACT.Tanh).then_inc(lora_ready, 1)
            act.activation(R_lora[:, 2:4], R_lora[:, 2:4], ACT.Sigmoid).then_inc(lora_ready, 1)

            w_up_v = rwkv_w_up[0].rearrange("a r n -> r a n")
            g_up_v = rwkv_g_up[0].rearrange("(i p) n -> p i n", p=P)

            def next_act(n, piece):
                if piece == 0:
                    if not (isinstance(n, int) and n == 0):
                        act.wait_ge(up_done, n)
                    act.dma_start(R_up[0:LORA, 0:2, :], w_up_v[:, :, bass.ds(n * P, P)]).then_inc(up_in, 16)
                    act.dma_start(R_up[0:LORA, 2, :], rwkv_a_up[0][:, bass.ds(n * P, P)]).then_inc(up_in, 16)
                    act.dma_start(R_up[:, 3:5, :], g_up_v[:, :, bass.ds(n * P, P)]).then_inc(up_in, 16)
                    act.wait_ge(rk_turned, n + 1)
                    if not (isinstance(n, int) and n == 0):
                        act.wait_ge(rkv_mixed, n)
                    act.activation(R_zf[:, 0:2, 1:1 + SEQ], pb[:, 0].rearrange("p (j t) -> p j t", t=SEQ), ACT.Copy)
                    act.activation(R_zf[:, 2, 1:1 + SEQ], pb[:, 1, 0:SEQ], ACT.Copy).then_inc(zf_ready, 1)
                elif piece == 1:
                    act.wait_ge(up_done, n + 1)
                    if not (isinstance(n, int) and n == 0):
                        act.wait_ge(ab_ready, n)
                    for j in range(2):
                        act.activation(R_lw[:, j], pb[:, 0, j * SEQ:(j + 1) * SEQ], ACT.Sigmoid,
                                       bias=tab[:, bass.ds(n + (T_W0 + 8 * j), 1)])
                elif piece == 2:
                    act.activation(R_lw[:, 2], pb[:, 1, 0:SEQ], ACT.Sigmoid, bias=tab[:, bass.ds(n + (T_W0 + 16), 1)])
                    act.activation(R_gn[:], pb[:, 1, SEQ:W], ACT.Copy).then_inc(up_act, 1)
                elif piece == 3:
                    act.wait_ge(ss_clamped, n + 1)
                    act.activation(R_sh[:, 1], R_sh[:, 1], ACT.Ln, scale=65536.0)
                    act.drain()
                elif piece == 4:
                    act.activation(R_sh[:, 1], R_sh[:, 1], ACT.Exp, scale=-0.5).then_inc(rn_ready, 1)
                elif piece == 5:
                    act.wait_ge(logs_ready, n + 1)
                    act.activation(R_e1[:], R_b[:], ACT.Exp)
                    act.activation(R_e2[:], R_b[:], ACT.Exp, scale=-1.0)
                else:
                    act.activation(R_lw[:, 0:2], R_lw[:, 0:2], ACT.Exp).then_inc(exps_ready, 1)

            def act_tail(t):
                act.wait_ge(ys_var, t + 1)
                act.activation(small[:, 20:24], small[:, 16:20], ACT.Ln)
                act.drain()
                act.activation(small[:, 24:28], small[:, 20:24], ACT.Exp, scale=-0.5).then_inc(ys_rstd, 1)

            def act_pair(t, more, tail=True):
                if tail:
                    act_tail(t - 1)
                act.wait_ge(pair_done, t + 1)
                act.wait_ge(exps_ready, t + 1)
                act.activation(R_dec[:, 0], R_e1[:, 0].rearrange("p (c n) -> p c n", n=CH)[:, :, CH - 1], ACT.Copy)
                act.activation(R_dec[:, 1], R_e1[:, 1].rearrange("p (c n) -> p c n", n=CH)[:, :, 0], ACT.Copy)
                act.wait_ge(v_turned, t + 1)
                act.wait_ge(init_ready, t + 1)
                for d in range(2):
                    us = slice(d * NCH, (d + 1) * NCH)
                    act.activation(R_UV[CH:P, 0, us], pt[CH:P, 0].rearrange("p (c n) -> p c n", n=P)[:, :, 0:CH], ACT.Copy)
                    ins = act.activation(R_UV[0:CH, 1, us], pt[0:CH, 1].rearrange("p (c n) -> p c n", n=P)[:, :, CH:P],
                                         ACT.Copy)
                ins.then_inc(uv_ready, 1)
                act.wait_ge(ab_turned, t + 1)
                for d in range(2):
                    ins = act.activation(R_ABt[:, d * NCH:(d + 1) * NCH].rearrange("p u c -> p (u c)"), pt[:, d], ACT.Copy)
                ins.then_inc(abt_ready, 1)

                def ahead(lv, point):
                    if more and (lv, point) in ACT_AT:
                        next_act(t + 1, ACT_AT[lv, point])
                for lv in range(1, LEVELS):
                    if lv == 1:
                        act.wait_ge(v_done, t * (LEVELS - 1) + 1)
                        act.activation(R_Vbd[0:CH, :, 0:CH], tiles(pt, 0), ACT.Copy).then_inc(vc_ready, 1)
                        if tail:
                            act.wait_ge(tail_done, t)
                        act.activation(R_g[:], R_gn[:], ACT.Copy).then_inc(kept_ready, 1)
                        if more:
                            next_act(t + 1, 0)
                    act.wait_ge(q_done, t * (LEVELS - 1) + lv)
                    act.activation(R_Qbd[0:CH, :, 0:CH], tiles(py, 0), ACT.Copy).then_inc(qc_ready, 1)
                    ahead(lv, 0)
                    if lv < LEVELS - 1:
                        act.wait_ge(v_done, t * (LEVELS - 1) + lv + 1)
                        act.activation(R_Vbd[0:CH, :, 0:CH], tiles(pt, 0), ACT.Copy).then_inc(vc_ready, 1)
                        ahead(lv, 1)
                    act.wait_ge(w_done, t * (LEVELS - 1) + lv)
                    if lv < LEVELS - 1:
                        act.activation(flat(R_wc)[0:CH], pa[0:CH, 0], ACT.Copy).then_inc(wc_ready, 1)
                    else:
                        act.activation(R_Wbd[0:CH, :, 0:CH], pa[0:CH, 0].rearrange("p (u n) -> p u n", n=CH),
                                       ACT.Copy).then_inc(wbd_ready, 1)
                    ahead(lv, 2)
                for i in range(NCH):
                    u = NCH + NCH - 1 - i
                    act.wait_ge(x_done[1], t * NCH + i + 1)
                    act.activation(R_X[:, 1], pb[:, 1, (u % NCH) * CH:(u % NCH + 1) * CH], ACT.Copy).then_inc(xs_ready[1], 1)
                    act.wait_ge(u_done[1], t * NCH + i + 1)
                    act.activation(R_UV[0:CH, 0, u], py[0:CH, 1, 0:CH], ACT.Copy, scale=-1.0)
                    act.activation(R_UV[CH:P, 1, u], py[CH:P, 1, 0:CH], ACT.Copy, scale=-1.0).then_inc(u_ready[1], 1)
            for piece in range(7):
                next_act(0, piece)
            act_pair(0, True, False)
            with act.Fori(1, PAIRS - 1) as t:
                act_pair(t, True)
            act_pair(PAIRS - 1, False)
            act_tail(PAIRS - 1)
            for i in range(NT):
                act.activation(z[:, i, Z_OG:Z], z[:, i, Z_OG:Z], ACT.Silu).then_inc(og_ready, 1)
            act.wait_ge(tail_done, PAIRS)
            act.wait_ge(gg_turned, 1)
            act.activation(L_gg[0:GLORA], py[0:GLORA, 1, 0:SEQ], ACT.Copy).then_inc(gg_ready, 1)

            def gla_next_act(n):
                act.wait_ge(g_turned, n + 1)
                if not (isinstance(n, int) and n == 0):
                    act.wait_ge(g_prod, n)
                act.activation(L_qk[:].rearrange("p j t -> p (j t)"), pt[:, 0], ACT.Copy).then_inc(g_qk, 1)
                act.wait_ge(g_x, n + 1)
                act.activation(L_t[:], L_t[:], ACT.Exp, scale=-1.0)
                act.drain()

            def gla_next_ln(n):
                act.activation(L_t[:], L_t[:], ACT.Ln, bias=1.0).then_inc(g_soft, 1)

            def gla_act(t, more):
                act.wait_ge(g_logs, t + 1)
                act.activation(L_e1[:], L_b[:], ACT.Exp)
                act.activation(L_e2[:], L_b[:], ACT.Exp, scale=-1.0)
                for d in range(2):
                    for c in range(NCH):
                        end = c * CH + (CH - 1 if d == 0 else 0)
                        ins = act.activation(L_e3[:, d, c * CH:(c + 1) * CH], L_b[:, d, c * CH:(c + 1) * CH], ACT.Exp,
                                             scale=-1.0, bias=L_b[:, d, end:end + 1])
                ins.then_inc(g_exps, 1)
                act.wait_ge(g_kdt_done, t + 1)
                act.activation(L_kdt[:].rearrange("p d i n -> p (d i n)"), pt[:, 1], ACT.Copy).then_inc(g_kdt, 1)
                if more:
                    gla_next_act(t + 1)
                act.wait_ge(g_o, t + 1)
                for i in range(NT):
                    act.activation(L_sq[:, i], pa[:, 1, i * DV:(i + 1) * DV], ACT.Square, accum_out=small[:, 28 + i:29 + i])
                act.drain().then_inc(g_sq, 1)
                if more:
                    gla_next_ln(t + 1)
                act.wait_ge(g_var, t + 1)
                act.activation(small[:, 30:32], small[:, 28:30], ACT.Ln)
                act.drain()
                act.activation(small[:, 32:34], small[:, 30:32], ACT.Exp, scale=-0.5).then_inc(g_rstd, 1)
            gla_next_act(0)
            gla_next_ln(0)
            with act.Fori(0, GH - 1) as t:
                gla_act(t, True)
            gla_act(GH - 1, False)
            act.wait_ge(head_done, 1 + GH)
            split_act(act, 0)
            act.wait_ge(split_lo, 8)
            act.dma_start(xt[:], x_in[0].rearrange("(i p) d -> p i d", p=P)).then_inc(x_in_sem, 16)
            out_act(act, 13, 13, 0)
            high(act, C_FFN0, 0)
            high(act, C_FFN0, 1)
            end_act(act, 0)
            turn_act(act, 1)
            ffn_act(act, C_FFN0, 0, 17, 1)
            high(act, C_DIFF, 0)
            high(act, C_DIFF, 1)
            end_act(act, 1)
            turn_act(act, 2)
            in_act(act, C_DIFF, qkv)
            act.wait_ge(unit_done, 2 + 4 * C_OUT1)
            act.dma_start(A_lam[0:1, 0:256], diff_lambda.rearrange("a b n -> a (b n)")).then_inc(lam_in, 16)
            act.wait_ge(lam_prod, 1)
            act.activation(A_lam[0:1, 258:260], A_lam[0:1, 256:258], ACT.Exp).then_inc(lam_exp, 1)

            def exps(h, slot, first=False):
                if not first:
                    act.wait_ge(at_pturned, h)
                act.wait_ge(at_bias, h + 1)
                for c in range(2):
                    for i in range(NT):
                        m = 2 * c + i
                        act.activation(A_p[:, slot, c, i], py[:, c, i * SEQ:(i + 1) * SEQ], ACT.Exp, scale=0.125,
                                       bias=A_s[:, slot, 4 + m:5 + m], accum_out=A_s[:, slot, 8 + m:9 + m])
                act.drain().then_inc(at_exp, 1)

            def turned_qk(h, first=False):
                if not first:
                    act.wait_ge(at_scores, h)
                act.wait_ge(at_turned, h + 1)
                act.activation(A_qkT[:].rearrange("p j t -> p (j t)"), pt[:, 0], ACT.Copy).then_inc(at_T, 1)

            def act_head(h, slot, more):
                if more == 2:
                    turned_qk(h + 2)
                act.wait_ge(at_pturned, h + 1)
                act.activation(A_pT[:].rearrange("p k t -> p (k t)"), pt[:, 1], ACT.Copy).then_inc(at_pT, 1)
                if more:
                    exps(h + 1, 1 - slot)
                act.drain()
                act.wait_ge(at_out, h + 1)
                for i in range(NT):
                    if i:
                        act.drain()
                    act.activation(A_sq[:], qkv[:, i, bass.ds(h * P, P)], ACT.Square,
                                   accum_out=A_ss[:, i, bass.ds(h, 1)])
            turned_qk(0, first=True)
            turned_qk(1)
            exps(0, 0, first=True)
            heads(act, act_head)
            act.drain().then_inc(at_sq, 1)
            act.wait_ge(at_var, 1)
            act.activation(A_ss[:], A_ss[:], ACT.Ln)
            act.drain()
            act.activation(A_rs[:], A_ss[:], ACT.Exp, scale=-0.5).then_inc(at_rstd, 1)
            for m in range(DH // 2):
                act.wait_ge(at_scaled, m + 1)
                act.activation(hth[:, 2 * m:2 * m + 2], A_t2[:, m % 2], ACT.Copy).then_inc(at_hi, 1)
            out_act(act, C_OUT1, 17 + FG + 12, 2)
            high(act, C_FFN1, 0)
            high(act, C_FFN1, 1)
            end_act(act, 2)
            turn_act(act, 3)
            ffn_act(act, C_FFN1, FG, n_of[FG], 3)
            end_act(act, 3)

        @block.vector
        def _(dve):
            dve.sem_inc(lo_done, 4)
            dve.sem_inc(ada_step, 1)
            dve.wait_ge(tab_copied, 1)
            dve.tensor_scalar(hmu[:], tab[:, T_MU:T_MU + 28], 0.5, None, ALU.mult)
            dve.tensor_scalar(omu[:], tab[:, T_MU:T_MU + 28], -1.0, 1.0, ALU.mult, ALU.add)
            dve.tensor_scalar(neg[:, 0:24], tab[:, T_W0:T_W0 + 24], -1.0, None, ALU.mult)
            dve.tensor_scalar(neg[:, 24:32], tab[:, T_KA:T_KA + 8], -1.0, 1.0, ALU.mult, ALU.add)
            dve.wait_ge(silu_ready, 1)
            for s in range(4):
                cond_unit(dve, 0, s, raw)
            cond_sum(dve, 0, first=True)
            with dve.Fori(1, 8) as j:
                cond_unit(dve, j, 0, raw)
                cond_unit(dve, j, 1, raw)
                cond_store(dve, j - 1)
                cond_unit(dve, j, 2, raw)
                cond_unit(dve, j, 3, raw)
                cond_sum(dve, j)
            cond_store(dve, 7)
            dve.drain()
            factors_dve(dve, 0)
            low(dve, 0, 0)
            low(dve, 0, 1)
            turn_dve(dve, 0)
            low(dve, 0, 2)
            low(dve, 0, 3)
            with dve.Fori(1, 12) as c:
                for s in range(4):
                    low(dve, c, s)
            for s in range(4):
                low(dve, 12, s, LASTW)
            dve.wait_ge(lora_padded, 1)
            pad4 = R_G[:].rearrange("p a b c -> p (a b c)")[:, 0:4 * (SEQ + 2)].rearrange("p (j t) -> p j t", t=SEQ + 2)
            for lo, hi, n in ((0, 2, LORA), (2, 4, P)):
                dve.tensor_tensor(R_lora[0:n, lo:hi], pad4[0:n, lo:hi, 0:SEQ], pad4[0:n, lo:hi, 2:2 + SEQ], ALU.add)
            dve.drain()
            for j in range(4):
                n = LORA if j < 2 else P
                dve.tensor_scalar(R_lora[0:n, j], R_lora[0:n, j], hmu[0:n, 24 + j:25 + j], None, ALU.mult)
            dve.drain()
            for j in range(4):
                n = LORA if j < 2 else P
                ins = dve.scalar_tensor_tensor(R_lora[0:n, j], pad4[0:n, j, 1:1 + SEQ], omu[0:n, 24 + j:25 + j],
                                               R_lora[0:n, j], ALU.mult, ALU.add)
            ins.then_inc(lora_mixed, 1)
            dve.drain().then_inc(lora_ready, 1)
            dve.sem_inc(pair_done, 1)
            top, low_half = slice(0, CH), slice(CH, P)

            def next_dve(n, piece):
                if piece == 0:
                    dve.wait_ge(zf_ready, n + 1)
                    if not (isinstance(n, int) and n == 0):
                        dve.wait_ge(ab_ready, n)
                    dve.tensor_tensor(R_sh[:], R_zf[:, :, 0:SEQ], R_zf[:, :, 2:2 + SEQ], ALU.add)
                    dve.drain()
                    for j in range(3):
                        dve.tensor_scalar(R_sh[:, j], R_sh[:, j], hmu[:, bass.ds(n + 8 * j, 1)], None, ALU.mult)
                    dve.drain()
                elif piece == 1:
                    if not (isinstance(n, int) and n == 0):
                        dve.wait_ge(v_turned, n)
                    for j in range(3):
                        o = R_rk[:, j] if j < 2 else R_vp[:, CH:CH + SEQ]
                        dve.scalar_tensor_tensor(o, R_zf[:, j, 1:1 + SEQ], omu[:, bass.ds(n + 8 * j, 1)], R_sh[:, j],
                                                 ALU.mult, ALU.add)
                    dve.drain().then_inc(rkv_mixed, 1)
                    dve.tensor_scalar(R_kk[:], R_rk[:, 1], tab[:, bass.ds(n + T_KK, 1)], None, ALU.mult)
                    dve.drain()
                    dve.tensor_tensor(R_sh[:, 0], R_kk[:], R_kk[:], ALU.mult).then_inc(sq_ready, 1)
                elif piece == 2:
                    dve.wait_ge(up_act, n + 1)
                    dve.tensor_scalar(R_lw[:, 0:2], R_lw[:, 0:2], -DECAY, None, ALU.mult)
                    dve.drain()
                    reset = cst[:, C_RESET:C_RESET + SEQ]
                    dve.tensor_tensor_scan(R_b[:, 0], reset, R_lw[:, 0], 0.0, ALU.mult, ALU.add)
                    dve.tensor_tensor_scan(R_b[:, 1][:, ::-1], reset, R_lw[:, 1][:, ::-1], 0.0, ALU.mult, ALU.add)
                elif piece == 3:
                    dve.wait_ge(ss_done, n + 1)
                    dve.tensor_scalar(R_sh[:, 1], pb[:, 0, 0:SEQ], 1e-24, None, ALU.max).then_inc(ss_clamped, 1)
                    dve.drain()
                    dve.tensor_tensor(R_lw[:, 0:2], R_b[:], R_lw[:, 0:2], ALU.subtract).then_inc(logs_ready, 1)
                elif piece == 4:
                    dve.tensor_scalar(R_sh[:, 2], R_lw[:, 2], tab[:, bass.ds(n + T_KA, 1)], neg[:, bass.ds(n + 24, 1)],
                                      ALU.mult, ALU.add)
                    dve.drain()
                    dve.tensor_tensor(R_rk[:, 1], R_rk[:, 1], R_sh[:, 2], ALU.mult)
                    dve.wait_ge(rn_ready, n + 1)
                    dve.scalar_tensor_tensor(R_kk[:], R_kk[:], 256.0, R_sh[:, 1], ALU.mult, ALU.mult)
                    dve.drain()
                    dve.tensor_tensor(R_sh[:, 0], R_kk[:], R_lw[:, 2], ALU.mult)
                    dve.scalar_tensor_tensor(R_sh[:, 1], R_rk[:, 0], tab[:, bass.ds(n + T_RK, 1)], R_rk[:, 1],
                                             ALU.mult, ALU.mult)
                    dve.drain().then_inc(q_ready, 1)

            def normed(t):
                cond_store(dve, t * 2 + 9, pb[:, 1, SEQ:SEQ + 4])
                dve.wait_ge(ys_rstd, t + 1)
                for h, r in enumerate((top, low_half)):
                    for c in range(NCH):
                        dve.tensor_scalar(R_Vbd[r, c, h * CH:(h + 1) * CH], R_y[r, c], R_mv[r, c, 0:1], small[r, 24 + c:25 + c],
                                          ALU.subtract, ALU.mult)
                dve.drain().then_inc(ybd_ready, 1)

            def finish(t):
                dve.wait_ge(yt_done, t + 1)
                dve.tensor_scalar(flat(R_y), pb[:, 1, 0:SEQ], tab[:, bass.ds(t + T_GNG, 1)], tab[:, bass.ds(t + T_GNB, 1)],
                                  ALU.mult, ALU.add)
                dve.drain()
                dve.tensor_tensor(flat(R_y), flat(R_y), R_bonus[:], ALU.add)
                dve.drain()
                dve.tensor_tensor(xf[:, bass.ds(t, 1), :], flat(R_y).unsqueeze(1), R_g[:].unsqueeze(1), ALU.mult)
                dve.drain().then_inc(tail_done, 1)

            def dve_pair(t, more, tail=True):
                if tail:
                    normed(t - 1)

                def cond_pair(a, b):
                    for j in range(2):
                        lo, hi = max(a - 17 * j, 0), min(b - 17 * j, 17)
                        cond_steps(dve, t * 2 + (8 + j), lo, min(hi, 16))
                        if lo <= 16 < hi:
                            cond_sum(dve, t * 2 + (8 + j))
                for d in range(2):
                    mask = cst[:, C_SCORE + d * P:C_SCORE + (d + 1) * P].unsqueeze(1).to_broadcast((P, NCH, P))
                    for h, bank in enumerate((py, pa)):
                        k = 2 * d + h
                        cond_pair(S_AT[k], S_AT[k + 1])
                        dve.wait_ge(scores_done, t * 4 + 2 * d + h + 1)
                        dve.tensor_tensor(R_G[:, h, d * NCH:(d + 1) * NCH],
                                          bank[:, d].rearrange("p (c n) -> p c n", n=P), mask, ALU.mult)
                dve.drain().then_inc(g_ready, 1)

                level(dve, 0)
                dve.drain()
                dve.tensor_tensor(R_wc[:], R_C[:, 0], cst[:, C_I2:C_I2 + CH].unsqueeze(1).to_broadcast((P, NU, CH)),
                                  ALU.add).then_inc(first_ready, 1)
                if tail:
                    finish(t - 1)
                dve.wait_ge(bonus_done, t + 1)
                dve.tensor_tensor(R_bonus[:], pb[:, 0, SEQ:W], R_vp[:, CH:CH + SEQ], ALU.mult).then_inc(bonus_out, 1)
                level(dve, 1).then_inc(c1_ready, 1)

                def ahead(lv, point):
                    k = 3 * (lv - 1) + point
                    cond_pair(L_AT[k], L_AT[k + 1])
                    if more and (lv, point) in DVE_AT:
                        next_dve(t + 1, DVE_AT[lv, point])
                for lv in range(1, LEVELS):
                    if lv == 1:
                        dve.wait_ge(v_done, t * (LEVELS - 1) + 1)
                        dve.tensor_copy(R_Vbd[low_half, :, CH:P], tiles(pt, 1)).then_inc(vc_ready, 1)
                    dve.wait_ge(q_done, t * (LEVELS - 1) + lv)
                    dve.tensor_copy(R_Qbd[low_half, :, CH:P], tiles(py, 1)).then_inc(qc_ready, 1)
                    ahead(lv, 0)
                    if lv < LEVELS - 1:
                        dve.wait_ge(v_done, t * (LEVELS - 1) + lv + 1)
                        dve.tensor_copy(R_Vbd[low_half, :, CH:P], tiles(pt, 1)).then_inc(vc_ready, 1)
                        ahead(lv, 1)
                    dve.wait_ge(w_done, t * (LEVELS - 1) + lv)
                    if lv < LEVELS - 1:
                        dve.tensor_copy(flat(R_wc)[low_half], pa[low_half, 1]).then_inc(wc_ready, 1)
                    else:
                        dve.tensor_copy(R_Wbd[CH:P, :, CH:P], pa[CH:P, 1].rearrange("p (u n) -> p u n", n=CH)).then_inc(wbd_ready, 1)
                    ahead(lv, 2)
                dve.wait_ge(kept_ready, t + 1)
                for i in range(NCH):
                    u = i
                    dve.wait_ge(x_done[0], t * NCH + i + 1)
                    dve.tensor_copy(R_X[:, 0], pb[:, 0, u * CH:(u + 1) * CH]).then_inc(xs_ready[0], 1)
                    cond_pair(X_AT[i], X_AT[i + 1])
                    dve.wait_ge(u_done[0], t * NCH + i + 1)
                    dve.tensor_scalar(R_UV[0:CH, 0, u], py[0:CH, 0, 0:CH], -1.0, None, ALU.mult)
                    dve.tensor_scalar(R_UV[CH:P, 1, u], py[CH:P, 0, 0:CH], -1.0, None, ALU.mult).then_inc(u_ready[0], 1)
                    if i == NCH - 1:
                        break
                    for d in range(2):
                        c = i if d == 0 else NCH - 1 - i
                        dve.wait_ge(s_done[d], t * (NCH - 1) + i + 1)
                        decay = R_dec[:, d, c:c + 1]
                        if i:
                            dve.tensor_tensor(R_S[:, d], R_S[:, d], pa[:, d, 0:CH], ALU.add)
                            dve.drain()
                            dve.tensor_scalar(R_S[:, d], R_S[:, d], decay, None, ALU.mult).then_inc(s_ready[d], 1)
                        else:
                            dve.tensor_scalar(R_S[:, d], pa[:, d, 0:CH], decay, None, ALU.mult).then_inc(s_ready[d], 1)
                dve.wait_ge(y_done[0], t + 1)
                dve.wait_ge(y_done[1], t + 1)
                dve.tensor_copy(flat(R_y), pt[:, 0, 0:SEQ]).then_inc(pair_done, 1)
                dve.drain()
                for c in range(NCH):
                    dve.bn_stats(R_st[:, c], R_y[:, c])
                dve.drain()
                for c in range(NCH):
                    dve.bn_aggr(R_mv[:, c], R_st[:, c])
                dve.drain()
                dve.tensor_scalar(small[:, 16:20], R_mv[:, :, 1], GN_EPS, None, ALU.add).then_inc(ys_var, 1)
                cond_store(dve, t * 2 + 8, pb[:, 1, SEQ:SEQ + 4])
                cond_pair(X_AT[NCH], 34)
            for piece in range(5):
                next_dve(0, piece)
            dve_pair(0, True, False)
            with dve.Fori(1, PAIRS - 1) as t:
                dve_pair(t, True)
            dve_pair(PAIRS - 1, False)
            normed(PAIRS - 1)
            finish(PAIRS - 1)
            dve.sem_inc(head_done, 1)
            dve.wait_ge(og_ready, 2)

            xx, tt = (v[:].rearrange("p d t -> p (d t)") for v in (L_x, L_t))

            def gla_logits(n):
                dve.wait_ge(g_gate, n + 1)
                for d in range(2):
                    dve.tensor_scalar(L_x[:, d], pa[:, 0, d * SEQ:(d + 1) * SEQ], tab[:, bass.ds(n + T_GB + d * GH, 1)], None, ALU.add)
                dve.drain()
                dve.scalar_tensor_tensor(tt, xx, -1.0, xx, ALU.mult, ALU.max).then_inc(g_x, 1)
                dve.drain()
                dve.tensor_scalar(xx, xx, 0.0, 1.0 / 16, ALU.min, ALU.mult)

            def gla_logs(n):
                dve.drain()
                dve.wait_ge(g_soft, n + 1)
                dve.scalar_tensor_tensor(xx, tt, -1.0 / 16, xx, ALU.mult, ALU.add)
                dve.drain()
                if not (isinstance(n, int) and n == 0):
                    dve.wait_ge(g_exps, n)
                reset = cst[:, C_RESET:C_RESET + SEQ]
                dve.tensor_tensor_scan(L_b[:, 0], reset, L_x[:, 0], 0.0, ALU.mult, ALU.add)
                dve.tensor_tensor_scan(L_b[:, 1][:, ::-1], reset, L_x[:, 1][:, ::-1], 0.0, ALU.mult, ALU.add).then_inc(g_logs, 1)

            def gla_dve(t, more):
                dve.wait_ge(g_qk, t + 1)
                dve.wait_ge(g_exps, t + 1)
                for d in range(2):
                    dve.scalar_tensor_tensor(L_qb[:, d], L_qk[:, 0], float(DK) ** -0.5, L_e1[:, d], ALU.mult, ALU.mult)
                kk2 = L_qk[:, 1:2].to_broadcast((P, 2, SEQ))
                dve.tensor_tensor(L_kb[:], kk2, L_e2[:], ALU.mult)
                dve.tensor_tensor(L_kd[:], kk2, L_e3[:], ALU.mult).then_inc(g_prod, 1)
                dve.wait_ge(g_att, t + 1)
                for d in range(2):
                    ins = dve.scalar_tensor_tensor(
                        L_att[:, d], pb[:, 0, d * SEQ:(d + 1) * SEQ].rearrange("p (i n) -> p i n", n=P), 3e38,
                        cst[:, C_GLA + d * P:C_GLA + (d + 1) * P].unsqueeze(1).to_broadcast((P, NT, P)), ALU.min, ALU.mult)
                ins.then_inc(g_attm, 1)
                dve.wait_ge(g_kv, t + 1)
                place = {(0, 0): py[:, 0, 0:DV], (0, 1): py[:, 1, 0:DV], (0, 2): py[:, 0, DV:2 * DV],
                         (1, 3): py[:, 1, DV:2 * DV], (1, 2): pa[:, 0, 0:DV], (1, 1): pb[:, 1, 0:DV]}
                for i in range(NCH - 1):
                    for d in range(2):
                        c = i if d == 0 else NCH - 1 - i
                        end = c * CH + (CH - 1 if d == 0 else 0)
                        if i == 0:
                            ins = dve.tensor_copy(L_S[:, d, 0], place[d, c])
                        else:
                            ins = dve.scalar_tensor_tensor(L_S[:, d, i], L_S[:, d, i - 1], L_e1[:, d, end:end + 1],
                                                           place[d, c], ALU.mult, ALU.add)
                    dve.drain()
                dve.drain().then_inc(g_states, 1)
                if more:
                    gla_logits(t + 1)
                dve.wait_ge(g_sq, t + 1)
                dve.tensor_scalar(small[:, 28:30], small[:, 28:30], 1.0 / DV, EPS, ALU.mult, ALU.add).then_inc(g_var, 1)
                dve.wait_ge(g_rstd, t + 1)
                for i in range(NT):
                    ins = dve.scalar_tensor_tensor(L_o[:, i], pa[:, 1, i * DV:(i + 1) * DV], small[:, 32 + i:33 + i],
                                                   z[:, i, bass.ds(t * DV + Z_OG, DV)], ALU.mult, ALU.mult)
                ins.then_inc(g_on, 1)
                if more:
                    gla_logs(t + 1)
                dve.wait_ge(g_oT, t + 1)
                for j in range(2):
                    dve.tensor_scalar(xf[:, bass.ds(t * 2 + 8 + j, 1), :], pt[:, 0:1, j * SEQ:(j + 1) * SEQ],
                                      tab[:, T_NG + j:T_NG + j + 1], None, ALU.mult)
                dve.drain().then_inc(head_done, 1)
            gla_logits(0)
            gla_logs(0)
            with dve.Fori(0, GH - 1) as t:
                gla_dve(t, True)
            gla_dve(GH - 1, False)
            split_dve(dve, 0)
            dve.wait_ge(x_in_sem, 32)
            out_dve(dve, 13, 13, 0)
            end_dve(dve, 0, C_FFN0)
            turn_dve(dve, 1)
            ffn_dve(dve, C_FFN0, 0, 0, 1, 24)
            end_dve(dve, 1, C_DIFF)
            turn_dve(dve, 2)
            for u in range(2, 10):
                low(dve, u // 4 + C_DIFF, u % 4)
                cond_unit(dve, 46 + (u - 2) // 4, (u - 2) % 4)
                if u == 5:
                    cond_sum(dve, 46)
            cond_store(dve, 46)
            cond_sum(dve, 47)
            low(dve, 2 + C_DIFF, 2)
            low(dve, 2 + C_DIFF, 3)
            with dve.Fori(3, 12) as t:
                for s in range(4):
                    low(dve, t + C_DIFF, s)
            cond_store(dve, 47)
            dve.wait_ge(lam_in, 16)
            lam4 = A_lam[0:1, 0:256].rearrange("p (a b n) -> p a b n", a=2, b=2)
            dve.tensor_tensor(lam4[:, :, 0], lam4[:, :, 0], lam4[:, :, 1], ALU.mult)
            dve.drain()
            dve.tensor_reduce(A_lam[0:1, 256:258], lam4[:, :, 0], AX_X, ALU.add).then_inc(lam_prod, 1)
            dve.wait_ge(lam_exp, 1)
            dve.tensor_tensor(A_lam[0:1, 260:261], A_lam[0:1, 259:260], A_lam[0:1, 258:259], ALU.subtract)
            dve.drain()
            dve.tensor_scalar(A_lam[0:1, 261:262], A_lam[0:1, 260:261], LAMBDA_INIT, None, ALU.subtract)
            dve.drain().then_inc(lam_prod, 1)
            dve.wait_ge(lam_mm, 1)
            dve.tensor_copy(small[:, 74:75], pb[:, 1, 0:1])
            dve.tensor_scalar(small[:, 75:76], tab[:, T_SUB:T_SUB + 1], 1.0 - LAMBDA_INIT, None, ALU.mult)
            dve.drain()
            dve.wait_ge(pa_free, 2 + 2 * (17 + FG + 12))

            def maxima(h, slot):
                dve.wait_ge(at_scores, h + 1)
                for c in range(2):
                    dve.tensor_reduce(A_s[:, slot, 2 * c:2 * c + 2], py[:, c].rearrange("p (i k) -> p i k", k=SEQ), AX_X, ALU.max)
                dve.drain()
                dve.tensor_scalar(A_s[:, slot, 4:8], A_s[:, slot, 0:4], -0.125, None, ALU.mult).then_inc(at_bias, 1)

            def dve_head(h, slot, more):
                dve.wait_ge(at_exp, h + 1)
                dve.reciprocal(A_s[:, slot, 8:12], A_s[:, slot, 8:12])
                dve.drain()
                dve.tensor_scalar(A_s[:, slot, 10:12], A_s[:, slot, 10:12], small[:, 74:75], None, ALU.mult)
                for i in range(NT):
                    dve.tensor_scalar(A_p[:, slot, 0, i], A_p[:, slot, 0, i], A_s[:, slot, 8 + i:9 + i], None, ALU.mult)
                dve.drain()
                for i in range(NT):
                    ins = dve.scalar_tensor_tensor(A_p[:, slot, 0, i], A_p[:, slot, 1, i], A_s[:, slot, 10 + i:11 + i],
                                                   A_p[:, slot, 0, i], ALU.mult, ALU.add)
                ins.then_inc(at_p, 1)
                if more:
                    maxima(h + 1, 1 - slot)
                dve.wait_ge(at_o, h + 1)
                dve.tensor_copy(qkv[:, :, bass.ds(h * P, P)], pa[:, 0, 0:NT * P].rearrange("p (i n) -> p i n", n=P)).then_inc(at_out, 1)
            maxima(0, 0)
            heads(dve, dve_head)
            dve.wait_ge(at_sq, 1)
            dve.tensor_scalar(A_ss[:], A_ss[:], 1.0 / P, EPS, ALU.mult, ALU.add).then_inc(at_var, 1)
            dve.wait_ge(at_rstd, 1)

            def normed(m):
                if m >= 2:
                    dve.wait_ge(at_oT, m - 1)
                for h in range(2):
                    for i in range(NT):
                        ins = dve.tensor_scalar(A_on[:, m % 2, i, h * P:(h + 1) * P], qkv[:, i, (2 * m + h) * P:(2 * m + h + 1) * P],
                                                A_rs[:, i, 2 * m + h:2 * m + h + 1], None, ALU.mult)
                ins.then_inc(at_on, 1)

            def lower(m):
                dve.wait_ge(at_hi, m + 1)
                dve.tensor_tensor(htl[:, 2 * m:2 * m + 2], A_t2[:, m % 2], hth[:, 2 * m:2 * m + 2].bitcast(F32),
                                  ALU.subtract).then_inc(at_done, 1)
            normed(0)
            for m in range(DH // 2):
                if m + 1 < DH // 2:
                    normed(m + 1)
                dve.wait_ge(at_oT, m + 1)
                if m >= 2:
                    dve.wait_ge(at_done, m - 1)
                dve.tensor_scalar(A_t2[:, m % 2].rearrange("p h t -> p (h t)"), pb[:, m % 2], small[:, 75:76], None,
                                  ALU.mult).then_inc(at_scaled, 1)
                if m:
                    lower(m - 1)
            lower(DH // 2 - 1)
            dve.drain()
            dve.wait_ge(at_done, DH // 2)
            out_dve(dve, C_OUT1, 17 + FG + 12, 2)
            end_dve(dve, 2, C_FFN1)
            turn_dve(dve, 3)
            ffn_dve(dve, C_FFN1, FG, 44, 3)
            end_dve(dve, 3)
            dve.wait_ge(ln_in, 4 * 32)
            dve.drain()
            parts = ((0, slice(0, D)), (1, slice(0, D // 2)))
            for i, cols in parts:
                dve.tensor_tensor(xt[:, i, cols], xt[:, i, cols], lng[:, cols], ALU.mult)
                dve.drain()
                dve.tensor_tensor(xt[:, i, cols], xt[:, i, cols], lnb[:, cols], ALU.add).then_inc(out_ready, 1)

        @block.tensor
        def _(pe):
            pe.sem_inc(unit_done, 2)
            pe.sem_inc(pa_free, 2)
            pe.wait_ge(const_in, 16)
            pe.wait_ge(rows_in, 16 * len(list(vectors())))
            for i in range(4):
                n = TABS[i + 1] - TABS[i]
                mm = pe.transpose(pa[:, 0, TABS[i]:TABS[i + 1]], rows[0:n, i, :], ident[0:n, 0:n])
            mm.then_inc(tab_turned, 1)
            cond_cols(pe, 0, first=True)
            with pe.Fori(1, 8) as j:
                cond_cols(pe, j)
            pe.wait_ge(x_in_sem, 16)
            turn_pe(pe, 0)
            project(pe, 0, 0, (hth, htl), pa_done, pa_free, pa, call=0)
            with pe.Fori(1, 12) as c:
                project(pe, c, c, (hth, htl), pa_done, pa_free, pa)
            project(pe, 12, 12, (hth, htl), pa_done, pa_free, pa, LASTW)
            pe.wait_ge(pa_free, 2 + 2 * ABC)
            for j, (a, b) in enumerate(((Z_WD, Z_AD), (Z_AD, Z_GD), (Z_GD, Z_GD + P), (Z_GD + P, Z_Q))):
                for i in range(NT):
                    at = (j % 2) * SEQ + i * P
                    mm = pe.transpose(py[0:b - a, j // 2, at:at + P], z[:, i, a:b], ident)
            mm.then_inc(lora_turned, 1)
            pe.wait_ge(lora_ready, 3)
            def next_pe(n, piece):
                if piece == 0:
                    pe.wait_ge(zs_ready, n + 1)
                    if not (isinstance(n, int) and n == 0):
                        pe.wait_ge(bonus_out, n)
                    for j in range(3):
                        for i in range(NT):
                            at = (j % 2) * SEQ + i * P
                            mm = pe.transpose(pb[:, j // 2, at:at + P], R_zs[:, i, j], ident)
                    mm.then_inc(rk_turned, 1)
                elif piece == 1:
                    pe.wait_ge(up_in, n * 48 + 48)
                    pe.wait_ge(zf_ready, n + 1)
                    for j in range(3):
                        lora = R_lora[0:LORA, 0 if j < 2 else 1]
                        pe.matmul(pb[:, j // 2, (j % 2) * SEQ:(j % 2 + 1) * SEQ], R_up[0:LORA, j], lora, start=True, stop=True)
                    for j in range(2):
                        mm = pe.matmul(pb[:, 1, SEQ:W], R_up[:, 3 + j], R_lora[:, 2 + j], start=(j == 0), stop=(j == 1))
                    mm.then_inc(up_done, 1)
                else:
                    pe.wait_ge(sq_ready, n + 1)
                    pe.wait_ge(up_act, n + 1)
                    pe.matmul(pb[:, 0, 0:SEQ], heads1, R_sh[:, 0], start=True, stop=True).then_inc(ss_done, 1)

            def pe_cols(t):
                cond_cols(pe, t * 2 + 9, bank=pb[:, 1, SEQ:SEQ + 4])

            def pe_tail(t):
                pe.wait_ge(ybd_ready, t + 1)
                for c in range(NCH):
                    mm = pe.matmul(pb[:, 1, c * CH:(c + 1) * CH], R_Vbd[:, c], cst[:, C_I2:C_I2 + CH], start=True, stop=True)
                mm.then_inc(yt_done, 1)

            def pe_pair(t, more, tail=True):
                pe.wait_ge(pair_done, t + 1)
                pe.wait_ge(rkv_mixed, t + 1)
                for h in range(2):
                    for c in range(NCH):
                        mm = pe.transpose(pt[:, h, c * P:(c + 1) * P], R_vp[:, (c + h) * CH:(c + h) * CH + P], ident)
                mm.then_inc(v_turned, 1)
                pe.wait_ge(q_ready, t + 1)
                pe.wait_ge(ss_clamped, t + 1)
                pe.matmul(pb[:, 0, SEQ:W], heads1, R_sh[:, 1], start=True, stop=True).then_inc(bonus_done, 1)
                if tail:
                    pe_cols(t - 1)
                pe.wait_ge(ab_ready, t + 1)
                for d in range(2):
                    for h, bank in enumerate((py, pa)):
                        half = slice(h * CH, (h + 1) * CH)
                        for c in range(NCH):
                            u = d * NCH + c
                            mm = pe.matmul(bank[:, d, c * P:(c + 1) * P], R_AB[half, u], R_KR[half, u], start=True, stop=True)
                        mm.then_inc(scores_done, 1)
                if tail:
                    pe_tail(t - 1)
                pe.wait_ge(uv_ready, t + 1)
                for u in range(NU):
                    mm = pe.transpose(pt[:, u // NCH, (u % NCH) * P:(u % NCH + 1) * P], R_AB[:, u], ident)
                mm.then_inc(ab_turned, 1)
                def products(bank, lhs, rhs, start):
                    for u in range(NU):
                        for h in range(2):
                            r = slice(h * CH, (h + 1) * CH)
                            mm = pe.matmul(bank[r, h, u * CH:(u + 1) * CH], lhs(u, h), rhs(u, h),
                                           start=(start or (start is None and u == 0)), stop=True,
                                           skip_group_check=True)
                    return mm

                def stacked(tile):
                    return lambda u, h: tile[:, u]

                def alone(tile):
                    return lambda u, h: tile[:, u, h * CH:(h + 1) * CH]

                def eye(u, h):
                    return ident[:, h * CH:(h + 1) * CH]
                pe.wait_ge(first_ready, t + 1)
                pe.wait_ge(abt_ready, t + 1)
                products(pt, stacked(R_wc), eye, None).then_inc(v_done, 1)
                products(pa, eye, stacked(R_wc), None)
                if more:
                    if tail:
                        pe.wait_ge(tail_done, t)
                    next_pe(t + 1, 0)
                for lv in range(1, LEVELS):
                    done = t * (LEVELS - 1) + lv
                    pe.wait_ge(c1_ready if lv == 1 else c_ready, t + 1 if lv == 1 else t * (LEVELS - 2) + lv - 1)
                    pe.wait_ge(vc_ready, 2 * done)
                    products(py, stacked(R_C[:, lv % 2]), alone(R_Vbd), True).then_inc(q_done, 1)
                    if lv > 1:
                        pe.wait_ge(wc_ready, t * 2 * (LEVELS - 2) + 2 * (lv - 1))
                    pe.wait_ge(qc_ready, 2 * done)
                    if lv < LEVELS - 1:
                        products(pt, stacked(R_wc), alone(R_Qbd), False).then_inc(v_done, 1)
                    products(pa, alone(R_Qbd), stacked(R_wc), False).then_inc(w_done, 1)
                    if more and lv in PE_AT:
                        next_pe(t + 1, PE_AT[lv])
                pe.wait_ge(wbd_ready, (t + 1) * 2)
                pe.wait_ge(krbd_ready, t + 1)
                pe.wait_ge(abt_ready, t + 1)
                if more:
                    pe.wait_ge(ss_clamped, t + 2)
                for i in range(NCH):
                    for d in range(2):
                        c = i if d == 0 else NCH - 1 - i
                        u = d * NCH + c
                        for h in range(2):
                            mm = pe.matmul(pb[h * CH:(h + 1) * CH, d, c * CH:(c + 1) * CH], R_G[:, h, u, 0:CH],
                                           R_UV[:, h, u], start=(i == 0), stop=True, skip_group_check=True)
                        if i == 0:
                            mm.then_inc(x_done[d], 1)
                    for d in range(2):
                        c = i if d == 0 else NCH - 1 - i
                        u = d * NCH + c
                        if i:
                            pe.wait_ge(s_ready[d], t * (NCH - 1) + i)
                            pe.matmul(pb[:, d, c * CH:(c + 1) * CH], R_Kbd[:, u], R_S[:, d], start=False, stop=True,
                                      skip_group_check=True).then_inc(x_done[d], 1)
                    for d in range(2):
                        c = i if d == 0 else NCH - 1 - i
                        u = d * NCH + c
                        pe.wait_ge(xs_ready[d], t * NCH + i + 1)
                        pe.matmul(py[:, d, 0:CH], R_Wbd[:, u], R_X[:, d], start=True, stop=True).then_inc(u_done[d], 1)
                    for d in range(2):
                        c = i if d == 0 else NCH - 1 - i
                        u = d * NCH + c
                        pe.wait_ge(u_ready[d], t * NCH + i + 1)
                        if i < NCH - 1:
                            for h in range(2):
                                mm = pe.matmul(pa[h * CH:(h + 1) * CH, d, 0:CH], R_ABt[:, u, h * CH:(h + 1) * CH],
                                               R_UV[:, h, u], start=True, stop=True)
                        at = slice(c * CH, (c + 1) * CH)
                        for h in range(2):
                            mm = pe.matmul(pt[h * CH:(h + 1) * CH, 0, at], R_G[:, h, u, CH:P], R_UV[:, h, u],
                                           start=(i == 0 and d == 0), stop=True, skip_group_check=True)
                        if i:
                            mm = pe.matmul(pt[:, 0, at], R_Rbd[:, u], R_S[:, d], start=False, stop=True,
                                           skip_group_check=True)
                        mm.then_inc(y_done[d] if i == NCH - 1 else s_done[d], 1)
                cond_cols(pe, t * 2 + 8, bank=pb[:, 1, SEQ:SEQ + 4])
            for piece in range(3):
                next_pe(0, piece)
            pe_pair(0, True, False)
            with pe.Fori(1, PAIRS - 1) as t:
                pe_pair(t, True)
            pe_pair(PAIRS - 1, False)
            pe_cols(PAIRS - 1)
            pe_tail(PAIRS - 1)
            pe.wait_ge(tail_done, PAIRS)
            for i in range(NT):
                mm = pe.transpose(py[0:GLORA, 1, i * P:(i + 1) * P], z[:, i, Z_GG:Z_OG], ident)
            mm.then_inc(gg_turned, 1)
            pe.wait_ge(gg_ready, 1)

            def gla_turn(n):
                pe.wait_ge(gz_ready, n + 1)
                if not (isinstance(n, int) and n == 0):
                    pe.wait_ge(head_done, n)
                for j in range(2):
                    for i in range(NT):
                        mm = pe.transpose(pt[:, 0, j * SEQ + i * P:j * SEQ + (i + 1) * P], L_zs[:, i, j], ident)
                mm.then_inc(g_turned, 1)

            def gla_gate(n):
                if not (isinstance(n, int) and n == 0):
                    pe.wait_ge(g_states, n)
                pe.wait_ge(gla_in, n * 16 + 16)
                for d in range(2):
                    mm = pe.matmul(pa[:, 0, d * SEQ:(d + 1) * SEQ], L_up[0:GLORA, d], L_gg[0:GLORA], start=True, stop=True)
                mm.then_inc(g_gate, 1)

            def gla_pe(t, more):
                pe.wait_ge(g_prod, t + 1)
                for d in range(2):
                    for i in range(NT):
                        ts_ = slice(i * P, (i + 1) * P)
                        mm = pe.matmul(pb[:, 0, (d * NT + i) * P:(d * NT + i + 1) * P], L_kb[:, d, ts_], L_qb[:, d, ts_],
                                       start=True, stop=True)
                mm.then_inc(g_att, 1)
                for d in range(2):
                    for i in range(NT):
                        mm = pe.transpose(pt[:, 1, (d * NT + i) * P:(d * NT + i + 1) * P], L_kd[:, d, i * P:(i + 1) * P], ident)
                mm.then_inc(g_kdt_done, 1)
                pe.wait_ge(g_kdt, t + 1)
                pe.wait_ge(gv_ready, t + 1)
                place = {(0, 0): py[:, 0, 0:DV], (0, 1): py[:, 1, 0:DV], (0, 2): py[:, 0, DV:2 * DV],
                         (1, 3): py[:, 1, DV:2 * DV], (1, 2): pa[:, 0, 0:DV], (1, 1): pb[:, 1, 0:DV]}
                for (d, c), bank in place.items():
                    r = slice(c % 2 * CH, c % 2 * CH + CH)
                    mm = pe.matmul(bank, L_kdt[r, d, c // 2], L_v[r, c // 2], start=True, stop=True)
                mm.then_inc(g_kv, 1)
                if more:
                    gla_turn(t + 1)
                pe.wait_ge(g_attm, t + 1)
                for i in range(NT):
                    for d in range(2):
                        pe.matmul(pa[:, 1, i * DV:(i + 1) * DV], L_att[:, d, i], L_v[:, i], start=(i == 0 and d == 0),
                                  stop=True, skip_group_check=True)
                pe.wait_ge(g_states, t + 1)
                for d in range(2):
                    for i in range(1, NCH):
                        c = i if d == 0 else NCH - 1 - i
                        mm = pe.matmul(pa[c % 2 * CH:c % 2 * CH + CH, 1, c // 2 * DV:c // 2 * DV + DV],
                                       L_qb[:, d, c * CH:(c + 1) * CH], L_S[:, d, i - 1], start=False, stop=True,
                                       skip_group_check=True)
                mm.then_inc(g_o, 1)
                if more:
                    gla_gate(t + 1)
                pe.wait_ge(g_on, t + 1)
                for j in range(2):
                    for i in range(NT):
                        mm = pe.transpose(pt[:, 0, j * SEQ + i * P:j * SEQ + (i + 1) * P], L_o[:, i, j * P:(j + 1) * P], ident)
                mm.then_inc(g_oT, 1)
            gla_turn(0)
            gla_gate(0)
            with pe.Fori(0, GH - 1) as t:
                gla_pe(t, True)
            gla_pe(GH - 1, False)
            pe.wait_ge(split_lo, 8)
            out_pe(pe, 13, 13, 0)
            pe.sem_inc(pb_free, 2)
            pe.sem_inc(py_free, 2)
            turn_pe(pe, 1)
            ffn_pe(pe, C_FFN0, 0, 0, 1, 24)
            turn_pe(pe, 2)
            for t in range(3):
                project(pe, t + C_DIFF, t + (17 + FG), (hth, htl), pa_done, pa_free, pa, call=2 if t == 0 else None)
                if t:
                    cond_cols(pe, t + 45)
            with pe.Fori(3, 12) as t:
                project(pe, t + C_DIFF, t + (17 + FG), (hth, htl), pa_done, pa_free, pa)
            pe.wait_ge(lam_prod, 2)
            pe.matmul(pb[:, 1, 0:1], ones[0:1, :], A_lam[0:1, 261:262], start=True, stop=True).then_inc(lam_mm, 1)

            def turn_qk(h, slot, first=False):
                if not first:
                    pe.wait_ge(at_T, h)
                pe.wait_ge(at_rot, h + 1)
                for j in range(2):
                    for i in range(NT):
                        mm = pe.transpose(pt[:, 0, j * SEQ + i * P:j * SEQ + (i + 1) * P],
                                          A_qk[:, slot, i, j].rearrange("p c f -> p (c f)"), ident)
                mm.then_inc(at_turned, 1)

            def scores(h, first=False):
                if not first:
                    pe.wait_ge(at_exp, h)
                pe.wait_ge(at_T, h + 1)
                pe.sem_inc(passed, 1)
                for c in range(2):
                    r = slice(c * 64, c * 64 + 64)
                    for i in range(NT):
                        mm = pe.matmul(py[:, c, i * SEQ:(i + 1) * SEQ], A_qkT[r, 0, i * P:(i + 1) * P], A_qkT[r, 1],
                                       start=True, stop=True)
                mm.then_inc(at_scores, 1)

            def pe_head(h, slot, more):
                if more:
                    scores(h + 1)
                if more == 2:
                    turn_qk(h + 2, slot)
                pe.wait_ge(at_p, h + 1)
                for k in range(NT):
                    for i in range(NT):
                        mm = pe.transpose(pt[:, 1, k * SEQ + i * P:k * SEQ + (i + 1) * P],
                                          A_p[:, slot, 0, i, k * P:(k + 1) * P], ident)
                mm.then_inc(at_pturned, 1)
                pe.wait_ge(at_pT, h + 1)
                for i in range(NT):
                    for k in range(NT):
                        mm = pe.matmul(pa[:, 0, i * P:(i + 1) * P], A_pT[:, k, i * P:(i + 1) * P],
                                       qkv[:, k, bass.ds(h * P + 2 * D, P)], start=(k == 0), stop=(k == NT - 1))
                mm.then_inc(at_o, 1)
            turn_qk(0, 0, first=True)
            scores(0, first=True)
            turn_qk(1, 1)
            heads(pe, pe_head)
            for m in range(DH // 2):
                pe.wait_ge(at_on, m + 1)
                if m >= 2:
                    pe.wait_ge(at_scaled, m - 1)
                for h in range(2):
                    for i in range(NT):
                        mm = pe.transpose(pb[:, m % 2, h * SEQ + i * P:h * SEQ + (i + 1) * P],
                                          A_on[:, m % 2, i, h * P:(h + 1) * P], ident)
                mm.then_inc(at_oT, 1)
            pe.wait_ge(at_done, DH // 2)
            out_pe(pe, C_OUT1, 17 + FG + 12, 2)
            turn_pe(pe, 3)
            ffn_pe(pe, C_FFN1, FG, 44, 3)


INPUTS = ["x", "c", "ada_w", "ada_b", "ln_g", "ln_b", "ffn_w_in", "ffn_w_out", "ab_w_in", "ab_w_out",
          "rwkv_mu", "rwkv_w0", "rwkv_w_up", "rwkv_a0", "rwkv_a_up", "rwkv_g_up", "rwkv_k_k", "rwkv_k_a",
          "rwkv_r_k", "rwkv_gn_g", "rwkv_gn_b", "gla_gate_up", "gla_gate_b", "gla_norm_g",
          "diff_w_in", "diff_w_out", "diff_lambda", "diff_subln_g"]


def kernel(**inputs):
    import concourse.bacc as bacc
    from concourse.bass_utils import run_bass_kernel_spmd

    nc = bacc.Bacc("TRN2", target_bir_lowering=False, num_devices=1)
    arrays, args = {}, []
    for name in INPUTS:
        a = np.ascontiguousarray(inputs[name])
        arrays[f"in_{name}"] = a
        args.append(nc.dram_tensor(f"in_{name}", a.shape, mybir.dt.from_np(a.dtype), kind="ExternalInput").ap())
    arrays["in_constants"] = constants()
    args.append(nc.dram_tensor("in_constants", (P, C_N), F32, kind="ExternalInput").ap())
    out = nc.dram_tensor("out_0", (1, SEQ, D), F32, kind="ExternalOutput").ap()
    build_trunk(nc, *args, out)
    r = run_bass_kernel_spmd(nc, [arrays], core_ids=[0])
    return r.results[0]["out_0"]
```
